# Optimizing a Trainium2 kernel written in Bass

```python
import jax, jax.numpy as jnp
from jax import lax
import numpy as np

D_MODEL = 1024
BATCH = 1
SEQ = 512
DEPTH = 4
DEC_BATCH = 8
DEC_SEQ = 1
PAST_LEN = 1024
PAGE_SIZE = 128

N_MIXERS = 3
N_NSA = (DEPTH + 2) // 3
N_GDN = (DEPTH + 1) // 3
N_LRU = DEPTH // 3

NSA_DH = 64
NSA_HEADS = D_MODEL // NSA_DH
NSA_HPG = 4
NSA_KV = NSA_HEADS // NSA_HPG
NSA_Q = NSA_HEADS * NSA_DH
NSA_KVW = NSA_KV * NSA_DH
NSA_IN = NSA_Q + 6 * NSA_KVW + 3 * NSA_HEADS
ROT_DIM = NSA_DH // 4
ROPE_THETA = 500000.0
L_CMP = 32
L_SEL = 64
N_SEL = 16
WINDOW = 512
Q_BLOCK = 128

GDN_DK = 128
GDN_DV = 128
GDN_HEADS = D_MODEL // GDN_DV
GDN_QK = GDN_HEADS * GDN_DK
GDN_VW = GDN_HEADS * GDN_DV
GDN_CONV = 4
GDN_CONV_CH = 2 * GDN_QK + GDN_VW
GDN_IN = GDN_CONV_CH + GDN_VW + 2 * GDN_HEADS
GDN_CHUNK = 64

D_RNN = D_MODEL
LRU_BLOCKS = 8
LRU_BW = D_RNN // LRU_BLOCKS
LRU_CONV = 4
LRU_C = 8.0

D_FF = ((8 * D_MODEL // 3 + 127) // 128) * 128
FFN_CONV = 3

EPS = 1e-6
NEG = -1e30
FORCE = 1e4

kernel_name = 'nsa_gdn_rglru_hybrid_step'

def rmsnorm(x, g):
    xf = x.astype(jnp.float32)
    y = xf * lax.rsqrt(jnp.mean(xf * xf, axis=-1, keepdims=True) + EPS)
    return (y * g.astype(jnp.float32)).astype(x.dtype)

def l2norm(x):
    xf = x.astype(jnp.float32)
    return xf * lax.rsqrt(jnp.sum(xf * xf, axis=-1, keepdims=True) + EPS)

def rope(x, pos):
    half = ROT_DIM // 2
    inv = ROPE_THETA ** (-jnp.arange(half, dtype=jnp.float32) / half)
    ang = pos.astype(jnp.float32)[:, None] * inv[None, :]
    cos = jnp.cos(ang)[:, None, :]
    sin = jnp.sin(ang)[:, None, :]
    xr = x[..., :ROT_DIM].astype(jnp.float32)
    x1, x2 = xr[..., :half], xr[..., half:]
    rot = jnp.concatenate([x1 * cos - x2 * sin, x2 * cos + x1 * sin], axis=-1).astype(x.dtype)
    return jnp.concatenate([rot, x[..., ROT_DIM:]], axis=-1)

def causal_conv(x, buf, w):
    width = w.shape[0]
    T = x.shape[1]
    xp = jnp.concatenate([buf.astype(x.dtype), x], axis=1)
    y = xp[:, 0:T] * w[0]
    for j in range(1, width):
        y = y + xp[:, j:j + T] * w[j]
    return y, xp[:, T:]

def nsa_project(h, w_in, pos):
    B, T, _ = h.shape
    z = h @ w_in
    cuts = np.cumsum([NSA_Q] + [NSA_KVW] * 6).tolist()
    q, kc, vc, ks, vs, kw, vw, gl = jnp.split(z, cuts, axis=-1)
    q = q.reshape(B, T, NSA_HEADS, NSA_DH)
    kc, vc, ks, vs, kw, vw = [t.reshape(B, T, NSA_KV, NSA_DH) for t in (kc, vc, ks, vs, kw, vw)]
    gates = jax.nn.sigmoid(gl.astype(jnp.float32)).reshape(B, T, 3, NSA_HEADS)
    return q, rope(q, pos), kc, vc, rope(ks, pos), vs, rope(kw, pos), vw, gates

def nsa_compress(k, pe, w):
    B, L = k.shape[:2]
    blk = k.reshape(B, L // L_CMP, L_CMP, NSA_KV, NSA_DH) + pe[:, None, :]
    return jnp.einsum('bclgd,lde->bcge', blk, w)

def nsa_compressed_select(q, kc, vc, pe, wc, qpos):
    B, T = q.shape[:2]
    L = kc.shape[1]
    kcmp = nsa_compress(kc, pe[0], wc[0])
    vcmp = nsa_compress(vc, pe[1], wc[1])
    qg = q.astype(jnp.float32).reshape(B, T, NSA_KV, NSA_HPG, NSA_DH) * NSA_DH ** -0.5
    s = jnp.einsum('btgjd,bcgd->bgjtc', qg, kcmp.astype(jnp.float32))
    n_cmp = L // L_CMP
    c_end = (jnp.arange(n_cmp, dtype=jnp.int32) + 1) * L_CMP - 1
    valid = c_end[None, :] <= qpos[:, None]
    p = jax.nn.softmax(jnp.where(valid, s, NEG), axis=-1) * jnp.any(valid, axis=-1)[:, None].astype(jnp.float32)
    o_c = jnp.einsum('bgjtc,bcgd->btgjd', p.astype(vcmp.dtype), vcmp).reshape(B, T, NSA_HEADS, NSA_DH)
    n_sel = L // L_SEL
    imp = p.sum(axis=2).reshape(B, NSA_KV, T, n_sel, L_SEL // L_CMP).sum(-1)
    blk = jnp.arange(n_sel, dtype=jnp.int32)
    forced = (blk[None, :] == 0) | (blk[None, :] == (qpos // L_SEL)[:, None])
    avail = blk[None, :] * L_SEL <= qpos[:, None]
    imp = jnp.where(forced, FORCE, jnp.where(avail, imp, -1.0))
    _, idx = lax.top_k(imp, min(N_SEL, n_sel))
    return o_c, idx

def nsa_blocks(k):
    B, L = k.shape[:2]
    return k.reshape(B, L // L_SEL, L_SEL, NSA_KV, NSA_DH).transpose(0, 3, 1, 2, 4)

def nsa_local(qg, idx, qpos, ks_blk, vs_blk, kw, vw, kwpos):
    B, Tb = qg.shape[:2]
    qf = qg.astype(jnp.float32) * NSA_DH ** -0.5
    bi = jnp.arange(B)[:, None, None, None]
    gi = jnp.arange(NSA_KV)[None, :, None, None]
    kg = ks_blk[bi, gi, idx]
    vg = vs_blk[bi, gi, idx]
    s = jnp.einsum('btgjd,bgtkld->bgjtkl', qf, kg.astype(jnp.float32))
    kpos = idx[..., None] * L_SEL + jnp.arange(L_SEL, dtype=jnp.int32)
    m = kpos <= qpos[None, None, :, None, None]
    s = jnp.where(m[:, :, None], s, NEG)
    p = jax.nn.softmax(s.reshape(s.shape[:4] + (-1,)), axis=-1)
    o_s = jnp.einsum('bgjtn,bgtnd->btgjd', p.astype(vg.dtype), vg.reshape(B, NSA_KV, Tb, -1, NSA_DH))
    sw = jnp.einsum('btgjd,blgd->bgjtl', qf, kw.astype(jnp.float32))
    dist = qpos[:, None] - kwpos[None, :]
    mw = (dist >= 0) & (dist <= WINDOW) & (kwpos >= 0)[None, :]
    pw = jax.nn.softmax(jnp.where(mw, sw, NEG), axis=-1)
    o_w = jnp.einsum('bgjtl,blgd->btgjd', pw.astype(vw.dtype), vw)
    return o_s, o_w

def nsa_merge(o_c, o_s, o_w, gates, w_out):
    B, T = gates.shape[:2]
    o = (gates[:, :, 0, :, None] * o_c.astype(jnp.float32)
         + gates[:, :, 1, :, None] * o_s.astype(jnp.float32)
         + gates[:, :, 2, :, None] * o_w.astype(jnp.float32))
    return o.reshape(B, T, NSA_Q).astype(w_out.dtype) @ w_out

def nsa_prompt(h, w_in, pe, wc, w_out):
    B, T, _ = h.shape
    pos = jnp.arange(T, dtype=jnp.int32)
    q, q_r, kc, vc, ks, vs, kw, vw, gates = nsa_project(h, w_in, pos)
    o_c, idx = nsa_compressed_select(q, kc, vc, pe, wc, pos)
    ks_blk, vs_blk = nsa_blocks(ks), nsa_blocks(vs)
    qg = q_r.reshape(B, T, NSA_KV, NSA_HPG, NSA_DH)
    kw_pad = jnp.pad(kw, ((0, 0), (WINDOW, 0), (0, 0), (0, 0)))
    vw_pad = jnp.pad(vw, ((0, 0), (WINDOW, 0), (0, 0), (0, 0)))

    def body(i):
        q0 = i * Q_BLOCK
        qb = lax.dynamic_slice_in_dim(qg, q0, Q_BLOCK, axis=1)
        idxb = lax.dynamic_slice_in_dim(idx, q0, Q_BLOCK, axis=2)
        qposb = q0 + jnp.arange(Q_BLOCK, dtype=jnp.int32)
        kwb = lax.dynamic_slice_in_dim(kw_pad, q0, WINDOW + Q_BLOCK, axis=1)
        vwb = lax.dynamic_slice_in_dim(vw_pad, q0, WINDOW + Q_BLOCK, axis=1)
        kwposb = q0 - WINDOW + jnp.arange(WINDOW + Q_BLOCK, dtype=jnp.int32)
        return nsa_local(qb, idxb, qposb, ks_blk, vs_blk, kwb, vwb, kwposb)

    o_s, o_w = lax.map(body, jnp.arange(T // Q_BLOCK, dtype=jnp.int32))
    o_s = jnp.moveaxis(o_s, 0, 1).reshape(B, T, NSA_HEADS, NSA_DH)
    o_w = jnp.moveaxis(o_w, 0, 1).reshape(B, T, NSA_HEADS, NSA_DH)
    y = nsa_merge(o_c, o_s, o_w, gates, w_out)
    wl = min(WINDOW, T)
    new_win = jnp.stack([kw[:, T - wl:], vw[:, T - wl:]], axis=2)
    return y, jnp.stack([kc, vc], axis=2), jnp.stack([ks, vs], axis=2), new_win

def nsa_sample(h, cache_cmp, cache_sel, win_buf, page_table, j, w_in, pe, wc, w_out):
    B, T, _ = h.shape
    pos = PAST_LEN + jnp.arange(T, dtype=jnp.int32)
    q, q_r, kc, vc, ks, vs, kw, vw, gates = nsa_project(h, w_in, pos)
    pad = (-(PAST_LEN + T)) % L_SEL

    def full_seq(cache, k_new, v_new):
        rows = cache[j, page_table].reshape(B, PAST_LEN, 2, NSA_KV, NSA_DH)
        seq = jnp.concatenate([rows, jnp.stack([k_new, v_new], axis=2).astype(rows.dtype)], axis=1)
        seq = jnp.pad(seq, ((0, 0), (0, pad), (0, 0), (0, 0), (0, 0)))
        return seq[:, :, 0], seq[:, :, 1]

    kc_all, vc_all = full_seq(cache_cmp, kc, vc)
    ks_all, vs_all = full_seq(cache_sel, ks, vs)
    o_c, idx = nsa_compressed_select(q, kc_all, vc_all, pe, wc, pos)
    wb = win_buf.shape[1]
    win_all = jnp.concatenate([win_buf, jnp.stack([kw, vw], axis=2).astype(win_buf.dtype)], axis=1)
    kwpos = PAST_LEN - wb + jnp.arange(wb + T, dtype=jnp.int32)
    qg = q_r.reshape(B, T, NSA_KV, NSA_HPG, NSA_DH)
    o_s, o_w = nsa_local(qg, idx, pos, nsa_blocks(ks_all), nsa_blocks(vs_all),
                         win_all[:, :, 0], win_all[:, :, 1], kwpos)
    y = nsa_merge(o_c, o_s.reshape(B, T, NSA_HEADS, NSA_DH), o_w.reshape(B, T, NSA_HEADS, NSA_DH), gates, w_out)
    return y, jnp.stack([kc, vc], axis=2), jnp.stack([ks, vs], axis=2), win_all[:, T:]

def chunk_gated_delta(q, k, v, beta, g, S0):
    B, T, H, DK = q.shape
    DV = v.shape[-1]
    C = min(GDN_CHUNK, T)
    pad = (-T) % C
    n = (T + pad) // C

    def prep(x):
        x = jnp.pad(x.astype(jnp.float32), [(0, 0), (0, pad)] + [(0, 0)] * (x.ndim - 2))
        x = x.reshape((B, n, C) + x.shape[2:])
        return jnp.moveaxis(jnp.moveaxis(x, 3, 2), 1, 0)

    qc, kc, vc, bc, gc = [prep(t) for t in (q, k, v, beta, g)]
    gcum = jnp.cumsum(gc, axis=-1)
    ar = jnp.arange(C)
    incl = ar[:, None] >= ar[None, :]
    strict = (ar[:, None] > ar[None, :]).astype(jnp.float32)
    decay = jnp.exp(jnp.where(incl, gcum[..., :, None] - gcum[..., None, :], NEG))
    kb = kc * bc[..., None]
    lower = jnp.einsum('nbhid,nbhjd->nbhij', kb, kc) * decay * strict
    A = lower + jnp.eye(C, dtype=jnp.float32)
    rhs = jnp.concatenate([vc * bc[..., None], kb * jnp.exp(gcum)[..., None]], axis=-1)
    sol = lax.linalg.triangular_solve(A, rhs, left_side=True, lower=True, unit_diagonal=True)
    u_base, w_dec = sol[..., :DV], sol[..., DV:]
    attn = jnp.einsum('nbhid,nbhjd->nbhij', qc, kc) * decay

    def step(S, xs):
        q_i, k_i, ub, wd, at, g_i = xs
        u = ub - jnp.einsum('bhck,bhkv->bhcv', wd, S)
        o = jnp.einsum('bhck,bhkv->bhcv', q_i * jnp.exp(g_i)[..., None], S) + jnp.einsum('bhij,bhjv->bhiv', at, u)
        g_last = g_i[..., -1]
        S = S * jnp.exp(g_last)[..., None, None] + jnp.einsum(
            'bhck,bhcv->bhkv', k_i * jnp.exp(g_last[..., None] - g_i)[..., None], u)
        return S, o

    S, o = lax.scan(step, S0.astype(jnp.float32), (qc, kc, u_base, w_dec, attn, gcum))
    o = jnp.moveaxis(jnp.moveaxis(o, 0, 1), 2, 3).reshape(B, n * C, H, DV)[:, :T]
    return o, S

def gdn_mixer(h, S0, conv_buf, w_in, conv_w, A_log, dt_bias, norm_g, w_out):
    B, T, _ = h.shape
    z = h @ w_in
    qkv, gate, a_in, b_in = jnp.split(z, [GDN_CONV_CH, GDN_CONV_CH + GDN_VW, GDN_CONV_CH + GDN_VW + GDN_HEADS], axis=-1)
    qkv_c, new_buf = causal_conv(qkv, conv_buf, conv_w)
    qkv_c = jax.nn.silu(qkv_c)
    q, k, v = jnp.split(qkv_c, [GDN_QK, 2 * GDN_QK], axis=-1)
    q = l2norm(q.reshape(B, T, GDN_HEADS, GDN_DK)) * GDN_DK ** -0.5
    k = l2norm(k.reshape(B, T, GDN_HEADS, GDN_DK))
    v = v.reshape(B, T, GDN_HEADS, GDN_DV)
    beta = jax.nn.sigmoid(b_in.astype(jnp.float32))
    g = -jnp.exp(A_log.astype(jnp.float32)) * jax.nn.softplus(a_in.astype(jnp.float32) + dt_bias.astype(jnp.float32))
    o, S = chunk_gated_delta(q, k, v, beta, g, S0)
    o = rmsnorm(o.astype(h.dtype), norm_g) * jax.nn.silu(gate.reshape(B, T, GDN_HEADS, GDN_DV))
    return o.reshape(B, T, GDN_VW) @ w_out, S.astype(S0.dtype), new_buf

def linear_combine(left, right):
    a_l, b_l = left
    a_r, b_r = right
    return a_l * a_r, a_r * b_l + b_r

def lru_mixer(h, h0, conv_buf, w_in, conv_w, conv_b, w_ga, b_ga, w_gx, b_gx, lam, w_out):
    B, T, _ = h.shape
    z = h @ w_in
    gate, xb = jnp.split(z, 2, axis=-1)
    xc, new_buf = causal_conv(xb, conv_buf, conv_w)
    xc = xc + conv_b
    xblk = xc.reshape(B, T, LRU_BLOCKS, LRU_BW)
    r = jax.nn.sigmoid((jnp.einsum('btnc,ncd->btnd', xblk, w_ga).reshape(B, T, D_RNN) + b_ga).astype(jnp.float32))
    i = jax.nn.sigmoid((jnp.einsum('btnc,ncd->btnd', xblk, w_gx).reshape(B, T, D_RNN) + b_gx).astype(jnp.float32))
    log_a = -LRU_C * r * jax.nn.softplus(-lam.astype(jnp.float32))
    a = jnp.exp(log_a)
    b = jnp.sqrt(-jnp.expm1(2.0 * log_a)) * i * xc.astype(jnp.float32)
    b = b.at[:, 0].add(a[:, 0] * h0.astype(jnp.float32))
    _, hs = lax.associative_scan(linear_combine, (a, b), axis=1)
    y = hs.astype(h.dtype) * jax.nn.gelu(gate)
    return y @ w_out, hs[:, -1].astype(h0.dtype), new_buf

def conv_ffn(h, buf, w_in, conv_w, w_out):
    u, new_buf = causal_conv(h @ w_in, buf, conv_w)
    val, gt = jnp.split(u, 2, axis=-1)
    return (val * jax.nn.silu(gt)) @ w_out, new_buf

def trunk(x, nsa_call, gdn_S, gdn_conv, lru_h, lru_conv, ffn_conv,
          norm_mix_g, norm_ffn_g, norm_final_g,
          gdn_w_in, gdn_conv_w, gdn_A_log, gdn_dt_bias, gdn_norm_g, gdn_w_out,
          lru_w_in, lru_conv_w, lru_conv_b, lru_w_ga, lru_b_ga, lru_w_gx, lru_b_gx, lru_lambda, lru_w_out,
          ffn_w_in, ffn_conv_w, ffn_w_out):
    nsa_new, gdn_new, lru_new, ffn_new = [], [], [], []
    for li in range(DEPTH):
        j = li // N_MIXERS
        kind = li % N_MIXERS
        hn = rmsnorm(x, norm_mix_g[li])
        if kind == 0:
            y, s_cmp, s_sel, s_win = nsa_call(j, hn)
            nsa_new.append((s_cmp, s_sel, s_win))
        elif kind == 1:
            y, S, cb = gdn_mixer(hn, gdn_S[j], gdn_conv[j], gdn_w_in[j], gdn_conv_w[j], gdn_A_log[j],
                                 gdn_dt_bias[j], gdn_norm_g[j], gdn_w_out[j])
            gdn_new.append((S, cb))
        else:
            y, hl, cb = lru_mixer(hn, lru_h[j], lru_conv[j], lru_w_in[j], lru_conv_w[j], lru_conv_b[j],
                                  lru_w_ga[j], lru_b_ga[j], lru_w_gx[j], lru_b_gx[j], lru_lambda[j], lru_w_out[j])
            lru_new.append((hl, cb))
        x = x + y
        y, fb = conv_ffn(rmsnorm(x, norm_ffn_g[li]), ffn_conv[li], ffn_w_in[li], ffn_conv_w[li], ffn_w_out[li])
        ffn_new.append(fb)
        x = x + y
    return rmsnorm(x, norm_final_g), nsa_new, gdn_new, lru_new, ffn_new

def stack_states(entries, n):
    return [jnp.stack([e[k] for e in entries]) for k in range(n)]

def setup_inputs(seed: int = 0) -> dict:
    key = jax.random.key(seed)
    ks = iter(jax.random.split(key, 48))

    def nrm(shape, scale):
        return jax.random.normal(next(ks), shape, jnp.float32) * scale

    n_pages = PAST_LEN // PAGE_SIZE
    n_used = DEC_BATCH * n_pages
    n_phys = n_used + n_used // 4
    w_buf = min(WINDOW, PAST_LEN)
    x_prompt = nrm((BATCH, SEQ, D_MODEL), 1.0)
    x_sample = nrm((DEC_BATCH, DEC_SEQ, D_MODEL), 1.0)
    cache_nsa_cmp = nrm((N_NSA, n_phys, PAGE_SIZE, 2, NSA_KV, NSA_DH), 1.0)
    cache_nsa_sel = nrm((N_NSA, n_phys, PAGE_SIZE, 2, NSA_KV, NSA_DH), 1.0)
    state_nsa_win = nrm((N_NSA, DEC_BATCH, w_buf, 2, NSA_KV, NSA_DH), 1.0)
    state_gdn_S = nrm((N_GDN, DEC_BATCH, GDN_HEADS, GDN_DK, GDN_DV), 0.1)
    state_gdn_conv = nrm((N_GDN, DEC_BATCH, GDN_CONV - 1, GDN_CONV_CH), 1.0)
    state_lru_h = nrm((N_LRU, DEC_BATCH, D_RNN), 0.5)
    state_lru_conv = nrm((N_LRU, DEC_BATCH, LRU_CONV - 1, D_RNN), 1.0)
    state_ffn_conv = nrm((DEPTH, DEC_BATCH, FFN_CONV - 1, 2 * D_FF), 1.0)
    page_table = jax.random.permutation(next(ks), n_phys)[:n_used].reshape(DEC_BATCH, n_pages).astype(jnp.int32)
    norm_mix_g = 1.0 + nrm((DEPTH, D_MODEL), 0.1)
    norm_ffn_g = 1.0 + nrm((DEPTH, D_MODEL), 0.1)
    norm_final_g = 1.0 + nrm((D_MODEL,), 0.1)
    nsa_w_in = nrm((N_NSA, D_MODEL, NSA_IN), D_MODEL ** -0.5)
    nsa_cmp_pe = nrm((N_NSA, 2, L_CMP, NSA_DH), 0.1)
    nsa_cmp_w = nrm((N_NSA, 2, L_CMP, NSA_DH, NSA_DH), (L_CMP * NSA_DH) ** -0.5)
    nsa_w_out = nrm((N_NSA, NSA_Q, D_MODEL), NSA_Q ** -0.5)
    gdn_w_in = nrm((N_GDN, D_MODEL, GDN_IN), D_MODEL ** -0.5)
    gdn_conv_w = nrm((N_GDN, GDN_CONV, GDN_CONV_CH), GDN_CONV ** -0.5)
    gdn_A_log = jnp.log(jax.random.uniform(next(ks), (N_GDN, GDN_HEADS), jnp.float32, 1.0, 16.0))
    dt = jnp.exp(jax.random.uniform(next(ks), (N_GDN, GDN_HEADS), jnp.float32, np.log(1e-3), np.log(1e-1)))
    gdn_dt_bias = dt + jnp.log(-jnp.expm1(-dt))
    gdn_norm_g = 1.0 + nrm((N_GDN, GDN_DV), 0.1)
    gdn_w_out = nrm((N_GDN, GDN_VW, D_MODEL), GDN_VW ** -0.5)
    lru_w_in = nrm((N_LRU, D_MODEL, 2 * D_RNN), D_MODEL ** -0.5)
    lru_conv_w = nrm((N_LRU, LRU_CONV, D_RNN), LRU_CONV ** -0.5)
    lru_conv_b = nrm((N_LRU, D_RNN), 0.01)
    lru_w_ga = nrm((N_LRU, LRU_BLOCKS, LRU_BW, LRU_BW), LRU_BW ** -0.5)
    lru_b_ga = nrm((N_LRU, D_RNN), 0.01)
    lru_w_gx = nrm((N_LRU, LRU_BLOCKS, LRU_BW, LRU_BW), LRU_BW ** -0.5)
    lru_b_gx = nrm((N_LRU, D_RNN), 0.01)
    s8 = jax.random.uniform(next(ks), (N_LRU, D_RNN), jnp.float32, 0.9, 0.999) ** (1.0 / LRU_C)
    lru_lambda = jnp.log(s8) - jnp.log1p(-s8)
    lru_w_out = nrm((N_LRU, D_RNN, D_MODEL), D_RNN ** -0.5)
    ffn_w_in = nrm((DEPTH, D_MODEL, 2 * D_FF), D_MODEL ** -0.5)
    ffn_conv_w = nrm((DEPTH, FFN_CONV, 2 * D_FF), FFN_CONV ** -0.5)
    ffn_w_out = nrm((DEPTH, D_FF, D_MODEL), D_FF ** -0.5)
    return {'x_prompt': x_prompt, 'x_sample': x_sample,
            'cache_nsa_cmp': cache_nsa_cmp, 'cache_nsa_sel': cache_nsa_sel, 'state_nsa_win': state_nsa_win,
            'state_gdn_S': state_gdn_S, 'state_gdn_conv': state_gdn_conv,
            'state_lru_h': state_lru_h, 'state_lru_conv': state_lru_conv, 'state_ffn_conv': state_ffn_conv,
            'page_table': page_table,
            'norm_mix_g': norm_mix_g, 'norm_ffn_g': norm_ffn_g, 'norm_final_g': norm_final_g,
            'nsa_w_in': nsa_w_in, 'nsa_cmp_pe': nsa_cmp_pe, 'nsa_cmp_w': nsa_cmp_w, 'nsa_w_out': nsa_w_out,
            'gdn_w_in': gdn_w_in, 'gdn_conv_w': gdn_conv_w, 'gdn_A_log': gdn_A_log, 'gdn_dt_bias': gdn_dt_bias,
            'gdn_norm_g': gdn_norm_g, 'gdn_w_out': gdn_w_out,
            'lru_w_in': lru_w_in, 'lru_conv_w': lru_conv_w, 'lru_conv_b': lru_conv_b,
            'lru_w_ga': lru_w_ga, 'lru_b_ga': lru_b_ga, 'lru_w_gx': lru_w_gx, 'lru_b_gx': lru_b_gx,
            'lru_lambda': lru_lambda, 'lru_w_out': lru_w_out,
            'ffn_w_in': ffn_w_in, 'ffn_conv_w': ffn_conv_w, 'ffn_w_out': ffn_w_out}

def reference(x_prompt, x_sample, cache_nsa_cmp, cache_nsa_sel, state_nsa_win, state_gdn_S, state_gdn_conv,
              state_lru_h, state_lru_conv, state_ffn_conv, page_table,
              norm_mix_g, norm_ffn_g, norm_final_g,
              nsa_w_in, nsa_cmp_pe, nsa_cmp_w, nsa_w_out,
              gdn_w_in, gdn_conv_w, gdn_A_log, gdn_dt_bias, gdn_norm_g, gdn_w_out,
              lru_w_in, lru_conv_w, lru_conv_b, lru_w_ga, lru_b_ga, lru_w_gx, lru_b_gx, lru_lambda, lru_w_out,
              ffn_w_in, ffn_conv_w, ffn_w_out):
    shared = (norm_mix_g, norm_ffn_g, norm_final_g,
              gdn_w_in, gdn_conv_w, gdn_A_log, gdn_dt_bias, gdn_norm_g, gdn_w_out,
              lru_w_in, lru_conv_w, lru_conv_b, lru_w_ga, lru_b_ga, lru_w_gx, lru_b_gx, lru_lambda, lru_w_out,
              ffn_w_in, ffn_conv_w, ffn_w_out)

    def nsa_prompt_call(j, hn):
        return nsa_prompt(hn, nsa_w_in[j], nsa_cmp_pe[j], nsa_cmp_w[j], nsa_w_out[j])

    def nsa_sample_call(j, hn):
        return nsa_sample(hn, cache_nsa_cmp, cache_nsa_sel, state_nsa_win[j], page_table, j,
                          nsa_w_in[j], nsa_cmp_pe[j], nsa_cmp_w[j], nsa_w_out[j])

    dt = x_prompt.dtype
    B = x_prompt.shape[0]
    y_prompt, p_nsa, p_gdn, p_lru, p_ffn = trunk(
        x_prompt, nsa_prompt_call,
        jnp.zeros((N_GDN, B, GDN_HEADS, GDN_DK, GDN_DV), dt),
        jnp.zeros((N_GDN, B, GDN_CONV - 1, GDN_CONV_CH), dt),
        jnp.zeros((N_LRU, B, D_RNN), dt),
        jnp.zeros((N_LRU, B, LRU_CONV - 1, D_RNN), dt),
        jnp.zeros((DEPTH, B, FFN_CONV - 1, 2 * D_FF), dt),
        *shared)
    y_sample, s_nsa, s_gdn, s_lru, s_ffn = trunk(
        x_sample, nsa_sample_call, state_gdn_S, state_gdn_conv, state_lru_h, state_lru_conv, state_ffn_conv,
        *shared)
    p_cmp, p_sel, p_win = stack_states(p_nsa, 3)
    s_cmp, s_sel, s_win = stack_states(s_nsa, 3)
    p_gS, p_gconv = stack_states(p_gdn, 2)
    s_gS, s_gconv = stack_states(s_gdn, 2)
    p_lh, p_lconv = stack_states(p_lru, 2)
    s_lh, s_lconv = stack_states(s_lru, 2)
    p_fconv = jnp.stack(p_ffn)
    s_fconv = jnp.stack(s_ffn)
    return (y_prompt, y_sample, p_cmp, s_cmp, p_sel, s_sel, p_win, s_win,
            p_gS, s_gS, p_gconv, s_gconv, p_lh, s_lh, p_lconv, s_lconv, p_fconv, s_fconv)


_drawn_inputs = setup_inputs


def setup_inputs(seed=0):
    import zlib

    import numpy as np

    out = dict(_drawn_inputs(seed))
    spreads = {}
    factors = {'lru_b_ga': 25.219, 'lru_b_gx': 8.0}
    for name, (base, spread) in spreads.items():
        noise = np.random.default_rng([zlib.crc32(name.encode()), seed]).standard_normal(out[name].shape)
        drawn = base * np.exp(spread * noise) if base else spread * noise
        out[name] = __import__('jax').numpy.asarray(drawn.astype(out[name].dtype))
    for name, factor in factors.items():
        out[name] = (out[name] * factor).astype(out[name].dtype)
    return out
```

```python
from contextlib import ExitStack

import concourse.bass as bass
from concourse import mybir

F32 = mybir.dt.float32
F32R = mybir.dt.float32r
BF16 = mybir.dt.bfloat16
I32 = mybir.dt.int32
ACT = mybir.ActivationFunctionType
ALU = mybir.AluOpType
AX = mybir.AxisListType.X

P = 128
D = 1024
KT = D // P
T = 512
B = 8
N = T + B
H = N // 2
EPS = 1e-6
NEG = -1e30
DFF = 2816
FT = DFF // P
CH = 128
NCH = T // CH
HEADS = 16
PAGES = 8
N_PHYS = 80
NCMP = 32
PCMP = T // 32

CONST_PARTS = [("ident", 128), ("ones", 128), ("neg_upper", 128), ("strict_t", 128), ("same16", 128),
               ("pair16", 128), ("pair32", 128), ("pair64", 128), ("causal", 128), ("rope_swap", 128),
               ("four_sum", 128), ("cmp_mask", 4 * PCMP), ("cmp_any", 4), ("new_mask", B), ("block_no", 16)]
CONST_AT, _at = {}, 0
for _name, _n in CONST_PARTS:
    CONST_AT[_name] = (_at, _at + _n)
    _at += _n
CONST_COLS = _at


class Steps:

    def __init__(self, eng, sem):
        self.eng, self.sem, self.n, self.at = eng, sem, 0, 0

    def did(self, ins):
        ins.then_inc(self.sem, 1)
        self.n += 1

    def settle(self):
        self.eng.wait_ge(self.sem, self.at + self.n)


def flat(ap):
    return ap.rearrange("p o n -> p (o n)")


class Scope:

    def __init__(self, nc, ctx, prefix):
        self.nc, self.ctx, self.prefix, self.sems = nc, ctx, prefix, []
        ctx.callback(self.clear)

    def clear(self):
        if self.sems:
            self.nc.clear_and_free_semaphores(self.sems)
            self.nc.all_engine_barrier()

    def sb(self, name, shape, dt=F32):
        return self.ctx.enter_context(self.nc.sbuf_tensor(f"{self.prefix}_{name}_sb", shape, dt))

    def ps(self, name, shape, dt=F32):
        return self.ctx.enter_context(self.nc.psum_tensor(f"{self.prefix}_{name}", shape, dt))

    def sem(self, name):
        self.sems.append(self.nc.alloc_semaphore(f"{self.prefix}_{name}"))
        return self.sems[-1]


class Norm:

    def __init__(self, sc, g, ps):
        self.sc, self.g, self.ps = sc, g, ps
        self.sq = sc.sb("norm_sq", [P, 2, N])
        self.rstd = sc.sb("norm_rstd", [P, N])
        self.squared = sc.sem("norm_squared")
        self.summed = sc.sem("norm_summed")
        self.rooted = sc.sem("norm_rooted")
        self.inverted = sc.sem("norm_inverted")
        self.normed = sc.sem("norm_normed")

    def act(self, act, xt, eps):
        for kt in range(KT):
            if kt >= 2:
                act.wait_ge(self.summed, kt - 1)
            act.activation(self.sq[:, kt % 2, :], xt[:, kt, :], ACT.Square).then_inc(self.squared, 1)
        act.wait_ge(self.summed, KT)
        act.activation(self.rstd[:, :].rearrange("p (h n) -> p h n", h=2), self.ps[:, 0:2, 0:H], ACT.Sqrt,
                       bias=eps[:, 0:1], scale=1.0 / D).then_inc(self.rooted, 1)

    def pe(self, pe, ones):
        for kt in range(KT):
            pe.wait_ge(self.squared, kt + 1)
            for h in range(2):
                mm = pe.matmul(self.ps[:, h, 0:H], ones, self.sq[:, kt % 2, h * H:(h + 1) * H],
                               start=(kt == 0), stop=(kt == KT - 1))
            mm.then_inc(self.summed, 1)

    def dve(self, dve, xt, xn):
        dve.wait_ge(self.rooted, 1)
        dve.reciprocal(self.rstd[:, :], self.rstd[:, :]).then_inc(self.inverted, 1)
        dve.wait_ge(self.inverted, 1)
        for kt in range(KT):
            dve.scalar_tensor_tensor(xn[:, kt, :], xt[:, kt, :], self.g[:, kt:kt + 1], self.rstd[:, :],
                                     ALU.mult, ALU.mult).then_inc(self.normed, 1)


def load_stage(nc, d, g):
    with ExitStack() as ctx:
        sc = Scope(nc, ctx, "load")
        loaded = sc.sem("loaded")
        block = ctx.enter_context(nc.Block())

        @block.sync
        def _(sp):
            sp.dma_start(g.xt[:], d["x_t"]).then_inc(loaded, 16)
            sp.dma_start(g.const[:], d["consts"]).then_inc(loaded, 16)
            sp.dma_start(g.norm_g[:], d["norm_g"]).then_inc(loaded, 16)
            sp.wait_ge(loaded, 48)

        @block.vector
        def _(dve):
            dve.memset(g.eps[:], EPS)
            dve.memset(g.bias_one[:], 1.0)


def ffn_stage(nc, d, o, g, layer):
    groups = ((0, 12), (12, 10))
    with ExitStack() as ctx:
        sc = Scope(nc, ctx, f"ffn{layer}")
        raw = sc.sb("raw", [P, 2, 2 * KT * P])
        w_hi = sc.sb("w_hi", [P, 2, 2 * KT * P], F32R)
        w_lo = sc.sb("w_lo", [P, 2, 2 * KT * P], F32R)
        x_hi = sc.sb("x_hi", [P, KT, N], F32R)
        x_lo = sc.sb("x_lo", [P, KT, N], F32R)
        inner_hi = sc.sb("inner_hi", [P, groups[0][1], N], F32R)
        inner_lo = sc.sb("inner_lo", [P, groups[0][1], N], F32R)
        product = sc.sb("product", [P, N])
        conv_w = sc.sb("conv_w", [P, FT * 2 * 3])
        state = sc.sb("state", [P, FT * 2, 2, B])
        pre = sc.sb("pre", [P, 2, 2, 2 + N])
        conv = sc.sb("conv", [P, 2, 2, N])
        gate = sc.sb("gate", [P, 2, N])
        last = sc.sb("last", [P, FT * 2, 10])
        ps = sc.ps("ps", [P, 2, 2, 2, 512])
        psf = ps[:, :, :, :, :].rearrange("p a b c n -> p (a b c) n")
        norm = Norm(sc, g.norm_g[:, 4 + layer, :], psf)
        small_in = sc.sem("small_in")
        raw_in = [sc.sem(f"raw_in{s}") for s in range(2)]
        hi_done = sc.sem("hi_done")
        lo_done = sc.sem("lo_done")
        x_hi_done = sc.sem("x_hi_done")
        x_lo_done = sc.sem("x_lo_done")
        zeroed = sc.sem("zeroed")
        projected = sc.sem("projected")
        copied = sc.sem("copied")
        convolved = sc.sem("convolved")
        gated = sc.sem("gated")
        joined = sc.sem("joined")
        dve_own = sc.sem("dve_own")
        out_done = sc.sem("out_done")
        added = sc.sem("added")
        stored = sc.sem("stored")
        block = ctx.enter_context(nc.Block())

        def at(f, a, b):
            return f[0] * (2 * a) + (a * f[1] + b)

        def starts(f):
            return isinstance(f[0], int) and 2 * f[0] + f[1] < 2

        def before(f):
            return f[0], f[1] - 1

        def pairs(eng, gi, pair):
            n = groups[gi][1]
            pair(0, True, False)
            with eng.Fori(1, n // 2 - 1) as i:
                pair(i, False, False)
            pair(n // 2 - 1, False, True)

        @block.sync
        def _(sp):
            def w_in_load(f, gi):
                s = f[1] % 2
                if not starts(f):
                    sp.wait_ge(lo_done, at(f, 1, 8 * gi - 1))
                src = d["ffn_w_in"][layer, bass.ds(at(f, 1, 0), 1)].rearrange("o p n -> p (o n)")
                sp.dma_start(raw[:, s], src).then_inc(raw_in[s], 16)

            for gi, (f0, n) in enumerate(groups):
                w_in_load((0, f0), gi), w_in_load((0, f0 + 1), gi)
                if gi == 0:
                    sp.dma_start(conv_w[:], d["ffn_conv_w"][layer]).then_inc(small_in, 16)
                    sp.dma_start(state[:], d["ffn_state"][layer]).then_inc(small_in, 16)
                with sp.Fori(1, n // 2) as i:
                    w_in_load((i, f0), gi), w_in_load((i, f0 + 1), gi)
                for m in range(KT):
                    sp.wait_ge(lo_done, f0 + n + 8 * gi + m - 1)
                    sp.dma_start(raw[:, m % 2, 0:n * P], d["ffn_w_out"][layer, m, :, f0 * P:(f0 + n) * P]).then_inc(raw_in[m % 2], 16)
            sp.wait_ge(joined, FT)
            sp.dma_start(o["ffn_last"][layer], last[:]).then_inc(stored, 16)
            sp.dma_start(o["ffn_old"][layer], state[:, :, 1, :]).then_inc(stored, 16)
            sp.wait_ge(stored, 32)

        @block.tensor
        def _(pe):
            norm.pe(pe, g.ones)

            def three(bank, w, xh, xl, start, stop):
                for k, (wp, xp) in enumerate(((w_hi, xh), (w_hi, xl), (w_lo, xh))):
                    for h in range(2):
                        mm = pe.matmul(psf[:, bank + h, 0:H], wp[:, w[0], w[1]:w[1] + P], xp[:, h * H:(h + 1) * H],
                                       start=start and k == 0, stop=stop and k == 2)
                return mm

            def tile(f, gi):
                s = f[1] % 2
                pe.wait_ge(lo_done, at(f, 1, 8 * gi + 1))
                if not starts(f):
                    pe.wait_ge(copied, at(f, 2, -2))
                for vg in range(2):
                    for kt in range(KT):
                        if starts(f) and s == 0 and vg == 0:
                            pe.wait_ge(x_lo_done, kt + 1)
                        mm = three(4 * s + 2 * vg, (s, (vg * KT + kt) * P), x_hi[:, kt], x_lo[:, kt],
                                   kt == 0, kt == KT - 1)
                    mm.then_inc(projected, 1)

            for gi, (f0, n) in enumerate(groups):
                if gi:
                    pe.wait_ge(added, KT * gi)
                pairs(pe, gi, lambda i, *_: (tile((i, f0), gi), tile((i, f0 + 1), gi)))
                for m in range(KT):
                    pe.wait_ge(lo_done, f0 + n + 8 * gi + m + 1)
                    if m == 0:
                        pe.wait_ge(copied, 2 * (f0 + n) - 2)
                        pe.wait_ge(joined, f0 + n - 2)
                    if m >= 4:
                        pe.wait_ge(added, KT * gi + m - 3)
                    for k in range(n):
                        if m == 0 and k >= n - 2:
                            pe.wait_ge(joined, f0 + k + 1)
                        mm = three(2 * (m % 4), (m % 2, k * P), inner_hi[:, k], inner_lo[:, k], k == 0, k == n - 1)
                    mm.then_inc(out_done, 1)

        @block.scalar
        def _(act):
            def split(gi, s, size, f=None, c=None):
                act.wait_ge(raw_in[s], 16 * (c // 2 + 1) if f is None
                            else f[0] * 16 + 16 * ((f[1] + 8 * gi) // 2 + 2))
                act.activation(w_hi[:, s, 0:size], raw[:, s, 0:size], ACT.Copy).then_inc(hi_done, 1)

            norm.act(act, g.xt, g.eps)
            split(0, 0, 2 * KT * P, c=0)
            for kt in range(KT):
                act.wait_ge(norm.normed, kt + 1)
                act.activation(x_hi[:, kt, :], g.xn[:, kt, :], ACT.Copy).then_inc(x_hi_done, 1)
            split(0, 1, 2 * KT * P, c=1)
            act.wait_ge(small_in, 32)

            def copy(f):
                s = f[1] % 2
                for vg in range(2):
                    if not starts(f):
                        if vg == 0:
                            act.wait_ge(joined, at(f, 1, -1))
                        act.wait_ge(convolved, at(f, 2, vg - 3))
                    act.wait_ge(projected, at(f, 2, vg + 1))
                    src = ps[:, s, vg, :, 0:H]
                    act.activation(pre[:, s, vg, 2:2 + N].rearrange("p (h n) -> p h n", h=2), src, ACT.Copy)
                    tap = conv_w[:, bass.ds(at(f, 6, 3 * vg + 2), 1)]
                    act.activation(conv[:, s, vg, :].rearrange("p (h n) -> p h n", h=2), src, ACT.Copy,
                                   scale=tap).then_inc(copied, 1)

            def silu(f):
                act.wait_ge(convolved, at(f, 2, 2))
                act.activation(gate[:, f[1] % 2, :], conv[:, f[1] % 2, 1, :], ACT.Silu).then_inc(gated, 1)

            for gi, (f0, n) in enumerate(groups):
                def pair(i, first, last_pair):
                    for f in ((i, f0), (i, f0 + 1)):
                        copy(f)
                        if not last_pair or f[1] == f0:
                            split(gi, f[1] % 2, n * P if last_pair else 2 * KT * P, f=f)
                        if not first or f[1] > f0:
                            silu(before(f))

                pairs(act, gi, pair)
                silu((n // 2 - 1, f0 + 1))
                split(gi, 1, n * P, f=(n // 2 - 1, f0 + 1))
                for m in range(KT):
                    c = f0 + n + 8 * gi + m + 2
                    if c < FT + 2 * KT:
                        act.wait_ge(out_done, KT * gi + m + 1)
                        split(gi, m % 2, n * P if m < KT - 2 else 2 * KT * P, c=c)

        @block.vector
        def _(dve):
            own = Steps(dve, dve_own)

            def split(s, size, count):
                dve.wait_ge(hi_done, count)
                dve.tensor_tensor(w_lo[:, s, 0:size], raw[:, s, 0:size], w_hi[:, s, 0:size], ALU.subtract).then_inc(lo_done, 1)

            dve.memset(pre[:, :, :, 0:2], 0.0).then_inc(zeroed, 1)
            norm.dve(dve, g.xt, g.xn)
            split(0, 2 * KT * P, 1)
            for kt in range(KT):
                dve.wait_ge(x_hi_done, kt + 1)
                dve.tensor_tensor(x_lo[:, kt, :], g.xn[:, kt, :], x_hi[:, kt, :], ALU.subtract).then_inc(x_lo_done, 1)
            split(1, 2 * KT * P, 2)
            dve.wait_ge(small_in, 32)
            dve.wait_ge(zeroed, 1)

            def taps(f, vg):
                dve.wait_ge(copied, at(f, 2, vg + 1))
                y, x = conv[:, f[1] % 2, vg, :], pre[:, f[1] % 2, vg, :]
                row = bass.ds(at(f, 2, vg), 1)
                w = [conv_w[:, bass.ds(at(f, 6, 3 * vg + j), 1)] for j in range(2)]
                old = [state[:, row, j, :].rearrange("p o b -> p (o b)") for j in range(2)]
                own.did(dve.scalar_tensor_tensor(y[:, 0:T], x[:, 1:1 + T], w[1], y[:, 0:T], ALU.mult, ALU.add))
                own.did(dve.scalar_tensor_tensor(y[:, T:N], old[1], w[1], y[:, T:N], ALU.mult, ALU.add))
                dve.tensor_copy(last[:, row, :].rearrange("p o c -> p (o c)"), x[:, T:T + 10])
                own.settle()
                dve.scalar_tensor_tensor(y[:, 0:T], x[:, 0:T], w[0], y[:, 0:T], ALU.mult, ALU.add)
                dve.scalar_tensor_tensor(y[:, T:N], old[0], w[0], y[:, T:N], ALU.mult, ALU.add).then_inc(convolved, 1)

            def join(f, f0):
                s = f[1] % 2
                k = bass.ds(at(f, 1, -f0), 1)
                dve.wait_ge(gated, at(f, 1, 1))
                dve.wait_ge(convolved, at(f, 2, 1))
                if not starts(f):
                    dve.wait_ge(joined, at(f, 1, 0))
                own.did(dve.tensor_tensor(flat(inner_hi[:, k, :]), conv[:, s, 0, :], gate[:, s, :], ALU.mult))
                own.did(dve.tensor_tensor(product[:, :], conv[:, s, 0, :], gate[:, s, :], ALU.mult))
                own.settle()
                dve.tensor_tensor(flat(inner_lo[:, k, :]), product[:, :], flat(inner_hi[:, k, :]), ALU.subtract).then_inc(joined, 1)

            for gi, (f0, n) in enumerate(groups):
                base = 6 * f0

                def pair(i, first, last_pair):
                    own.n, own.at = 0, (base if first else i * 12 + (base - 2))
                    for f in ((i, f0), (i, f0 + 1)):
                        taps(f, 0), taps(f, 1)
                        if not last_pair or f[1] == f0:
                            split(f[1] % 2, n * P if last_pair else 2 * KT * P, at(f, 1, 8 * gi + 3))
                        if not first or f[1] > f0:
                            join(before(f), f0)

                pairs(dve, gi, pair)
                join((n // 2 - 1, f0 + 1), f0)
                split(1, n * P, at((n // 2 - 1, f0 + 1), 1, 8 * gi + 3))
                for m in range(KT):
                    dve.wait_ge(out_done, KT * gi + m + 1)
                    x = g.xt[:, m, :].rearrange("p (h n) -> p h n", h=2)
                    dve.tensor_tensor(x, x, psf[:, 2 * (m % 4):2 * (m % 4) + 2, 0:H], ALU.add).then_inc(added, 1)
                    c = f0 + n + 8 * gi + m + 2
                    if c < FT + 2 * KT:
                        split(m % 2, n * P if m < KT - 2 else 2 * KT * P, c + 1)


class OutProjection:

    def __init__(self, sc, ps):
        self.ps = ps
        self.w = sc.sb("out_w", [P, KT, KT, P])
        self.w_in = [sc.sem(f"out_w_in{k}") for k in range(2)]
        self.done = sc.sem("out_done")
        self.added = sc.sem("out_added")

    def load(self, sp, src):
        for k in range(2):
            sp.dma_start(self.w[:, 4 * k:4 * k + 4].rearrange("p m k c -> p m (k c)"),
                         src[4 * k:4 * k + 4].rearrange("m p n -> p m n")).then_inc(self.w_in[k], 16)

    def pe(self, pe, y):
        for m in range(KT):
            pe.wait_ge(self.w_in[m // 4], 16)
            if m >= 4:
                pe.wait_ge(self.added, m - 3)
            for kt in range(KT):
                for h in range(2):
                    mm = pe.matmul(self.ps[:, 2 * (m % 4) + h, 0:H], self.w[:, m, kt, :],
                                   y[:, kt, h * H:(h + 1) * H], start=(kt == 0), stop=(kt == KT - 1))
            mm.then_inc(self.done, 1)

    def dve(self, dve, xt):
        for m in range(KT):
            dve.wait_ge(self.done, m + 1)
            x = xt[:, m, :].rearrange("p (h n) -> p h n", h=2)
            dve.tensor_tensor(x, x, self.ps[:, 2 * (m % 4):2 * (m % 4) + 2, 0:H], ALU.add).then_inc(self.added, 1)


def log1p_of(own, dve, out, x, tmp):
    s, z = tmp
    own.did(dve.tensor_scalar(z, x, 2.0, None, ALU.add))
    own.settle()
    own.did(dve.reciprocal(z, z))
    own.settle()
    own.did(dve.tensor_tensor(s, x, z, ALU.mult))
    own.settle()
    own.did(dve.tensor_tensor(z, s, s, ALU.mult))
    own.settle()
    terms = [2.0 / k for k in range(17, 0, -2)]
    own.did(dve.tensor_scalar(out, z, terms[0], terms[1], ALU.mult, ALU.add))
    for c in terms[2:]:
        own.settle()
        own.did(dve.tensor_tensor(out, out, z, ALU.mult))
        own.settle()
        own.did(dve.tensor_scalar(out, out, c, None, ALU.add))
    own.settle()
    own.did(dve.tensor_tensor(out, out, s, ALU.mult))
    own.settle()


def lru_stage(nc, d, o, g):
    with ExitStack() as ctx:
        sc = Scope(nc, ctx, "lru")
        w_in = sc.sb("w_in", [P, 2, 2, KT, P])
        small = sc.sb("small", [P, KT, 8])
        state = sc.sb("state", [P, KT, 3, B])
        h0 = sc.sb("h0", [P, KT, B])
        w_gates = sc.sb("w_gates", [P, 2, KT, P])
        pre = sc.sb("pre", [P, 2, 3 + N])
        xc = sc.sb("xc", [P, 2, N])
        raw = sc.sb("raw_gate", [P, 2, N])
        r = sc.sb("r", [P, 2, N])
        i_g = sc.sb("i", [P, 2, N])
        t2 = sc.sb("t", [P, 2, N])
        root = sc.sb("root", [P, 2, N])
        r1 = sc.sb("r1", [P, N])
        a = sc.sb("a", [P, N])
        bb = sc.sb("b", [P, N])
        hs = sc.sb("hs", [P, KT, N])
        gelu = sc.sb("gelu", [P, 2, N])
        y = sc.sb("y", [P, KT, N])
        rate = sc.sb("rate", [P, KT])
        rtmp = sc.sb("rtmp", [P, 4, KT])
        last = sc.sb("last", [P, KT, 11])
        ps = sc.ps("ps", [P, 8, 512])
        norm = Norm(sc, g.norm_g[:, 2, :], ps)
        proj = OutProjection(sc, ps)
        small_in = sc.sem("small_in")
        w_in_in = [sc.sem(f"w_in_in{s}") for s in range(2)]
        zeroed = sc.sem("zeroed")
        projected = sc.sem("projected")
        copied = sc.sem("copied")
        convolved = sc.sem("convolved")
        gates_done = sc.sem("gates_done")
        activated = sc.sem("activated")
        rooted = sc.sem("rooted")
        gelued = sc.sem("gelued")
        finished = sc.sem("finished")
        abs_done = sc.sem("abs_done")
        exp_done = sc.sem("exp_done")
        rate_done = sc.sem("rate_done")
        act_own = sc.sem("act_own")
        dve_own = sc.sem("dve_own")
        stored = sc.sem("stored")
        block = ctx.enter_context(nc.Block())

        @block.sync
        def _(sp):
            sp.dma_start(w_in[:, 0], d["lru_w_in"][0]).then_inc(w_in_in[0], 16)
            sp.dma_start(small[:], d["lru_small"]).then_inc(small_in, 16)
            sp.dma_start(state[:], d["lru_state"]).then_inc(small_in, 16)
            sp.dma_start(h0[:], d["lru_h0"]).then_inc(small_in, 16)
            sp.dma_start(w_gates[:], d["lru_w_gates"]).then_inc(small_in, 16)
            sp.dma_start(w_in[:, 1], d["lru_w_in"][1]).then_inc(w_in_in[1], 16)
            for n in range(2, KT):
                sp.wait_ge(projected, 2 * (n - 1))
                sp.dma_start(w_in[:, n % 2], d["lru_w_in"][n]).then_inc(w_in_in[n % 2], 16)
                if n == 3:
                    proj.load(sp, d["lru_w_out"])
            sp.wait_ge(finished, KT)
            sp.dma_start(o["lru_last"], last[:]).then_inc(stored, 16)
            sp.dma_start(o["lru_h"], hs[:, :, T - 1:N]).then_inc(stored, 16)
            sp.dma_start(o["lru_old"], state[:, :, 1:3, :]).then_inc(stored, 16)
            sp.wait_ge(stored, 48)

        @block.tensor
        def _(pe):
            norm.pe(pe, g.ones)
            pe.wait_ge(norm.normed, KT)
            pe.wait_ge(small_in, 64)

            def gate_products(n):
                pe.wait_ge(convolved, n + 1)
                if n >= 1:
                    pe.wait_ge(activated, n)
                for w in range(2):
                    for h in range(2):
                        mm = pe.matmul(ps[:, 4 + 2 * w + h, 0:H], w_gates[:, w, n, :],
                                       xc[:, n % 2, h * H:(h + 1) * H], start=True, stop=True)
                mm.then_inc(gates_done, 1)

            for n in range(KT):
                pe.wait_ge(w_in_in[n % 2], 16 * (n // 2 + 1))
                for w in range(2):
                    if n >= 1:
                        pe.wait_ge(copied, 2 * (n - 1) + w + 1)
                    for kt in range(KT):
                        for h in range(2):
                            mm = pe.matmul(ps[:, 2 * w + h, 0:H], w_in[:, n % 2, w, kt, :],
                                           g.xn[:, kt, h * H:(h + 1) * H], start=(kt == 0), stop=(kt == KT - 1))
                    mm.then_inc(projected, 1)
                if n >= 1:
                    gate_products(n - 1)
            gate_products(KT - 1)
            pe.wait_ge(finished, KT)
            proj.pe(pe, y)

        @block.scalar
        def _(act):
            norm.act(act, g.xt, g.eps)
            act.wait_ge(small_in, 64)
            own = Steps(act, act_own)
            act.wait_ge(abs_done, 1)
            act.activation(rtmp[:, 1, :], rtmp[:, 0, :], ACT.Exp, scale=-1.0).then_inc(exp_done, 1)

            def halves(ap):
                return ap.rearrange("p (h n) -> p h n", h=2)

            def gates(n):
                s = n % 2
                act.wait_ge(gates_done, n + 1)
                if n >= 2:
                    act.wait_ge(finished, n - 1)
                own.did(act.activation(halves(r[:, s, :]), ps[:, 4:6, 0:H], ACT.Sigmoid, bias=small[:, n, 5:6]))
                act.activation(halves(i_g[:, s, :]), ps[:, 6:8, 0:H], ACT.Sigmoid, bias=small[:, n, 6:7])
                own.settle()
                act.wait_ge(rate_done, 1)
                act.activation(t2[:, s, :], r[:, s, :], ACT.Tanh, scale=rate[:, n:n + 1]).then_inc(activated, 1)
                act.wait_ge(activated, n + 1)
                act.activation(gelu[:, s, :], raw[:, s, :], ACT.Gelu_apprx_tanh).then_inc(gelued, 1)
                act.activation(root[:, s, :], t2[:, s, :], ACT.Sqrt).then_inc(rooted, 1)

            for n in range(KT):
                s = n % 2
                act.wait_ge(projected, 2 * n + 1)
                if n >= 2:
                    act.wait_ge(finished, n - 1)
                act.activation(halves(pre[:, s, 3:3 + N]), ps[:, 0:2, 0:H], ACT.Copy)
                act.activation(halves(xc[:, s, :]), ps[:, 0:2, 0:H], ACT.Identity, bias=small[:, n, 4:5],
                               scale=small[:, n, 3:4]).then_inc(copied, 1)
                act.wait_ge(projected, 2 * n + 2)
                act.activation(halves(raw[:, s, :]), ps[:, 2:4, 0:H], ACT.Copy).then_inc(copied, 1)
                if n >= 1:
                    gates(n - 1)
            gates(KT - 1)

        @block.vector
        def _(dve):
            own = Steps(dve, dve_own)
            dve.memset(pre[:, :, 0:3], 0.0).then_inc(zeroed, 1)
            norm.dve(dve, g.xt, g.xn)
            dve.wait_ge(small_in, 64)
            dve.wait_ge(zeroed, 1)
            lam = small[:, :, 7]
            dve.scalar_tensor_tensor(rtmp[:, 0, :], lam, -1.0, lam, ALU.mult, ALU.max).then_inc(abs_done, 1)
            dve.wait_ge(exp_done, 1)
            log1p_of(own, dve, rate[:, :], rtmp[:, 1, :], (rtmp[:, 2, :], rtmp[:, 3, :]))
            own.did(dve.tensor_scalar(rtmp[:, 0, :], lam, -1.0, 0.0, ALU.mult, ALU.max))
            own.settle()
            own.did(dve.tensor_tensor(rate[:, :], rate[:, :], rtmp[:, 0, :], ALU.add))
            own.settle()
            dve.tensor_scalar(rate[:, :], rate[:, :], 4.0, None, ALU.mult).then_inc(rate_done, 1)

            def recur(n):
                s = n % 2
                dve.wait_ge(rooted, n + 1)
                own.did(dve.tensor_scalar(r1[:, :], t2[:, s, :], 1.0, None, ALU.add))
                dve.tensor_tensor(i_g[:, s, :], i_g[:, s, :], xc[:, s, :], ALU.mult)
                own.settle()
                own.did(dve.reciprocal(r1[:, :], r1[:, :]))
                own.settle()
                own.did(dve.tensor_scalar(a[:, :], r1[:, :], 2.0, -1.0, ALU.mult, ALU.add))
                own.did(dve.scalar_tensor_tensor(bb[:, :], root[:, s, :], 2.0, r1[:, :], ALU.mult, ALU.mult))
                own.settle()
                own.did(dve.tensor_tensor(bb[:, :], bb[:, :], i_g[:, s, :], ALU.mult))
                own.settle()
                own.did(dve.tensor_tensor_scan(hs[:, n, 0:T], a[:, 0:T], bb[:, 0:T], 0.0, ALU.mult, ALU.add))
                own.did(dve.tensor_tensor(hs[:, n, T:N], a[:, T:N], h0[:, n, :], ALU.mult))
                own.settle()
                own.did(dve.tensor_tensor(hs[:, n, T:N], hs[:, n, T:N], bb[:, T:N], ALU.add))
                own.settle()
                dve.wait_ge(gelued, n + 1)
                dve.tensor_tensor(y[:, n, :], hs[:, n, :], gelu[:, s, :], ALU.mult).then_inc(finished, 1)

            for n in range(KT):
                s = n % 2
                dve.wait_ge(copied, 2 * n + 1)
                x, u = pre[:, s, :], xc[:, s, :]
                for j in (2, 1, 0):
                    own.did(dve.scalar_tensor_tensor(u[:, 0:T], x[:, j:j + T], small[:, n, j:j + 1], u[:, 0:T],
                                                     ALU.mult, ALU.add))
                    ins = dve.scalar_tensor_tensor(u[:, T:N], state[:, n, j, :], small[:, n, j:j + 1], u[:, T:N],
                                                   ALU.mult, ALU.add)
                    if j:
                        own.did(ins)
                        own.settle()
                    else:
                        ins.then_inc(convolved, 1)
                dve.tensor_copy(last[:, n, :], x[:, T:T + 11])
                if n >= 1:
                    recur(n - 1)
            recur(KT - 1)
            proj.dve(dve, g.xt)


GH = 8
GR = 40


def gdn_project(nc, d, o, g, v):
    with ExitStack() as ctx:
        sc = Scope(nc, ctx, "gdnp")
        w_in = sc.sb("w_in", [P, 2, 4, KT, P])
        w_ab = sc.sb("w_ab", [P, KT, GR])
        taps_w = sc.sb("taps", [P, GH, 3, 4])
        state = sc.sb("state", [P, GH, 3, 3, B])
        heads_w = sc.sb("head_w", [GH, 2])
        decay = sc.sb("decay", [GH, 1])
        pre = sc.sb("pre", [P, 3, 3 + N])
        conv = sc.sb("conv", [P, 3, N])
        sq = sc.sb("sq", [P, 2, N])
        rs = sc.sb("rs", [P, 2, N])
        last = sc.sb("last", [P, GH, 3, 11])
        soft = sc.sb("soft", [GH, 4, N])
        ps = sc.ps("ps", [P, 8, 512])
        norm = Norm(sc, g.norm_g[:, 1, :], ps)
        small_in = sc.sem("small_in")
        w_in_in = [sc.sem(f"w_in_in{s}") for s in range(2)]
        zeroed = sc.sem("zeroed")
        ab_done = sc.sem("ab_done")
        ab_copied = sc.sem("ab_copied")
        abs_done = sc.sem("abs_done")
        exp_done = sc.sem("exp_done")
        projected = sc.sem("projected")
        copied = sc.sem("copied")
        convolved = sc.sem("convolved")
        silued = sc.sem("silued")
        squared = sc.sem("squared")
        summed = sc.sem("summed")
        rooted = sc.sem("rooted")
        scaled = sc.sem("scaled")
        cum_done = sc.sem("cum_done")
        turned = sc.sem("turned")
        dve_own = sc.sem("dve_own")
        stored = sc.sem("stored")
        block = ctx.enter_context(nc.Block())
        qkv = [v.q, v.k, v.v]

        @block.sync
        def _(sp):
            sp.dma_start(w_ab[:], d["gdn_w_ab"]).then_inc(small_in, 16)
            sp.dma_start(heads_w[:], d["gdn_head_w"]).then_inc(small_in, 16)
            sp.dma_start(w_in[:, 0], d["gdn_w_in"][0]).then_inc(w_in_in[0], 16)
            sp.dma_start(taps_w[:], d["gdn_taps"]).then_inc(small_in, 16)
            sp.dma_start(state[:], d["gdn_conv_state"]).then_inc(small_in, 16)
            sp.dma_start(v.norm_g[:], d["gdn_norm_g"]).then_inc(small_in, 16)
            sp.dma_start(w_in[:, 1], d["gdn_w_in"][1]).then_inc(w_in_in[1], 16)
            for h in range(2, GH):
                sp.wait_ge(projected, 4 * (h - 1))
                sp.dma_start(w_in[:, h % 2], d["gdn_w_in"][h]).then_inc(w_in_in[h % 2], 16)
            sp.wait_ge(convolved, 3 * GH)
            sp.dma_start(o["gdn_last"], last[:]).then_inc(stored, 16)
            sp.dma_start(o["gdn_old"], state[:, :, :, 1:3, :]).then_inc(stored, 16)
            sp.wait_ge(stored, 32)

        @block.tensor
        def _(pe):
            norm.pe(pe, g.ones)
            pe.wait_ge(norm.normed, KT)
            pe.wait_ge(small_in, 80)
            for kt in range(KT):
                for h in range(2):
                    mm = pe.matmul(ps[0:GR, 6 + h, 0:H], w_ab[:, kt, :], g.xn[:, kt, h * H:(h + 1) * H],
                                   start=(kt == 0), stop=(kt == KT - 1))
            mm.then_inc(ab_done, 1)

            def sums(h):
                for t in range(2):
                    at = 2 * h + t
                    pe.wait_ge(squared, at + 1)
                    if at == 0:
                        pe.wait_ge(ab_copied, 1)
                    else:
                        pe.wait_ge(rooted, at)
                    for u in range(2):
                        mm = pe.matmul(ps[:, 6 + u, 0:H], g.ones, sq[:, t, u * H:(u + 1) * H], start=True, stop=True)
                    mm.then_inc(summed, 1)

            for h in range(GH):
                pe.wait_ge(w_in_in[h % 2], 16 * (h // 2 + 1))
                for t in range(4):
                    at = 4 * h + t
                    if at >= 3:
                        pe.wait_ge(copied, at - 2)
                    for kt in range(KT):
                        for u in range(2):
                            mm = pe.matmul(ps[:, 2 * (at % 3) + u, 0:H], w_in[:, h % 2, t, kt, :],
                                           g.xn[:, kt, u * H:(u + 1) * H], start=(kt == 0), stop=(kt == KT - 1))
                    mm.then_inc(projected, 1)
                if h >= 1:
                    sums(h - 1)
            sums(GH - 1)
            pe.wait_ge(cum_done, 1)
            for c in range(NCH):
                mm = pe.transpose(ps[:, 0, GH * c:GH * c + GH], v.rows[0:GH, c * CH:(c + 1) * CH],
                                  g.ident[0:GH, 0:GH])
            mm.then_inc(turned, 1)

        @block.scalar
        def _(act):
            norm.act(act, g.xt, g.eps)
            act.wait_ge(small_in, 80)
            act.wait_ge(zeroed, 1)
            act.wait_ge(ab_done, 1)
            act.activation(soft[:, 0, :].rearrange("p (h n) -> p h n", h=2), ps[0:GH, 6:8, 0:H], ACT.Identity,
                           bias=heads_w[:, 1:2])
            act.activation(v.rows[32:GR, :].rearrange("p (h n) -> p h n", h=2), ps[32:GR, 6:8, 0:H],
                           ACT.Sigmoid).then_inc(ab_copied, 1)
            act.wait_ge(abs_done, 1)
            act.activation(decay[:, :], heads_w[:, 0:1], ACT.Exp)
            act.activation(soft[:, 1, :], soft[:, 1, :], ACT.Exp, scale=-1.0).then_inc(exp_done, 1)

            def norms(h):
                for t in range(2):
                    act.wait_ge(summed, 2 * h + t + 1)
                    if h >= 1:
                        act.wait_ge(scaled, 2 * (h - 1) + t + 1)
                    act.activation(rs[:, t, :].rearrange("p (h n) -> p h n", h=2), ps[:, 6:8, 0:H], ACT.Sqrt,
                                   bias=g.eps[:, 0:1]).then_inc(rooted, 1)

            for h in range(GH):
                for t in range(3):
                    at = 4 * h + t
                    act.wait_ge(projected, at + 1)
                    if h >= 1:
                        act.wait_ge(convolved, 3 * (h - 1) + t + 1)
                        act.wait_ge(silued, h)
                    src = ps[:, 2 * (at % 3):2 * (at % 3) + 2, 0:H]
                    act.activation(pre[:, t, 3:3 + N].rearrange("p (h n) -> p h n", h=2), src, ACT.Copy)
                    act.activation(conv[:, t, :].rearrange("p (h n) -> p h n", h=2), src, ACT.Copy,
                                   scale=taps_w[:, h, t, 3:4]).then_inc(copied, 1)
                at = 4 * h + 3
                act.wait_ge(projected, at + 1)
                act.activation(v.gate[:, h, :].rearrange("p (h n) -> p h n", h=2),
                               ps[:, 2 * (at % 3):2 * (at % 3) + 2, 0:H], ACT.Silu).then_inc(copied, 1)
                for t in range(3):
                    act.wait_ge(convolved, 3 * h + t + 1)
                    ins = act.activation(qkv[t][:, h, :], conv[:, t, :], ACT.Silu)
                ins.then_inc(silued, 1)
                if h >= 1:
                    norms(h - 1)
                act.wait_ge(silued, h + 1)
                for t in range(2):
                    if h >= 1:
                        act.wait_ge(summed, 2 * (h - 1) + t + 1)
                    act.activation(sq[:, t, :], qkv[t][:, h, :], ACT.Square).then_inc(squared, 1)
            norms(GH - 1)

        @block.vector
        def _(dve):
            own = Steps(dve, dve_own)
            dve.memset(pre[:, :, 0:3], 0.0)
            dve.memset(v.rows[:, :], 0.0).then_inc(zeroed, 1)
            norm.dve(dve, g.xt, g.xn)
            dve.wait_ge(small_in, 80)
            dve.wait_ge(zeroed, 1)
            dve.wait_ge(ab_copied, 1)
            dve.scalar_tensor_tensor(soft[:, 1, :], soft[:, 0, :], -1.0, soft[:, 0, :], ALU.mult,
                                     ALU.max).then_inc(abs_done, 1)
            dve.wait_ge(exp_done, 1)
            log1p_of(own, dve, v.rows[0:GH, :], soft[:, 1, :], (soft[:, 2, :], soft[:, 3, :]))
            own.did(dve.scalar_tensor_tensor(soft[:, 1, :], soft[:, 0, :], 0.0, v.rows[0:GH, :], ALU.max, ALU.add))
            own.settle()
            own.did(dve.tensor_scalar(soft[:, 0, :], soft[:, 1, :], decay[:, 0:1], -1.0, ALU.mult, ALU.mult))
            own.did(dve.memset(soft[:, 2, 0:CH], 1.0))
            own.settle()
            for c in range(NCH):
                sl = slice(c * CH, (c + 1) * CH)
                dve.tensor_tensor_scan(v.rows[0:GH, sl], soft[:, 2, 0:CH], soft[:, 0, sl], 0.0, ALU.mult, ALU.add)
            dve.tensor_copy(v.rows[0:GH, T:N], soft[:, 0, T:N]).then_inc(cum_done, 1)

            def scale(h):
                for t in range(2):
                    dve.wait_ge(rooted, 2 * h + t + 1)
                    own.did(dve.reciprocal(rs[:, t, :], rs[:, t, :]))
                    own.settle()
                    x = qkv[t][:, h, :]
                    dve.scalar_tensor_tensor(x, x, CH ** -0.5 if t == 0 else 1.0, rs[:, t, :], ALU.mult,
                                             ALU.mult).then_inc(scaled, 1)

            for h in range(GH):
                for t in range(3):
                    dve.wait_ge(copied, 4 * h + t + 1)
                    x, u = pre[:, t, :], conv[:, t, :]
                    for j in (2, 1, 0):
                        w = taps_w[:, h, t, j:j + 1]
                        own.did(dve.scalar_tensor_tensor(u[:, 0:T], x[:, j:j + T], w, u[:, 0:T], ALU.mult, ALU.add))
                        own.did(dve.scalar_tensor_tensor(u[:, T:N], state[:, h, t, j, :], w, u[:, T:N],
                                                         ALU.mult, ALU.add))
                        own.settle()
                    dve.tensor_copy(last[:, h, t, :], x[:, T:T + 11]).then_inc(convolved, 1)
                if h >= 1:
                    scale(h - 1)
            scale(GH - 1)
            dve.wait_ge(turned, 1)
            own.did(dve.tensor_copy(v.cum_tok[:, :, :], ps[:, 0, 0:NCH * GH].rearrange("p (c h) -> p c h", c=NCH)))
            for i in range(2 * GH):
                k = i if i < GH else 32 + i - GH
                dve.tensor_copy(v.spread[:, i, :], g.ident[:, k:k + 1].to_broadcast([P, P]))


def gdn_chunks(nc, d, o, g, v):
    pe_steps = ["spread_g", "spread_b", "qk", "kk", "turn_l", "square0", "square_t0", "grow0", "square1", "square_t1",
                "grow1", "square2", "grow2", "pair0", "turn0", "join0", "pair1", "turn1", "join1", "pair2",
                "turn2", "join2", "turn_v", "k_state", "solve", "turn_k", "out", "update"]
    act_steps = ["exp_g", "exp_decay", "lower", "power0", "power_t0", "power1", "power_t1", "power2", "paired0", "inv0",
                 "paired1", "inv1", "paired2", "inv2", "v_tok", "u"]
    dve_steps = ["k", "k_beta", "v_beta", "decay", "q_exp", "k_exp", "attn", "lower_t", "strict", "power_t", "inv_t",
                 "power", "grown0", "grown1", "grown2", "mask0", "joined0", "mask1", "joined1", "mask2", "joined2",
                 "rhs", "k_left", "store_o", "decay_s", "add_s"]
    with ExitStack() as ctx:
        sc = Scope(nc, ctx, "gdnc")
        names = ("k", "exp_g", "decay", "k_beta", "q_exp", "k_exp", "v_beta", "lower_t", "attn", "lower", "power",
                 "power_t", "inv_t", "inv", "mask", "u", "rhs", "k_left")
        buf = {n: sc.sb(n, [P, 2, 4, CH]) for n in names}
        state = sc.sb("state", [P, 2, 4, CH])
        ps = sc.ps("ps", [P, 2, 4, 4, CH])
        pe_did = [sc.sem(f"pe_did{x}") for x in range(2)]
        act_did = [sc.sem(f"act_did{x}") for x in range(2)]
        dve_did = [sc.sem(f"dve_did{x}") for x in range(2)]
        cleared = sc.sem("cleared")
        stored = sc.sem("stored")
        block = ctx.enter_context(nc.Block())

        def after(eng, who, x, step, c):
            sem, steps = {"pe": (pe_did, pe_steps), "act": (act_did, act_steps), "dve": (dve_did, dve_steps)}[who]
            eng.wait_ge(sem[x], c * len(steps) + (steps.index(step) + 1 if step else 0))

        def chunk(t, x, c):
            return t[:, 4 * x:4 * x + 4, bass.ds(c * CH, CH)]

        def wide(col):
            return col.to_broadcast([P, 4, CH])

        def mask(m):
            return m.rearrange("p (o c) -> p o c", o=1).to_broadcast([P, 4, CH])

        @block.tensor
        def _(pe):
            pe.wait_ge(cleared, 1)

            def products(x, bank, lhs, rhs):
                for j in range(4):
                    mm = pe.matmul(ps[:, x, bank, j, :], lhs(j), rhs(j), start=True, stop=True)
                mm.then_inc(pe_did[x], 1)

            def turns(x, bank, src):
                for j in range(4):
                    mm = pe.transpose(ps[:, x, bank, j, :], src[:, x, j, :], g.ident)
                mm.then_inc(pe_did[x], 1)

            with pe.Fori(0, NCH) as c:
                cols = bass.ds(c * CH, CH)
                for x in range(2):
                    after(pe, "dve", x, None, c)
                    after(pe, "act", x, None, c)
                    products(x, 0, lambda j: v.spread[:, 4 * x + j, :], lambda j: v.rows[:, cols])
                    products(x, 1, lambda j: v.spread[:, GH + 4 * x + j, :], lambda j: v.rows[:, cols])
                for x in range(2):
                    after(pe, "dve", x, "k", c)
                    products(x, 3, lambda j: buf["k"][:, x, j, :], lambda j: flat(v.q[:, 4 * x + j:4 * x + j + 1, cols]))
                for x in range(2):
                    after(pe, "dve", x, "k_beta", c)
                    products(x, 2, lambda j: buf["k"][:, x, j, :], lambda j: buf["k_beta"][:, x, j, :])
                for x in range(2):
                    after(pe, "dve", x, "strict", c)
                    turns(x, 0, buf["lower_t"])
                for e in range(3):
                    for x in range(2):
                        if e == 0:
                            after(pe, "dve", x, "power", c)
                        else:
                            after(pe, "act", x, f"power_t{e - 1}", c)
                        products(x, 2, lambda j: buf["power_t"][:, x, j, :], lambda j: buf["power"][:, x, j, :])
                        if e < 2:
                            products(x, 3, lambda j: buf["power"][:, x, j, :], lambda j: buf["power_t"][:, x, j, :])
                    for x in range(2):
                        after(pe, "act", x, f"power{e}", c)
                        after(pe, "dve", x, "inv_t" if e == 0 else f"grown{e - 1}", c)
                        products(x, 1, lambda j: buf["power"][:, x, j, :], lambda j: buf["inv_t"][:, x, j, :])
                for m in range(3):
                    for x in range(2):
                        after(pe, "dve", x, "grown2" if m == 0 else f"joined{m - 1}", c)
                        after(pe, "dve", x, f"mask{m}", c)
                        products(x, 2, lambda j: buf["mask"][:, x, j, :], lambda j: buf["inv_t"][:, x, j, :])
                        turns(x, 3, buf["inv_t"])
                    for x in range(2):
                        after(pe, "act", x, f"inv{m}", c)
                        products(x, 1, lambda j: buf["inv"][:, x, j, :], lambda j: buf["u"][:, x, j, :])
                for x in range(2):
                    turns(x, 0, buf["v_beta"])
                    after(pe, "dve", x, "joined2", c)
                    products(x, 1, lambda j: buf["k_exp"][:, x, j, :], lambda j: state[:, x, j, :])
                for x in range(2):
                    after(pe, "dve", x, "rhs", c)
                    products(x, 2, lambda j: buf["inv_t"][:, x, j, :], lambda j: buf["rhs"][:, x, j, :])
                    turns(x, 0, buf["k"])
                for x in range(2):
                    after(pe, "act", x, "u", c)
                    for j in range(4):
                        pe.matmul(ps[:, x, 3, j, :], state[:, x, j, :], buf["q_exp"][:, x, j, :], start=True, stop=False)
                        mm = pe.matmul(ps[:, x, 3, j, :], buf["u"][:, x, j, :], buf["attn"][:, x, j, :],
                                       start=False, stop=True)
                    mm.then_inc(pe_did[x], 1)
                    after(pe, "dve", x, "k_left", c)
                    products(x, 1, lambda j: buf["k_left"][:, x, j, :], lambda j: buf["u"][:, x, j, :])

        @block.scalar
        def _(act):
            def run(x, out, src, func=ACT.Copy):
                act.activation(out, src, func).then_inc(act_did[x], 1)

            with act.Fori(0, NCH) as c:
                for x in range(2):
                    after(act, "dve", x, None, c)
                    after(act, "pe", x, "spread_g", c)
                    run(x, buf["exp_g"][:, x], ps[:, x, 0], ACT.Exp)
                for x in range(2):
                    after(act, "dve", x, "decay", c)
                    run(x, buf["decay"][:, x], buf["decay"][:, x], ACT.Exp)
                for x in range(2):
                    after(act, "pe", x, "turn_l", c)
                    run(x, buf["lower"][:, x], ps[:, x, 0])
                for e in range(3):
                    for x in range(2):
                        after(act, "pe", x, f"square_t{e}" if e < 2 else "square2", c)
                        run(x, buf["power"][:, x], ps[:, x, 2])
                        if e < 2:
                            run(x, buf["power_t"][:, x], ps[:, x, 3])
                for m in range(3):
                    for x in range(2):
                        after(act, "pe", x, f"pair{m}", c)
                        run(x, buf["u"][:, x], ps[:, x, 2])
                        after(act, "pe", x, f"turn{m}", c)
                        run(x, buf["inv"][:, x], ps[:, x, 3])
                for x in range(2):
                    after(act, "pe", x, "turn_v", c)
                    run(x, buf["rhs"][:, x], ps[:, x, 0])
                for x in range(2):
                    after(act, "pe", x, "solve", c)
                    run(x, buf["u"][:, x], ps[:, x, 2])

        @block.vector
        def _(dve):
            def tt(x, out, a, b, op=ALU.mult):
                dve.tensor_tensor(out, a, b, op).then_inc(dve_did[x], 1)

            dve.memset(state[:], 0.0).then_inc(cleared, 1)
            dve.wait_ge(cleared, 1)
            with dve.Fori(0, NCH) as c:
                for x in range(2):
                    after(dve, "pe", x, None, c)
                    dve.tensor_copy(buf["k"][:, x], chunk(v.k, x, c)).then_inc(dve_did[x], 1)
                for x in range(2):
                    after(dve, "pe", x, "spread_b", c)
                    after(dve, "dve", x, "k", c)
                    tt(x, buf["k_beta"][:, x], buf["k"][:, x], ps[:, x, 1])
                    tt(x, buf["v_beta"][:, x], chunk(v.v, x, c), ps[:, x, 1])
                    after(dve, "act", x, "exp_g", c)
                    for j in range(4):
                        at = v.cum_tok[:, bass.ds(c, 1), 4 * x + j:4 * x + j + 1].rearrange("p a b -> p (a b)")
                        ins = dve.scalar_tensor_tensor(buf["decay"][:, x, j, :], ps[:, x, 0, j, :], at,
                                                       g.neg_upper, ALU.subtract, ALU.add)
                    ins.then_inc(dve_did[x], 1)
                for x in range(2):
                    tt(x, buf["q_exp"][:, x], chunk(v.q, x, c), buf["exp_g"][:, x])
                    after(dve, "dve", x, "k_beta", c)
                    tt(x, buf["k_exp"][:, x], buf["k_beta"][:, x], buf["exp_g"][:, x])
                for x in range(2):
                    after(dve, "act", x, "exp_decay", c)
                    after(dve, "pe", x, "qk", c)
                    tt(x, buf["attn"][:, x], ps[:, x, 3], buf["decay"][:, x])
                    after(dve, "pe", x, "kk", c)
                    tt(x, buf["lower_t"][:, x], ps[:, x, 2], buf["decay"][:, x])
                for x in range(2):
                    after(dve, "dve", x, "lower_t", c)
                    tt(x, buf["lower_t"][:, x], buf["lower_t"][:, x], mask(g.strict_t))
                for x in range(2):
                    after(dve, "dve", x, "strict", c)
                    dve.scalar_tensor_tensor(buf["power_t"][:, x], buf["lower_t"][:, x], -1.0, mask(g.same16),
                                             ALU.mult, ALU.mult).then_inc(dve_did[x], 1)
                for x in range(2):
                    after(dve, "dve", x, "power_t", c)
                    tt(x, buf["inv_t"][:, x], buf["power_t"][:, x], mask(g.ident), ALU.add)
                for x in range(2):
                    after(dve, "act", x, "lower", c)
                    dve.scalar_tensor_tensor(buf["power"][:, x], buf["lower"][:, x], -1.0, mask(g.same16),
                                             ALU.mult, ALU.mult).then_inc(dve_did[x], 1)
                for e in range(3):
                    for x in range(2):
                        after(dve, "pe", x, f"grow{e}", c)
                        tt(x, buf["inv_t"][:, x], buf["inv_t"][:, x], ps[:, x, 1], ALU.add)
                for m, pair in enumerate((g.pair16, g.pair32, g.pair64)):
                    for x in range(2):
                        if m:
                            after(dve, "pe", x, f"pair{m - 1}", c)
                        tt(x, buf["mask"][:, x], buf["lower"][:, x], mask(pair))
                    for x in range(2):
                        after(dve, "pe", x, f"join{m}", c)
                        tt(x, buf["inv_t"][:, x], buf["inv_t"][:, x], ps[:, x, 1], ALU.subtract)
                for x in range(2):
                    after(dve, "act", x, "v_tok", c)
                    after(dve, "pe", x, "k_state", c)
                    tt(x, buf["rhs"][:, x], buf["rhs"][:, x], ps[:, x, 1], ALU.subtract)
                for x in range(2):
                    after(dve, "pe", x, "turn_k", c)
                    tt(x, buf["k_left"][:, x], ps[:, x, 0], wide(buf["decay"][:, x, :, CH - 1:CH]))
                for x in range(2):
                    after(dve, "pe", x, "out", c)
                    dve.tensor_copy(chunk(v.y, x, c), ps[:, x, 3]).then_inc(dve_did[x], 1)
                    tt(x, state[:, x], state[:, x], wide(buf["exp_g"][:, x, :, CH - 1:CH]))
                for x in range(2):
                    after(dve, "pe", x, "update", c)
                    after(dve, "dve", x, "decay_s", c)
                    tt(x, state[:, x], state[:, x], ps[:, x, 1], ALU.add)

        @block.sync
        def _(sp):
            for x in range(2):
                after(sp, "dve", x, None, NCH)
            sp.dma_start(o["gdn_state_p"], state[:]).then_inc(stored, 16)
            sp.wait_ge(stored, 16)


SQ = 16


def gdn_samples(nc, d, o, g, v):
    with ExitStack() as ctx:
        sc = Scope(nc, ctx, "gdns")
        pairs = GH * B
        state = sc.sb("state", [P, pairs, P])
        kq = sc.sb("kq", [P, pairs, 2])
        qk = sc.sb("qk", [P, pairs])
        eg, beta, u, t1, t2, dot = [sc.sb(n, [P, pairs]) for n in ("exp_g", "beta", "u", "t1", "t2", "dot")]
        k_t = sc.sb("k_t", [pairs, P])
        u_t = sc.sb("u_t", [pairs, P])
        spread_u = sc.sb("spread_u", [pairs, 2, SQ, P])
        ps = sc.ps("ps", [P, 8, 512])
        states_in = sc.sem("states_in")
        packed = sc.sem("packed")
        spread = sc.sem("spread")
        read = sc.sem("read")
        applied = sc.sem("applied")
        act_done = sc.sem("act_done")
        solved = sc.sem("solved")
        turned = sc.sem("turned")
        turned_copied = sc.sem("turned_copied")
        masked = sc.sem("masked")
        outer = sc.sem("outer")
        updated = sc.sem("updated")
        dve_own = sc.sem("dve_own")
        stored = sc.sem("stored")
        block = ctx.enter_context(nc.Block())

        def cols(t):
            return t[:, :, T:N]

        def by_head(t):
            return t.rearrange("p (h b) -> p h b", b=B)

        @block.sync
        def _(sp):
            sp.dma_start(state[:], d["gdn_state"]).then_inc(states_in, 16)
            for k in range(4):
                sp.wait_ge(updated, k + 1)
                sp.dma_start(o["gdn_state_s"][:, k * SQ:(k + 1) * SQ, :], state[:, k * SQ:(k + 1) * SQ, :]).then_inc(stored, 16)
            sp.wait_ge(stored, 64)

        @block.tensor
        def _(pe):
            for h in range(GH):
                pe.matmul(ps[:, 0, B * h:B * h + B], v.spread[:, h, :], v.rows[:, T:N], start=True, stop=True)
            for h in range(GH):
                mm = pe.matmul(ps[:, 1, B * h:B * h + B], v.spread[:, GH + h, :], v.rows[:, T:N], start=True, stop=True)
            mm.then_inc(spread, 1)
            pe.wait_ge(packed, 2)
            pe.matmul(ps[:, 2, 0:pairs], g.ones, qk[:, :], start=True, stop=True).then_inc(spread, 1)
            pe.transpose(ps[0:pairs, 3, 0:P], kq[:, :, 0], g.ident).then_inc(turned, 1)
            pe.wait_ge(states_in, 16)
            for i in range(pairs):
                mm = pe.matmul(ps[:, 4, 2 * i:2 * i + 2], state[:, i, :], kq[:, i, :], start=True, stop=True)
            mm.then_inc(applied, 1)
            pe.wait_ge(solved, 1)
            pe.transpose(ps[0:pairs, 5, 0:P], u[:, :], g.ident).then_inc(turned, 1)
            for k in range(4):
                pe.wait_ge(masked, k + 1)
                pe.wait_ge(turned_copied, 2)
                if k:
                    pe.wait_ge(updated, k)
                for n in range(4):
                    mm = pe.matmul(ps[:, n, :], k_t[:, :],
                                   spread_u[:, k % 2, 4 * n:4 * n + 4, :].rearrange("p a c -> p (a c)"),
                                   start=True, stop=True)
                mm.then_inc(outer, 1)

        @block.scalar
        def _(act):
            act.wait_ge(spread, 1)
            act.activation(eg[:, :], ps[:, 0, 0:pairs], ACT.Exp)
            act.activation(beta[:, :], ps[:, 1, 0:pairs], ACT.Copy).then_inc(act_done, 1)
            act.wait_ge(turned, 1)
            act.activation(k_t[:, :], ps[0:pairs, 3, 0:P], ACT.Copy).then_inc(turned_copied, 1)
            act.wait_ge(turned, 2)
            act.activation(u_t[:, :], ps[0:pairs, 5, 0:P], ACT.Copy).then_inc(turned_copied, 1)

        @block.vector
        def _(dve):
            own = Steps(dve, dve_own)
            dve.tensor_copy(kq[:, :, 0].rearrange("p (h b) -> p h b", b=B), cols(v.k))
            dve.tensor_copy(kq[:, :, 1].rearrange("p (h b) -> p h b", b=B), cols(v.q)).then_inc(packed, 1)
            dve.tensor_tensor(by_head(qk[:, :]), cols(v.k), cols(v.q), ALU.mult).then_inc(packed, 1)
            dve.wait_ge(act_done, 1)
            dve.wait_ge(spread, 2)
            dve.wait_ge(applied, 1)
            ks, qs = [ps[:, 4, 0:2 * pairs].rearrange("p (i w) -> p i w", w=2)[:, :, w] for w in range(2)]
            own.did(dve.tensor_tensor(t1[:, :], ks, eg[:, :], ALU.mult))
            own.did(dve.tensor_tensor(t2[:, :], qs, eg[:, :], ALU.mult))
            own.settle()
            own.did(dve.tensor_tensor(by_head(t1[:, :]), cols(v.v), by_head(t1[:, :]), ALU.subtract))
            own.settle()
            dve.tensor_tensor(u[:, :], t1[:, :], beta[:, :], ALU.mult).then_inc(solved, 1)
            dve.wait_ge(solved, 1)
            own.did(dve.tensor_tensor(dot[:, :], u[:, :], ps[:, 2, 0:pairs], ALU.mult))
            own.settle()
            own.did(dve.tensor_tensor(cols(v.y), by_head(dot[:, :]), by_head(t2[:, :]), ALU.add))
            dve.wait_ge(turned_copied, 2)

            def spread_rows(k):
                if k >= 2:
                    dve.wait_ge(outer, k - 1)
                at = g.ident[0:pairs, k * SQ:(k + 1) * SQ].rearrange("p (i o) -> p i o", o=1).to_broadcast([pairs, SQ, P])
                rows = u_t[:, :].rearrange("p (o c) -> p o c", o=1).to_broadcast([pairs, SQ, P])
                dve.tensor_tensor(spread_u[:, k % 2], rows, at, ALU.mult).then_inc(masked, 1)

            spread_rows(0)
            for k in range(4):
                if k < 3:
                    spread_rows(k + 1)
                part = state[:, k * SQ:(k + 1) * SQ, :]
                own.did(dve.tensor_tensor(part, part, eg[:, k * SQ:(k + 1) * SQ].rearrange("p (i o) -> p i o", o=1)
                                          .to_broadcast([P, SQ, P]), ALU.mult))
                own.settle()
                dve.wait_ge(outer, k + 1)
                dve.tensor_tensor(part, part, ps[:, 0:4, :].rearrange("p a (b c) -> p (a b) c", c=P),
                                  ALU.add).then_inc(updated, 1)


def gdn_out(nc, d, o, g, v):
    with ExitStack() as ctx:
        sc = Scope(nc, ctx, "gdno")
        ps = sc.ps("ps", [P, 8, 512])
        proj = OutProjection(sc, ps)
        sq = sc.sb("sq", [P, 2, N])
        rs = sc.sb("rs", [P, 2, N])
        squared = sc.sem("squared")
        summed = sc.sem("summed")
        rooted = sc.sem("rooted")
        scaled = sc.sem("scaled")
        dve_own = sc.sem("dve_own")
        block = ctx.enter_context(nc.Block())

        @block.sync
        def _(sp):
            proj.load(sp, d["gdn_w_out"])

        @block.tensor
        def _(pe):
            for h in range(GH):
                pe.wait_ge(squared, h + 1)
                if h >= 2:
                    pe.wait_ge(rooted, h - 1)
                for u in range(2):
                    mm = pe.matmul(ps[:, 2 * (h % 2) + u, 0:H], g.ones, sq[:, h % 2, u * H:(u + 1) * H], start=True, stop=True)
                mm.then_inc(summed, 1)
            pe.wait_ge(scaled, GH)
            proj.pe(pe, v.y)

        @block.scalar
        def _(act):
            for h in range(GH + 1):
                if h < GH:
                    if h >= 2:
                        act.wait_ge(summed, h - 1)
                    act.activation(sq[:, h % 2, :], v.y[:, h, :], ACT.Square).then_inc(squared, 1)
                if h >= 1:
                    s = (h - 1) % 2
                    act.wait_ge(summed, h)
                    if h >= 3:
                        act.wait_ge(scaled, h - 2)
                    act.activation(rs[:, s, :].rearrange("p (h n) -> p h n", h=2), ps[:, 2 * s:2 * s + 2, 0:H], ACT.Sqrt,
                                   bias=g.eps[:, 0:1], scale=1.0 / P).then_inc(rooted, 1)

        @block.vector
        def _(dve):
            own = Steps(dve, dve_own)
            for h in range(GH):
                dve.wait_ge(rooted, h + 1)
                own.did(dve.reciprocal(rs[:, h % 2, :], rs[:, h % 2, :]))
                own.settle()
                own.did(dve.scalar_tensor_tensor(v.y[:, h, :], v.y[:, h, :], v.norm_g[:, 0:1], rs[:, h % 2, :],
                                                 ALU.mult, ALU.mult))
                own.settle()
                dve.tensor_tensor(v.y[:, h, :], v.y[:, h, :], v.gate[:, h, :], ALU.mult).then_inc(scaled, 1)
            proj.dve(dve, g.xt)


def gdn_stage(nc, d, o, g):
    with ExitStack() as ctx:
        sc = Scope(nc, ctx, "gdn")
        v = Shared()
        v.q, v.k, v.v, v.gate = [sc.sb(n, [P, GH, N]) for n in ("q", "k", "v", "gate")]
        v.rows = sc.sb("rows", [P, N])
        v.cum_tok = sc.sb("cum_tok", [P, NCH, GH])
        v.spread = sc.sb("spread", [P, 2 * GH, P])
        v.norm_g = sc.sb("head_norm_g", [P, 1])
        v.y = g.xn
        gdn_project(nc, d, o, g, v)
        gdn_chunks(nc, d, o, g, v)
        gdn_samples(nc, d, o, g, v)
        gdn_out(nc, d, o, g, v)


def halves(ap):
    return ap.rearrange("p (h n) -> p h n", h=2)


def column(gr):
    return 8 * (gr % 2) + 4 * (gr // 2)


def nsa_project(nc, d, o, g, v, layer, j):
    with ExitStack() as ctx:
        sc = Scope(nc, ctx, f"nsap{j}")
        w_in = sc.sb("w_in", [P, 2, 2, KT, P])
        w_v = sc.sb("w_v", [P, KT, 560])
        rope = sc.sb("rope", [P, 2, N])
        turned = sc.sb("rope_part", [P, N])
        ps = sc.ps("ps", [P, 8, 512])
        norm = Norm(sc, g.norm_g[:, layer, :], ps)
        small_in = sc.sem("small_in")
        w_v_in = sc.sem("w_v_in")
        w_in_in = [sc.sem(f"w_in_in{s}") for s in range(2)]
        zeroed = sc.sem("zeroed")
        projected = sc.sem("projected")
        copied = sc.sem("copied")
        swapped = sc.sem("swapped")
        added = sc.sem("added")
        rotated = sc.sem("rotated")
        kn_done = sc.sem("kn_done")
        dve_own = sc.sem("dve_own")
        stored = sc.sem("stored")
        block = ctx.enter_context(nc.Block())
        rotate = list(range(8)) + list(range(12, 16))

        @block.sync
        def _(sp):
            for s in range(2):
                sp.dma_start(w_in[:, s], d["nsa_w_in"][j, s]).then_inc(w_in_in[s], 16)
            sp.dma_start(rope[:], d["rope"]).then_inc(small_in, 16)
            for k in range(2, 8):
                sp.wait_ge(projected, 2 * (k - 1))
                sp.dma_start(w_in[:, k % 2], d["nsa_w_in"][j, k]).then_inc(w_in_in[k % 2], 16)
                if k == 2:
                    sp.dma_start(w_v[:], d["nsa_w_v"][j]).then_inc(w_v_in, 16)
            sp.wait_ge(rotated, len(rotate))
            sp.wait_ge(copied, 21)
            sp.dma_start(o["nsa_kv"][j], v.kv[:]).then_inc(stored, 16)
            sp.dma_start(o["nsa_v"][j], v.vt[:]).then_inc(stored, 16)
            sp.dma_start(o["nsa_v_new"][j], v.vn[0:B, :]).then_inc(stored, 16)
            sp.wait_ge(stored, 48)

        def raw(i):
            return v.qu[:, i, :] if i < 8 else v.kv[:, i - 8, :]

        @block.tensor
        def _(pe):
            norm.pe(pe, g.ones)
            pe.wait_ge(norm.normed, KT)

            def swap(r):
                i = rotate[r]
                pe.wait_ge(copied, i + 1)
                if r:
                    pe.wait_ge(added, r)
                for h in range(2):
                    mm = pe.matmul(ps[:, 6 + h, 0:H], g.rope_swap, raw(i)[:, h * H:(h + 1) * H], start=True, stop=True)
                mm.then_inc(swapped, 1)

            for i in range(16):
                if i % 2 == 0:
                    pe.wait_ge(w_in_in[i // 2 % 2], 16 * (i // 4 + 1))
                if i >= 3:
                    pe.wait_ge(copied, i - 2)
                for kt in range(KT):
                    for h in range(2):
                        mm = pe.matmul(ps[:, 2 * (i % 3) + h, 0:H], w_in[:, i // 2 % 2, i % 2, kt, :],
                                       g.xn[:, kt, h * H:(h + 1) * H], start=(kt == 0), stop=(kt == KT - 1))
                mm.then_inc(projected, 1)
                if i - 1 in rotate:
                    swap(rotate.index(i - 1))
            pe.wait_ge(w_v_in, 16)
            for tt in range(5):
                i = 16 + tt
                m = min(P, N - tt * P)
                pe.wait_ge(copied, i - 2)
                for kt in range(KT):
                    x = g.xn[:, kt, tt * P:tt * P + m]
                    pe.matmul(ps[0:m, 2 * (i % 3), :], x, w_v[:, kt, 0:512], start=(kt == 0), stop=(kt == KT - 1))
                    mm = pe.matmul(ps[0:m, 2 * (i % 3) + 1, 0:48], x, w_v[:, kt, 512:560], start=(kt == 0),
                                   stop=(kt == KT - 1))
                mm.then_inc(projected, 1)
                if tt == 0:
                    swap(len(rotate) - 1)

        @block.scalar
        def _(act):
            norm.act(act, g.xt, g.eps)
            act.wait_ge(zeroed, 1)
            for i in range(16):
                act.wait_ge(projected, i + 1)
                act.activation(halves(raw(i)), ps[:, 2 * (i % 3):2 * (i % 3) + 2, 0:H], ACT.Copy,
                               scale=0.125 if i < 8 else 1.0).then_inc(copied, 1)
            for tt in range(5):
                i = 16 + tt
                m = min(P, N - tt * P)
                act.wait_ge(projected, i + 1)
                act.activation(v.vt[:, tt, :] if tt < 4 else v.vn[0:B, :], ps[0:m, 2 * (i % 3), :], ACT.Copy)
                act.activation(v.gate[:, tt, :] if tt < 4 else v.gate_new[0:B, :], ps[0:m, 2 * (i % 3) + 1, 0:48],
                               ACT.Sigmoid).then_inc(copied, 1)

        @block.vector
        def _(dve):
            own = Steps(dve, dve_own)
            dve.memset(v.vn[:, :], 0.0)
            dve.memset(v.kn[:, :, :], 0.0).then_inc(zeroed, 1)
            norm.dve(dve, g.xt, g.xn)
            dve.wait_ge(small_in, 16)
            dve.wait_ge(zeroed, 1)
            for r, i in enumerate(rotate):
                dve.wait_ge(swapped, r + 1)
                out = v.qr[:, i, :] if i < 8 else raw(i)
                dve.tensor_tensor(halves(turned[:, :]), ps[:, 6:8, 0:H], halves(rope[:, 1, :]), ALU.mult).then_inc(added, 1)
                own.did(dve.tensor_tensor(out, raw(i), rope[:, 0, :], ALU.mult))
                own.settle()
                dve.wait_ge(added, r + 1)
                dve.tensor_tensor(out, out, turned[:, :], ALU.add).then_inc(rotated, 1)
                dve.wait_ge(rotated, r + 1)
                if i >= 12:
                    dve.tensor_copy(v.kn[:, i - 12, 0:B], raw(i)[:, T:N])


def nsa_compress(nc, d, o, g, v, j):
    with ExitStack() as ctx:
        sc = Scope(nc, ctx, f"nsac{j}")
        w = sc.sb("w", [P, 2, 32, P])
        pe_in = sc.sb("pe", [P, 2, 32])
        table = sc.sb("table", [1, B * PAGES], I32)
        pages = sc.sb("pages", [P, 69, 256])
        slots = (pages[:, 0:37], pages[:, 37:69])
        free = g.xn[:].rearrange("p t n -> p (t n)")
        bias = sc.sb("bias", [P, 4])
        cmp_s = v.drop[:].rearrange("p t n -> p (t n)").rearrange("p (k n) -> p k n", k=4)
        v_tok = free[0:NCMP, KT * N - B * 2 * P:].rearrange("p (b t n) -> p b t n", b=B, t=2)    
        halves_of = free[0:16, 0:PAGES * 2 * 64].rearrange("p (t h n) -> p t h n", t=PAGES, h=2)
        drop_t, prob_t, st = [free[0:r, at * P:(at + 1) * P] for r, at in ((16, 8), (NCMP, 9), (NCMP, 10))]
        prob = sc.sb("prob", [P, NCMP])
        nmax, total, least, last_eq = [sc.sb(n, [P, 1]) for n in ("neg_max", "total", "least", "last_equal")]
        imp, equal, drop = [free[:, at:at + 16] for at in (11 * P, 11 * P + 16, 11 * P + 32)]
        ps = sc.ps("ps", [P, 8, 512])
        w_loaded = sc.sem("w_loaded")
        table_in = sc.sem("table_in")
        pages_in = [[sc.sem(f"pages_in{s}_{w}") for w in ("sp", "pool", "act")] for s in range(2)]
        permuted = sc.sem("permuted")
        bias_done = sc.sem("bias_done")
        unit_done = sc.sem("unit_done")
        unit_copied = sc.sem("unit_copied")
        pe_step = sc.sem("pe_step")
        act_step = sc.sem("act_step")
        dve_own = sc.sem("dve_own")
        normed = sc.sem("normed")
        dropped = sc.sem("dropped")
        expanded = sc.sem("expanded")
        c_exped = sc.sem("c_exped")
        block = ctx.enter_context(nc.Block())

        def page_loads(eng, which, u):
            lo, hi = ((0, 16), (16, 24), (24, 32))[which]
            if u >= 2:
                eng.wait_ge(unit_done, u - 1)
            kv, quad = u // 2, u % 2
            slot = slots[u % 2]
            with eng.Fori(lo // 4, hi // 4) as i:
                for k in range(4):
                    page = eng.value_load(table[0:1, bass.ds(i * 4 + (quad * 32 + k), 1)], min_val=0, max_val=N_PHYS - 1)
                    eng.dma_start(flat(slot[:, bass.ds(i * 4 + k, 1), :]),
                                  flat(d["cmp_pages"][j, bass.ds(page, 1), :, kv * 256:(kv + 1) * 256]
                                       .rearrange("o p n -> p o n"))).then_inc(pages_in[u % 2][which], 16)

        @block.sync
        def _(sp):
            sp.dma_start(table[:], d["page_table"]).then_inc(table_in, 16)
            sp.dma_start(pe_in[:], d["nsa_pe"][j]).then_inc(w_loaded, 16)
            sp.dma_start(w[:], d["nsa_w_cmp"][j]).then_inc(w_loaded, 16)
            sp.wait_ge(table_in, 16)
            for u in range(4):
                page_loads(sp, 0, u)

        @block.gpsimd
        def _(pool):
            pool.wait_ge(table_in, 16)
            for u in range(4):
                page_loads(pool, 1, u)

        @block.tensor
        def _(pe):
            pe.wait_ge(w_loaded, 32)
            for u in range(4):
                kv = u // 2
                for which, n in enumerate((16, 8, 8)):
                    pe.wait_ge(pages_in[u % 2][which], 16 * n * (u // 2 + 1))
                if u >= 2:
                    pe.wait_ge(unit_copied, u - 1)
                if u % 2 == 0:
                    pe.wait_ge(permuted, u // 2 + 1)
                cols = slots[u % 2].shape[1] * 4
                for gp in range(2):
                    for l in range(32):
                        at = gp * 128 + l * 4
                        rhs = slots[u % 2][:, :, at:at + 4]
                        mm = pe.matmul(ps[:, 1 + u % 2, gp * 256:gp * 256 + cols], w[:, kv, l, :], rhs,
                                       start=(l == 0), stop=(l == 31))
                mm.then_inc(unit_done, 1)
            pe.wait_ge(unit_copied, 4)
            for gp in range(2):
                pe.transpose(ps[0:PCMP, 3, gp * P:(gp + 1) * P], v.cmp_p[:, 2 + gp, :], g.ident)
            for b in range(B):
                for gp in range(2):
                    mm = pe.transpose(ps[0:NCMP, 4 + b // 2, (b % 2 * 2 + gp) * P:(b % 2 * 2 + gp + 1) * P],
                                      cmp_s[:, 2 + gp, b * NCMP:(b + 1) * NCMP], g.ident)
            mm.then_inc(pe_step, 1)
            for b in range(B):
                for gr in range(4):
                    gp, lo = gr // 2, 64 * (gr % 2)
                    at = b * 8 + 4 * gp
                    mm = pe.matmul(ps[0:NCMP, 2 * (gr % 2), at:at + 4],
                                   cmp_s[lo:lo + 64, gp, b * NCMP:(b + 1) * NCMP],
                                   v.qu[lo:lo + 64, 4 * gp:4 * gp + 4, T + b], start=True, stop=True)
            mm.then_inc(pe_step, 1)
            pe.wait_ge(act_step, 2)
            pe.transpose(ps[:, 1, 0:NCMP], st[:, :], g.ident[0:NCMP, 0:NCMP]).then_inc(pe_step, 1)
            pe.wait_ge(normed, 1)
            pe.transpose(ps[0:NCMP, 2, 0:P], prob[:, :], g.ident).then_inc(pe_step, 1)
            pe.matmul(ps[:, 0, 0:NCMP], g.four_sum, prob[:, :], start=True, stop=True).then_inc(pe_step, 1)
            pe.wait_ge(act_step, 3)
            for b in range(B):
                for gr in range(4):
                    gp, lo = gr // 2, 64 * (gr % 2)
                    mm = pe.matmul(ps[lo:lo + 64, 3, b * 8 + 4 * gp:b * 8 + 4 * gp + 4],
                                   v_tok[:, b, gp, lo:lo + 64],
                                   prob_t[:, b * 16 + column(gr):b * 16 + column(gr) + 4],
                                   start=True, stop=True)
            mm.then_inc(pe_step, 1)
            pe.wait_ge(dropped, 1)
            pe.transpose(ps[0:16, 1, 0:P], drop[:, :], g.ident).then_inc(pe_step, 1)
            pe.wait_ge(act_step, 5)
            pe.wait_ge(expanded, 1)
            for t in range(PAGES):
                mm = pe.matmul(ps[:, 4 + t // 4, t % 4 * P:(t % 4 + 1) * P],
                               halves_of[:, t].rearrange("p h n -> p (h n)"), drop_t[:, :], start=True, stop=True)
            mm.then_inc(pe_step, 1)

        @block.scalar
        def _(act):
            act.wait_ge(table_in, 16)
            for u in range(2):
                page_loads(act, 2, u)
            for u in range(4):
                kv, quad = u // 2, u % 2
                act.wait_ge(unit_done, u + 1)
                if quad == 0:
                    for gp in range(2):
                        k = 2 * kv + gp
                        ins = act.activation(bias[:, k:k + 1], ps[:, 1, gp * 256 + P + PCMP:gp * 256 + P + PCMP + 1],
                                             ACT.Copy)
                    ins.then_inc(bias_done, 1)
                    act.wait_ge(bias_done, kv + 1)
                    for gp in range(2):
                        k = 2 * kv + gp
                        act.activation(v.cmp_p[:, k, :], ps[:, 1, gp * 256 + P:gp * 256 + P + PCMP], ACT.Identity,
                                       bias=bias[:, k:k + 1])
                for gp in range(2):
                    k = 2 * kv + gp
                    ins = act.activation(cmp_s[:, k, quad * P:(quad + 1) * P], ps[:, 1 + u % 2, gp * 256:gp * 256 + P],
                                         ACT.Identity, bias=bias[:, k:k + 1])
                ins.then_inc(unit_copied, 1)
                if u < 2:
                    page_loads(act, 2, u + 2)
            act.wait_ge(pe_step, 1)
            act.activation(v.cmp_v[:, :, :].rearrange("p a n -> p (a n)"), ps[0:PCMP, 3, 0:2 * P], ACT.Copy)
            act.activation(v_tok[:, :, :, :].rearrange("p (q b) g n -> p q (b g n)", q=4), ps[0:NCMP, 4:8, :],
                           ACT.Copy).then_inc(act_step, 1)
            act.wait_ge(pe_step, 2)
            act.activation(st[:, :].rearrange("p (b a h) -> p a b h", a=2, h=8),
                           ps[0:NCMP, 0:4:2, 0:64].rearrange("p a (b h) -> p a b h", h=8), ACT.Copy).then_inc(act_step, 1)
            act.wait_ge(dve_own, 1)
            act.activation(prob[:, :], ps[:, 1, 0:NCMP], ACT.Exp, bias=nmax[:, 0:1],
                           accum_out=total[:, 0:1]).then_inc(c_exped, 1)
            act.wait_ge(pe_step, 4)
            act.activation(prob_t[:, :], ps[0:NCMP, 2, 0:P], ACT.Copy).then_inc(act_step, 1)
            act.wait_ge(pe_step, 6)
            act.activation(v.out_c[:, :, :].rearrange("p b t -> p (b t)"), ps[:, 3, 0:64], ACT.Copy).then_inc(act_step, 1)
            act.wait_ge(pe_step, 7)
            act.activation(drop_t[:, :], ps[0:16, 1, 0:P], ACT.Copy).then_inc(act_step, 1)
            act.wait_ge(pe_step, 8)
            act.activation(v.drop[:, :, :].rearrange("p (a b) n -> p a (b n)", a=2), ps[:, 4:6, :], ACT.Copy)

        @block.vector
        def _(dve):
            own = Steps(dve, dve_own)
            dve.wait_ge(w_loaded, 32)
            for kv in range(2):
                if kv:
                    dve.wait_ge(unit_done, 1)
                for gp in range(2):
                    part = slice(gp * P, (gp + 1) * P)
                    dve.tensor_copy(slots[0][:, 32:36, part].rearrange("p t (l c) -> p t l c", c=4),
                                    v.kv[:, 2 * kv + gp, 0:T].rearrange("p (t c l) -> p t l c", t=4, c=4))
                    ins = dve.tensor_copy(slots[0][:, 36, part].rearrange("p (l c) -> p l c", c=4),
                                          pe_in[:, kv, :].rearrange("p (l o) -> p l o", o=1).to_broadcast([P, 32, 4]))
                ins.then_inc(permuted, 1)
            dve.tensor_copy(halves_of[:].rearrange("p t h n -> p (t h) n"),
                            g.ident[0:16, 0:16].rearrange("p (a o) -> p a o", o=1).to_broadcast([16, 16, 64])).then_inc(expanded, 1)
            dve.wait_ge(pe_step, 3)
            own.did(dve.tensor_reduce(nmax[:, 0:1], ps[:, 1, 0:NCMP], AX, ALU.max, negate=True))
            dve.wait_ge(c_exped, 1)
            own.did(dve.reciprocal(total[:, 0:1], total[:, 0:1]))
            own.settle()
            dve.tensor_scalar(prob[:, :], prob[:, :], total[:, 0:1], None, ALU.mult).then_inc(normed, 1)
            dve.wait_ge(pe_step, 5)
            own.did(dve.tensor_reduce(imp[:, :], ps[:, 0, 0:NCMP].rearrange("p (a b) -> p a b", b=2), AX, ALU.add))
            own.settle()
            own.did(dve.tensor_reduce(least[:, 0:1], imp[:, 1:16], AX, ALU.min))
            own.settle()
            own.did(dve.scalar_tensor_tensor(equal[:, 1:16], imp[:, 1:16], least[:, 0:1], g.block_no[:, 1:16],
                                             ALU.is_equal, ALU.mult))
            own.settle()
            own.did(dve.tensor_reduce(last_eq[:, 0:1], equal[:, 1:16], AX, ALU.max))
            own.settle()
            dve.tensor_scalar(drop[:, :], g.block_no, last_eq[:, 0:1], NEG, ALU.is_equal, ALU.mult).then_inc(dropped, 1)


NT = PAGES + 1 + 4 + 1


def nsa_samples(nc, d, o, g, v, j):
    with ExitStack() as ctx:
        sc = Scope(nc, ctx, f"nsas{j}")
        table = sc.sb("table", [1, B * PAGES], I32)
        pages = sc.sb("pages", [P, 3, PAGES, 512])
        win = sc.sb("win", [P, 3, 2048])
        s = sc.sb("scores", [P, 2, NT, 16])
        pmax = sc.sb("pmax", [P, 2, 2, 16])
        m32 = sc.sb("m32", [32, 2])
        diag = sc.sb("diag", [32, 2, 32])
        psum_p = sc.sb("part_sums", [P, 2, 2, 16])
        inv = sc.sb("inv", [P, B, 3, 16])
        out = sc.sb("out", [P, B, 3, 8])
        rows = sc.sb("rows", [B, B, P])
        acc = sc.sb("acc", [P, 3, B, 8])
        q_pair = sc.sb("q_pair", [P, B, 2, 2, 4])
        ps = sc.ps("ps", [P, 8, 512])
        table_in = sc.sem("table_in")
        kv_in = [sc.sem(f"kv_in{x}") for x in range(3)]
        win_stored = [sc.sem(f"win_stored{x}") for x in range(3)]
        rows_done = sc.sem("rows_done")
        paired = sc.sem("paired")
        gates_done = sc.sem("gates_done")
        gates_copied = sc.sem("gates_copied")
        scored = sc.sem("scored")
        part_max = sc.sem("part_max")
        turned = sc.sem("turned")
        diagonal = sc.sem("diagonal")
        max_spread = sc.sem("max_spread")
        shifted = sc.sem("shifted")
        exped = sc.sem("exped")
        summed = sc.sem("summed")
        sum_spread = sc.sem("sum_spread")
        inverted = sc.sem("inverted")
        valued = sc.sem("valued")
        out_copied = sc.sem("out_copied")
        dve_own = sc.sem("dve_own")
        block = ctx.enter_context(nc.Block())

        @block.sync
        def _(sp):
            sp.dma_start(table[:], d["page_table"]).then_inc(table_in, 16)
            sp.wait_ge(table_in, 16)
            for b in range(B):
                x = b % 3
                if b >= 3:
                    sp.wait_ge(valued, b - 2)
                    sp.wait_ge(win_stored[x], 16 * (b // 3))
                with sp.Fori(0, PAGES // 4) as i:
                    for k in range(4):
                        page = sp.value_load(table[0:1, bass.ds(i * 4 + (b * PAGES + k), 1)], min_val=0, max_val=N_PHYS - 1)
                        sp.dma_start(flat(pages[:, x, bass.ds(i * 4 + k, 1), :]),
                                     flat(d["sel_pages"][j, bass.ds(page, 1)].rearrange("o p n -> p o n"))).then_inc(kv_in[x], 16)
                sp.dma_start(win[:, x], d["win_state"][j, b]).then_inc(kv_in[x], 16)

        @block.gpsimd
        def _(pool):
            for b in range(B):
                pool.wait_ge(kv_in[b % 3], 144 * (b // 3 + 1))
                pool.dma_start(o["win_kept"][j, b], win[:, b % 3]).then_inc(win_stored[b % 3], 16)
            for x in range(3):
                pool.wait_ge(win_stored[x], 16 * len(range(x, B, 3)))

        @block.tensor
        def _(pe):
            pe.wait_ge(rows_done, 1)
            for b in range(B):
                mm = pe.matmul(ps[:, 7, b * 48:b * 48 + 48], rows[:, b, :], v.gate_new[0:B, :], start=True, stop=True)
            mm.then_inc(gates_done, 1)

            def scores(b):
                x, y = b % 2, b % 3
                pe.wait_ge(kv_in[y], 144 * (b // 3 + 1))
                if b >= 2:
                    pe.wait_ge(part_max, b - 1)
                for t in range(NT):
                    for gp in range(2):
                        if t < PAGES:
                            keys = pages[:, y, t, gp * P:(gp + 1) * P]
                        elif t == PAGES:
                            keys = v.kn[:, gp, :]
                        elif t < NT - 1:
                            at = gp * 512 + (t - PAGES - 1) * P
                            keys = win[:, y, at:at + P]
                        else:
                            keys = v.kn[:, 2 + gp, :]
                        out_cols = ps[:, x, 16 * t:16 * t + 16].rearrange("p (a g h) -> p a g h", a=2, g=2)[:, :, gp]
                        mm = pe.matmul(out_cols, keys, q_pair[:, b, gp], start=True, stop=True)
                mm.then_inc(scored, 1)

            def values(b):
                x, y = b % 2, b % 3
                for br, tiles in ((1, range(0, PAGES + 1)), (2, range(PAGES + 1, NT))):
                    for gr in range(4):
                        gp, lo = gr // 2, 64 * (gr % 2)
                        for t in tiles:
                            if t < PAGES:
                                val = pages[:, y, t, 256 + 64 * gr:320 + 64 * gr]
                            elif t == PAGES:
                                val = v.vn[:, 64 * gr:64 * gr + 64]
                            elif t < NT - 1:
                                at = 1024 + (t - PAGES - 1) * 256 + 64 * gr
                                val = win[:, y, at:at + 64]
                            else:
                                val = v.vn[:, 256 + 64 * gr:320 + 64 * gr]
                            at = 8 * (br - 1) + 4 * gp
                            mm = pe.matmul(ps[lo:lo + 64, 7, at:at + 4], val, s[:, x, t, column(gr):column(gr) + 4],
                                           start=(t == tiles[0]), stop=(t == tiles[-1]))
                mm.then_inc(valued, 1)

            pe.wait_ge(paired, 1)
            scores(0)
            for b in range(B):
                x = b % 2
                pe.wait_ge(part_max, b + 1)
                if b:
                    pe.wait_ge(diagonal, b)
                pe.transpose(ps[0:32, 4, 0:P], pmax[:, x].rearrange("p a h -> p (a h)"), g.ident).then_inc(turned, 1)
                if b < B - 1:
                    scores(b + 1)
                pe.wait_ge(diagonal, b + 1)
                if b:
                    pe.wait_ge(shifted, b)
                pe.matmul(ps[:, 5, 0:32], g.ones[0:32, :], diag[:, x, :], start=True, stop=True).then_inc(max_spread, 1)
                pe.wait_ge(summed, b + 1)
                if b:
                    pe.wait_ge(inverted, b)
                pe.matmul(ps[:, 6, 0:32], g.ones, psum_p[:, x].rearrange("p a h -> p (a h)"), start=True,
                          stop=True).then_inc(sum_spread, 1)
                if b:
                    pe.wait_ge(out_copied, b)
                else:
                    pe.wait_ge(gates_copied, 1)
                values(b)

        @block.scalar
        def _(act):
            act.wait_ge(gates_done, 1)
            act.activation(inv[:].rearrange("p b r h -> p (b r h)"), ps[:, 7, 0:B * 48], ACT.Copy).then_inc(gates_copied, 1)
            for b in range(B):
                x = b % 2
                act.wait_ge(shifted, b + 1)
                act.activation(s[:, x], s[:, x], ACT.Exp).then_inc(exped, 1)
                act.wait_ge(valued, b + 1)
                act.activation(out[:, b, 1:3, :], ps[:, 7, 0:16].rearrange("p (r t) -> p r t", r=2),
                               ACT.Copy).then_inc(out_copied, 1)

        @block.vector
        def _(dve):
            own = Steps(dve, dve_own)
            dve.tensor_copy(rows[:], g.ident[0:B, 0:B].rearrange("p (a o) -> p a o", o=1).to_broadcast([B, B, P])).then_inc(rows_done, 1)
            dve.tensor_copy(out[:, :, 0, :], v.out_c[:, :, :])
            own.did(dve.memset(q_pair[:].rearrange("p b g a h -> p (b g a h)"), 0.0))
            own.settle()
            for g2 in range(2):
                half = slice(64 * g2, 64 * g2 + 64)
                for gp in range(2):
                    ins = dve.tensor_copy(q_pair[half, :, gp, g2, :],
                                          v.qr[half, 4 * gp:4 * gp + 4, T:N].rearrange("p h b -> p b h"))
            ins.then_inc(paired, 1)
            parts = (slice(0, PAGES + 1), slice(PAGES + 1, NT))

            def by_key(ap):
                return ap.rearrange("p t h -> p h t")

            def first(b):
                x = b % 2
                dve.wait_ge(scored, b + 1)
                if b >= 2:
                    dve.wait_ge(valued, b - 1)
                src = ps[:, x, 0:16 * NT].rearrange("p (t h) -> p t h", h=16)
                drop = v.drop[:, :, b * 16:b * 16 + 16]
                own.did(dve.tensor_tensor(s[:, x, 0:PAGES], src[:, 0:PAGES], drop, ALU.add))
                for t in (PAGES, NT - 1):
                    own.did(dve.tensor_scalar(s[:, x, t], src[:, t], g.new_mask[:, b:b + 1], None, ALU.add))
                own.did(dve.tensor_copy(s[:, x, PAGES + 1:NT - 1], src[:, PAGES + 1:NT - 1]))
                own.settle()
                for k, part in enumerate(parts):
                    ins = dve.tensor_reduce(pmax[:, x, k, :], by_key(s[:, x, part]), AX, ALU.max)
                ins.then_inc(part_max, 1)

            first(0)
            for b in range(B):
                x = b % 2
                dve.wait_ge(turned, b + 1)
                own.did(dve.tensor_reduce(m32[:, x:x + 1], ps[0:32, 4, 0:P], AX, ALU.max))
                own.settle()
                dve.tensor_scalar(diag[:, x, :], g.ident[0:32, 0:32], m32[:, x:x + 1], None, ALU.mult).then_inc(diagonal, 1)
                if b < B - 1:
                    first(b + 1)
                dve.wait_ge(max_spread, b + 1)
                for k, part in enumerate(parts):
                    n = part.stop - part.start
                    m = ps[:, 5, 16 * k:16 * k + 16].rearrange("p (o h) -> p o h", o=1).to_broadcast([P, n, 16])
                    ins = dve.tensor_tensor(s[:, x, part], s[:, x, part], m, ALU.subtract)
                ins.then_inc(shifted, 1)
                dve.wait_ge(exped, b + 1)
                for k, part in enumerate(parts):
                    ins = dve.tensor_reduce(psum_p[:, x, k, :], by_key(s[:, x, part]), AX, ALU.add)
                ins.then_inc(summed, 1)
                dve.wait_ge(sum_spread, b + 1)
                dve.reciprocal(pmax[:, x].rearrange("p a h -> p (a h)"), ps[:, 6, 0:32]).then_inc(inverted, 1)
                dve.wait_ge(inverted, b + 1)
                dve.wait_ge(gates_copied, 1)
                own.did(dve.tensor_tensor(inv[:, b, 1:3, :], inv[:, b, 1:3, :], pmax[:, x], ALU.mult))
            dve.wait_ge(out_copied, B)
            own.settle()
            for br in range(3):
                for gr in range(4):
                    gp, lo = gr // 2, 64 * (gr % 2)
                    half = slice(lo, lo + 64)
                    own.did(dve.tensor_tensor(acc[half, br, :, 4 * gp:4 * gp + 4], out[half, :, br, 4 * gp:4 * gp + 4],
                                              inv[half, :, br, column(gr):column(gr) + 4], ALU.mult))
            own.settle()
            own.did(dve.tensor_tensor(acc[:, 0], acc[:, 0], acc[:, 1], ALU.add))
            own.settle()
            dve.tensor_tensor(v.y[:, :, T:N].rearrange("p t b -> p b t"), acc[:, 0], acc[:, 2], ALU.add)


def nsa_prompt(nc, d, o, g, v, j):
    units = [(i, hh) for i in range(NCH) for hh in range(HEADS)]
    with ExitStack() as ctx:
        sc = Scope(nc, ctx, f"nsaq{j}")
        ident16 = sc.sb("ident16", [P, P], BF16)
        causal16 = sc.sb("causal16", [P, P], BF16)
        prob = sc.sb("prob", [P, 4, 512])
        prob_t = sc.sb("prob_t", [P, 4, 512])
        nmax = sc.sb("neg_max", [P, 4])
        total = sc.sb("total", [P, 4])
        factor = sc.sb("factor", [P, 2, 2])
        pc = sc.sb("prob_c", [P, HEADS, PCMP])
        pct = sc.sb("prob_c_t", [PCMP, 4, 512])
        stat = sc.sb("stat", [P, 2, HEADS])
        acc = sc.sb("acc", [P, 2, HEADS, 64])
        ps = sc.ps("ps", [P, 8, 512])
        proj = OutProjection(sc, ps)
        masks = sc.sem("masks")
        scored = sc.sem("scored")
        maxed = sc.sem("maxed")
        exped = sc.sem("exped")
        turned = sc.sem("turned")
        copied_t = sc.sem("copied_t")
        copied_w = sc.sem("copied_w")
        valued = sc.sem("valued")
        merged = sc.sem("merged")
        c_scored = sc.sem("c_scored")
        c_shifted = sc.sem("c_shifted")
        c_exped = sc.sem("c_exped")
        c_scaled = sc.sem("c_scaled")
        c_turned = sc.sem("c_turned")
        c_copied = sc.sem("c_copied")
        c_valued = sc.sem("c_valued")
        c_out = sc.sem("c_out")
        back = sc.sem("back")
        back_copied = sc.sem("back_copied")
        dve_own = sc.sem("dve_own")
        block = ctx.enter_context(nc.Block())

        def where(hh):
            t, g2 = hh // 2, hh % 2
            return t, slice(64 * g2, 64 * g2 + 64), t // 4, 2 * (t // 4) + g2

        @block.sync
        def _(sp):
            proj.load(sp, d["nsa_w_out"][j])

        @block.tensor
        def _(pe):
            pe.wait_ge(masks, 2)

            def compressed_scores(i):
                if i:
                    pe.wait_ge(back_copied, i)
                for hh in range(HEADS):
                    t, half, gp, _ = where(hh)
                    mm = pe.matmul(ps[:, 6 + hh % 2, t * PCMP:(t + 1) * PCMP], v.qu[half, t, i * P:(i + 1) * P],
                                   v.cmp_p[half, gp, :], start=True, stop=True)
                mm.then_inc(c_scored, 1)

            def compressed_values(i):
                pe.wait_ge(c_scaled, i + 1)
                for q in range(4):
                    if q == 0:
                        pe.wait_ge(exped, 2 * HEADS * i)
                        pe.wait_ge(maxed, 2 * HEADS * i)
                    for k in range(4):
                        mm = pe.transpose(ps[0:PCMP, q, k * P:(k + 1) * P], pc[:, 4 * q + k, :], g.ident)
                mm.then_inc(c_turned, 1)
                pe.wait_ge(c_copied, i + 1)
                for hh in range(HEADS):
                    _, _, gp, gr = where(hh)
                    hc = 8 * (hh % 2) + hh // 2
                    mm = pe.matmul(ps[:, 6 + hh // 8, hh % 8 * 64:hh % 8 * 64 + 64], pct[:, hc // 4, hc % 4 * P:(hc % 4 + 1) * P],
                                   v.cmp_v[:, gp, hh % 2 * 64:hh % 2 * 64 + 64], start=True, stop=True)
                mm.then_inc(c_valued, 1)

            def scores(n):
                i, hh = units[n]
                t, half, gp, _ = where(hh)
                for br in range(2):
                    k = 2 * n + br
                    if k >= 3:
                        pe.wait_ge(exped, k - 2)
                    bank = k % 3
                    pe.matmul(ps[:, bank, 0:(i + 1) * P], v.qr[half, t, i * P:(i + 1) * P],
                              v.kv[half, 4 + 2 * br + gp, 0:(i + 1) * P], start=True, stop=False)
                    pe.matmul(ps[:, bank, i * P:(i + 1) * P], ident16[:, :], causal16[:, :], start=False,
                              stop=True).then_inc(scored, 1)

            def turn(n):
                i, hh = units[n]
                for br in range(2):
                    k = 2 * n + br
                    pe.wait_ge(exped, k + 1)
                    if k >= 3:
                        prev = k - 3
                        pe.wait_ge(copied_t if prev % 2 == 0 else copied_w, prev // 2 + 1)
                    for kt in range(i + 1):
                        mm = pe.transpose(ps[:, 3 + k % 3, kt * P:(kt + 1) * P], prob[:, k % 4, kt * P:(kt + 1) * P], g.ident)
                    mm.then_inc(turned, 1)

            def values(n):
                i, hh = units[n]
                _, _, _, gr = where(hh)
                if n >= 2:
                    pe.wait_ge(merged, n - 1)
                for br in range(2):
                    k = 2 * n + br
                    pe.wait_ge(copied_t if br == 0 else copied_w, n + 1)
                    for kt in range(i + 1):
                        at = 256 * br + 64 * gr
                        mm = pe.matmul(ps[:, 6 + n % 2, br * 64:br * 64 + 64], prob_t[:, k % 4, kt * P:(kt + 1) * P],
                                       v.vt[:, kt, at:at + 64], start=(kt == 0), stop=(kt == i))
                mm.then_inc(valued, 1)

            for i in range(NCH):
                first, last = i * HEADS, (i + 1) * HEADS
                compressed_scores(i)
                compressed_values(i)
                pe.wait_ge(c_out, i + 1)
                for n in range(first, last + 2):
                    if n < last:
                        scores(n)
                    if first <= n - 1 < last:
                        turn(n - 1)
                    if first <= n - 2 < last:
                        values(n - 2)
                pe.wait_ge(merged, last)
                for t in range(KT):
                    mm = pe.transpose(ps[:, 6 + t // 4, t % 4 * P:(t % 4 + 1) * P],
                                      acc[:, i % 2, 2 * t:2 * t + 2, :].rearrange("p a n -> p (a n)"), g.ident)
                mm.then_inc(back, 1)
            pe.wait_ge(back_copied, NCH)
            pe.wait_ge(exped, 2 * len(units))
            proj.pe(pe, v.y)

        @block.scalar
        def _(act):
            act.activation(ident16[:, :], g.ident, ACT.Copy).then_inc(masks, 1)
            act.activation(causal16[:, :], g.causal, ACT.Copy).then_inc(masks, 1)
            for i in range(NCH):
                act.wait_ge(c_shifted, i + 1)
                act.activation(pc[:, :, :], pc[:, :, :], ACT.Exp).then_inc(c_exped, 1)
                act.wait_ge(c_turned, i + 1)
                act.activation(pct[:, :, :], ps[0:PCMP, 0:4, :], ACT.Copy).then_inc(c_copied, 1)
                act.wait_ge(c_valued, i + 1)
                if i >= 2:
                    act.wait_ge(back, i - 1)
                act.activation(acc[:, i % 2].rearrange("p (a h) n -> p a (h n)", a=2), ps[:, 6:8, :], ACT.Copy).then_inc(c_out, 1)
                first, last = i * HEADS, (i + 1) * HEADS
                for n in range(first, last + 1):
                    if n < last:
                        for br in range(2):
                            k = 2 * n + br
                            act.wait_ge(maxed, k + 1)
                            if k >= 4:
                                act.wait_ge(turned, k - 3)
                            act.activation(prob[:, k % 4, 0:(i + 1) * P], ps[:, k % 3, 0:(i + 1) * P], ACT.Exp,
                                           bias=nmax[:, k % 4:k % 4 + 1],
                                           accum_out=total[:, k % 4:k % 4 + 1]).then_inc(exped, 1)
                    if n > first:
                        m = n - 1
                        act.wait_ge(turned, 2 * m + 1)
                        if m >= 2:
                            act.wait_ge(valued, m - 1)
                        act.activation(prob_t[:, (2 * m) % 4, 0:(i + 1) * P], ps[:, 3 + (2 * m) % 3, 0:(i + 1) * P],
                                       ACT.Copy).then_inc(copied_t, 1)
                act.wait_ge(back, i + 1)
                act.activation(v.y[:, :, i * P:(i + 1) * P].rearrange("p (a b) n -> p a b n", a=2),
                               ps[:, 6:8, :].rearrange("p a (b n) -> p a b n", b=4), ACT.Copy).then_inc(back_copied, 1)

        @block.vector
        def _(dve):
            own = Steps(dve, dve_own)

            def spread16(ap, n):
                return ap.rearrange("p (h o) -> p h o", o=1).to_broadcast([P, HEADS, n])

            def compressed(i):
                dve.wait_ge(c_scored, i + 1)
                if i:
                    dve.wait_ge(c_turned, i)
                mask = g.cmp_mask[:, i * PCMP:(i + 1) * PCMP].rearrange("p (o c) -> p o c", o=1).to_broadcast([P, KT, PCMP])
                for g2 in range(2):
                    src = ps[:, 6 + g2, 0:KT * PCMP].rearrange("p (h c) -> p h c", c=PCMP)
                    own.did(dve.tensor_tensor(pc[:, 8 * g2:8 * g2 + 8, :], src, mask, ALU.add))
                own.settle()
                own.did(dve.tensor_reduce(stat[:, 0, :], pc[:, :, :], AX, ALU.max))
                own.settle()
                dve.tensor_tensor(pc[:, :, :], pc[:, :, :], spread16(stat[:, 0, :], PCMP), ALU.subtract).then_inc(c_shifted, 1)
                dve.wait_ge(c_exped, i + 1)
                own.did(dve.tensor_reduce(stat[:, 1, :], pc[:, :, :], AX, ALU.add))
                own.settle()
                own.did(dve.reciprocal(stat[:, 1, :], stat[:, 1, :]))
                own.settle()
                own.did(dve.scalar_tensor_tensor(stat[:, 1, :], stat[:, 1, :], g.cmp_any[:, i:i + 1],
                                                 v.gate[:, i, 0:16], ALU.mult, ALU.mult))
                own.settle()
                dve.tensor_tensor(pc[:, :, :], pc[:, :, :], spread16(stat[:, 1, :], PCMP), ALU.mult).then_inc(c_scaled, 1)

            def merge(n):
                i, hh = units[n]
                t, _, gp, gr = where(hh)
                f = factor[:, n % 2, :]
                dve.wait_ge(valued, n + 1)
                for br in range(2):
                    a = acc[:, i % 2, hh, :]
                    ins = dve.scalar_tensor_tensor(a, ps[:, 6 + n % 2, br * 64:br * 64 + 64], f[:, br:br + 1], a,
                                                   ALU.mult, ALU.add)
                    if br == 0:
                        own.did(ins)
                        own.settle()
                    else:
                        ins.then_inc(merged, 1)

            for i in range(NCH):
                compressed(i)
                dve.wait_ge(c_out, i + 1)
                first, last = i * HEADS, (i + 1) * HEADS
                for n in range(first, last + 2):
                    if n < last:
                        for br in range(2):
                            k = 2 * n + br
                            dve.wait_ge(scored, k + 1)
                            if k >= 4:
                                dve.wait_ge(exped, k - 3)
                            dve.tensor_reduce(nmax[:, k % 4:k % 4 + 1], ps[:, k % 3, 0:(i + 1) * P], AX, ALU.max,
                                              negate=True).then_inc(maxed, 1)
                    if first <= n - 1 < last:
                        m = n - 1
                        t, _, gp, gr = where(units[m][1])
                        dve.wait_ge(exped, 2 * m + 2)
                        if m >= 2:
                            dve.wait_ge(merged, m - 1)
                        f = factor[:, m % 2, :]
                        at = 16 + column(gr) + t % 4
                        own.did(dve.reciprocal(f, total[:, (2 * m) % 4:(2 * m) % 4 + 2]))
                        own.settle()
                        own.did(dve.tensor_tensor(f, f, v.gate[:, i, at:at + 17:16], ALU.mult))
                        dve.wait_ge(turned, 2 * m + 2)
                        if m >= 2:
                            dve.wait_ge(valued, m - 1)
                        dve.tensor_copy(prob_t[:, (2 * m + 1) % 4, 0:(i + 1) * P],
                                        ps[:, 3 + (2 * m + 1) % 3, 0:(i + 1) * P]).then_inc(copied_w, 1)
                    if first <= n - 2 < last:
                        merge(n - 2)
            proj.dve(dve, g.xt)


def nsa_stage(nc, d, o, g, layer):
    j = layer // 3
    with ExitStack() as ctx:
        sc = Scope(nc, ctx, f"nsa{j}")
        v = Shared()
        v.qu = sc.sb("q_plain", [P, KT, N])
        v.qr = sc.sb("q_rotated", [P, KT, N])
        v.kv = sc.sb("kv", [P, 8, N])
        v.vt = sc.sb("v_tokens", [P, NCH, 512])
        v.vn = sc.sb("v_new", [P, 512])
        v.kn = sc.sb("k_new", [P, 4, P])
        v.gate = sc.sb("gate", [P, NCH, 48])
        v.gate_new = sc.sb("gate_new", [B, 48])
        v.cmp_p = sc.sb("cmp_prompt", [P, 4, PCMP])
        v.cmp_v = sc.sb("cmp_values", [PCMP, 2, P])
        v.out_c = sc.sb("out_c", [P, B, 8])
        v.drop = sc.sb("drop_keys", [P, PAGES, P])
        v.y = g.xn
        nsa_project(nc, d, o, g, v, layer, j)
        nsa_compress(nc, d, o, g, v, j)
        nsa_samples(nc, d, o, g, v, j)
        nsa_prompt(nc, d, o, g, v, j)


def final_stage(nc, d, o, g):
    with ExitStack() as ctx:
        sc = Scope(nc, ctx, "final")
        ps = sc.ps("ps", [P, 2, 512])
        norm = Norm(sc, g.norm_g[:, 8, :], ps)
        stored = sc.sem("stored")
        block = ctx.enter_context(nc.Block())

        @block.tensor
        def _(pe):
            norm.pe(pe, g.ones)

        @block.scalar
        def _(act):
            norm.act(act, g.xt, g.eps)

        @block.vector
        def _(dve):
            norm.dve(dve, g.xt, g.xn)

        @block.sync
        def _(sp):
            sp.wait_ge(norm.normed, KT)
            sp.dma_start(o["y_t"], g.xn[:]).then_inc(stored, 16)
            sp.wait_ge(stored, 16)


class Shared:
    pass


def const(g, name):
    a, b = CONST_AT[name]
    return g.const[:, a:b]


OUTPUTS = {
    "y_t": (P, KT, N), "ffn_last": (4, P, FT * 2, 10), "ffn_old": (4, P, FT * 2, B),
    "nsa_kv": (2, P, 8, N), "nsa_v": (2, P, NCH, 512), "nsa_v_new": (2, B, 512), "win_kept": (2, B, P, 2048),
    "gdn_last": (P, 8, 3, 11), "gdn_old": (P, 8, 3, 2, B), "gdn_state_p": (P, 8, P), "gdn_state_s": (P, 8 * B, P),
    "lru_last": (P, KT, 11), "lru_h": (P, KT, 9), "lru_old": (P, KT, 2, B),
}


def trunk_program(nc, d, o):
    with ExitStack() as ctx:
        sc = Scope(nc, ctx, "all")
        g = Shared()
        g.xt = sc.sb("x_t", [P, KT, N])
        g.xn = sc.sb("xn_t", [P, KT, N])
        g.const = sc.sb("consts", [P, CONST_COLS])
        g.norm_g = sc.sb("norm_g", [P, 9, KT])
        g.eps = sc.sb("eps", [P, 1])
        g.bias_one = sc.sb("bias_one", [P, 1])
        g.ident, g.ones, g.neg_upper, g.strict_t, g.same16, g.pair16, g.pair32, g.pair64 = [
            const(g, n) for n in ("ident", "ones", "neg_upper", "strict_t", "same16", "pair16", "pair32", "pair64")]
        g.causal, g.rope_swap, g.four_sum, g.cmp_mask, g.cmp_any, g.new_mask, g.block_no = [
            const(g, n) for n in ("causal", "rope_swap", "four_sum", "cmp_mask", "cmp_any", "new_mask", "block_no")]
        load_stage(nc, d, g)
        for layer in range(4):
            if layer % 3 == 0:
                nsa_stage(nc, d, o, g, layer)
            elif layer % 3 == 1:
                gdn_stage(nc, d, o, g)
            else:
                lru_stage(nc, d, o, g)
            ffn_stage(nc, d, o, g, layer)
        final_stage(nc, d, o, g)


def constants():
    import numpy as np

    i = np.arange(P)
    r, c = i[:, None], i[None, :]

    def blocks(n):
        return (r // n) == (c // n)

    swap = np.zeros((P, P))
    for base in (0, 64):
        for k in range(8):
            swap[base + k + 8, base + k] = 1.0
            swap[base + k, base + k + 8] = 1.0
    q = np.arange(T).reshape(4, P)
    c_end = (np.arange(PCMP) + 1) * 32 - 1
    valid = c_end[None, None, :] <= q.T[:, :, None]
    parts = {
        "ident": np.eye(P), "ones": np.ones((P, P)),
        "neg_upper": np.where(c >= r, 0.0, NEG),
        "strict_t": (c > r) * 1.0,
        "same16": blocks(16) * 1.0, "pair16": (blocks(32) & ~blocks(16)) * 1.0,
        "pair32": (blocks(64) & ~blocks(32)) * 1.0, "pair64": (~blocks(64)) * 1.0,
        "causal": np.where(c <= r, 0.0, NEG),
        "rope_swap": swap,
        "four_sum": blocks(4) * 1.0,
        "cmp_mask": np.where(valid, 0.0, NEG).reshape(P, -1),
        "cmp_any": valid.any(-1) * 1.0,
        "new_mask": np.where(r == np.arange(B)[None], 0.0, NEG),
        "block_no": np.broadcast_to(np.arange(16.0)[None], (P, 16)),
    }
    return np.concatenate([parts[n] for n, _ in CONST_PARTS], axis=1).astype(np.float32)


def rope_tables():
    import numpy as np

    half = 8
    inv = np.float32(500000.0) ** (-np.arange(half, dtype=np.float32) / np.float32(half))
    pos = np.concatenate([np.arange(T), np.full(B, 1024)]).astype(np.float32)
    ang = pos[None, :] * inv[:, None].astype(np.float32)
    cos, sin = np.ones((P, N), np.float32), np.zeros((P, N), np.float32)
    for base in (0, 64):
        cos[base:base + 8] = cos[base + 8:base + 16] = np.cos(ang)
        sin[base:base + 8], sin[base + 8:base + 16] = -np.sin(ang), np.sin(ang)
    return np.stack([cos, sin], axis=1)


def feature_major(a, lead=()):
    import numpy as np

    t = a.reshape(a.shape[:-1] + (a.shape[-1] // P, P))
    return np.ascontiguousarray(np.moveaxis(np.moveaxis(t, -1, 0), -1, 1))


def weight_tiles(w, cols):
    import numpy as np

    k, m = w.shape
    return np.ascontiguousarray(w.reshape(k // P, P, m // cols, cols).transpose(2, 1, 0, 3))


def lay_out(i):
    import numpy as np

    d = {}
    x = np.concatenate([i["x_prompt"][0], i["x_sample"][:, 0]], axis=0)
    d["x_t"] = feature_major(x)
    d["consts"] = constants()
    g = np.concatenate([i["norm_mix_g"], i["norm_ffn_g"], i["norm_final_g"][None]])
    d["norm_g"] = np.ascontiguousarray(g.reshape(9, KT, P).transpose(2, 0, 1))
    w = i["ffn_w_in"].reshape(4, KT, P, 2, FT, P)
    d["ffn_w_in"] = np.ascontiguousarray(w.transpose(0, 4, 2, 3, 1, 5)).reshape(4, FT, P, 2 * KT * P)
    w = i["ffn_w_out"].reshape(4, FT, P, KT, P)
    d["ffn_w_out"] = np.ascontiguousarray(w.transpose(0, 3, 2, 1, 4)).reshape(4, KT, P, FT * P)
    w = i["ffn_conv_w"].reshape(4, 3, 2, FT, P)
    d["ffn_conv_w"] = np.ascontiguousarray(w.transpose(0, 4, 3, 2, 1)).reshape(4, P, FT * 6)
    w = i["state_ffn_conv"].reshape(4, B, 2, 2, FT, P)
    d["ffn_state"] = np.ascontiguousarray(w.transpose(0, 5, 4, 3, 2, 1)).reshape(4, P, FT * 2, 2, B)
    w = i["lru_w_in"][0].reshape(KT, P, 2, KT, P)
    d["lru_w_in"] = np.ascontiguousarray(w.transpose(3, 1, 2, 0, 4)[:, :, ::-1]).reshape(KT, P, 2 * KT * P)
    d["lru_w_out"] = weight_tiles(i["lru_w_out"][0], P).reshape(KT, P, KT * P)
    small = np.concatenate([i["lru_conv_w"][0], i["lru_conv_b"], i["lru_b_ga"], i["lru_b_gx"], i["lru_lambda"]])
    d["lru_small"] = np.ascontiguousarray(small.reshape(8, KT, P).transpose(2, 1, 0))
    d["lru_state"] = np.ascontiguousarray(i["state_lru_conv"][0].reshape(B, 3, KT, P).transpose(3, 2, 1, 0))
    d["lru_h0"] = np.ascontiguousarray(i["state_lru_h"][0].reshape(B, KT, P).transpose(2, 1, 0))
    w = np.concatenate([i["lru_w_ga"], i["lru_w_gx"]])
    d["lru_w_gates"] = np.ascontiguousarray(w.transpose(2, 0, 1, 3))
    w = i["gdn_w_in"][0]
    heads = w[:, :4096].reshape(KT, P, 4, 8, P)
    d["gdn_w_in"] = np.ascontiguousarray(heads.transpose(3, 1, 2, 0, 4)).reshape(8, P, 4 * KT * P)
    ab = np.zeros((P, KT, 40), np.float32)
    gates = w[:, 4096:].reshape(KT, P, 2, 8).transpose(1, 0, 2, 3)
    ab[:, :, 0:8], ab[:, :, 32:40] = gates[:, :, 0], gates[:, :, 1]
    d["gdn_w_ab"] = ab
    d["gdn_head_w"] = np.ascontiguousarray(np.stack([i["gdn_A_log"][0], i["gdn_dt_bias"][0]], axis=1))
    d["gdn_taps"] = np.ascontiguousarray(i["gdn_conv_w"][0].reshape(4, 3, 8, P).transpose(3, 2, 1, 0))
    d["gdn_conv_state"] = np.ascontiguousarray(i["state_gdn_conv"][0].reshape(B, 3, 3, 8, P).transpose(4, 3, 2, 1, 0))
    d["gdn_norm_g"] = np.ascontiguousarray(i["gdn_norm_g"].reshape(P, 1))
    d["gdn_state"] = np.ascontiguousarray(i["state_gdn_S"][0].transpose(2, 1, 0, 3)).reshape(P, 8 * B, P)
    d["gdn_w_out"] = weight_tiles(i["gdn_w_out"][0], P).reshape(KT, P, KT * P)
    head = np.array([(2 * gp + g2) * 4 + jj for gp in range(2) for jj in range(4) for g2 in range(2)])
    order = (head[:, None] * 64 + np.arange(64)).reshape(-1)
    w = i["nsa_w_in"]
    kv0 = 1024
    cols = np.concatenate([order] + [kv0 + 256 * k + np.arange(256) for k in (0, 1, 2, 4)])
    wf = w[:, :, cols].reshape(2, KT, P, 8, 2, P)
    d["nsa_w_in"] = np.ascontiguousarray(wf.transpose(0, 3, 2, 4, 1, 5)).reshape(2, 8, P, 2 * KT * P)
    gates = w[:, :, 2560:].reshape(2, D, 3, 2, 2, 4).transpose(0, 1, 2, 4, 3, 5).reshape(2, D, 48)
    wv = np.concatenate([w[:, :, kv0 + 768:kv0 + 1024], w[:, :, kv0 + 1280:kv0 + 1536], gates], axis=2)
    d["nsa_w_v"] = np.ascontiguousarray(wv.reshape(2, KT, P, 560).transpose(0, 2, 1, 3))
    wo = i["nsa_w_out"][:, order].reshape(2, KT, P, KT, P)
    d["nsa_w_out"] = np.ascontiguousarray(wo.transpose(0, 3, 2, 1, 4)).reshape(2, KT, P, KT * P)
    d["rope"] = rope_tables()
    pe = i["nsa_cmp_pe"].transpose(0, 3, 1, 2)
    d["nsa_pe"] = np.ascontiguousarray(np.concatenate([pe, pe], axis=1))
    wc = np.zeros((2, P, 2, 32, P), np.float32)
    wt = i["nsa_cmp_w"].transpose(0, 3, 1, 2, 4)
    wc[:, 0:64, :, :, 0:64], wc[:, 64:, :, :, 64:] = wt, wt
    d["nsa_w_cmp"] = wc
    d["page_table"] = i["page_table"].reshape(1, -1)
    c = i["cache_nsa_cmp"].reshape(2, 80, 4, 32, 2, 2, 2, 64)
    d["cmp_pages"] = np.ascontiguousarray(c.transpose(0, 1, 6, 7, 4, 5, 3, 2)).reshape(2, 80, P, 512)
    c = i["cache_nsa_sel"].reshape(2, 80, P, 2, 2, 2, 64)
    keys = c[:, :, :, 0].transpose(0, 1, 4, 5, 3, 2).reshape(2, 80, P, 256)
    d["sel_pages"] = np.concatenate([keys, c[:, :, :, 1].reshape(2, 80, P, 256)], axis=3)
    c = i["state_nsa_win"].reshape(2, B, 512, 2, 2, 2, 64)
    keys = c[:, :, :, 0].transpose(0, 1, 4, 5, 3, 2).reshape(2, B, P, 1024)
    vals = c[:, :, :, 1].reshape(2, B, 4, P, 256).transpose(0, 1, 3, 2, 4).reshape(2, B, P, 1024)
    d["win_state"] = np.concatenate([keys, vals], axis=3)
    return d


def assemble(r):
    import numpy as np

    out = {}
    y = r["y_t"].transpose(2, 1, 0).reshape(N, D)
    out["y_prompt"], out["y_sample"] = y[None, :T], y[T:, None]
    last = r["ffn_last"].reshape(4, P, FT, 2, 10).transpose(0, 4, 3, 2, 1).reshape(4, 10, 2 * DFF)
    old = r["ffn_old"].reshape(4, P, FT, 2, B).transpose(0, 4, 3, 2, 1).reshape(4, B, 2 * DFF)
    out["ffn_p"] = last[:, None, 0:2]
    out["ffn_s"] = np.stack([old, last[:, 2:]], axis=2)
    last = r["lru_last"].transpose(2, 1, 0).reshape(11, D)
    old = r["lru_old"].transpose(3, 2, 1, 0).reshape(B, 2, D)
    out["lc_p"] = last[None, None, 0:3]
    out["lc_s"] = np.concatenate([old, last[3:, None]], axis=1)[None]
    h = r["lru_h"].transpose(2, 1, 0).reshape(9, D)
    out["lh_p"], out["lh_s"] = h[None, 0:1], h[None, 1:]
    last = r["gdn_last"].transpose(3, 2, 1, 0).reshape(11, 3072)
    old = r["gdn_old"].transpose(4, 3, 2, 1, 0).reshape(B, 2, 3072)
    out["gc_p"] = last[None, None, 0:3]
    out["gc_s"] = np.concatenate([old, last[3:, None]], axis=1)[None]
    out["gS_p"] = r["gdn_state_p"].transpose(1, 0, 2)[None, None]
    out["gS_s"] = r["gdn_state_s"].reshape(P, 8, B, P).transpose(2, 1, 0, 3)[None]
    kv = r["nsa_kv"].reshape(2, 2, 64, 4, 2, N)
    kv = kv.transpose(3, 0, 5, 4, 1, 2).reshape(4, 2, N, 4, 64)
    vp = r["nsa_v"].transpose(0, 2, 1, 3).reshape(2, T, 2, 4, 64)
    v = np.concatenate([vp, r["nsa_v_new"].reshape(2, B, 2, 4, 64)], axis=1)
    cmp = np.stack([kv[0], kv[1]], axis=2)
    sel = np.stack([kv[2], v[:, :, 0]], axis=2)
    win = np.stack([kv[3], v[:, :, 1]], axis=2)
    for name, a in (("cmp", cmp), ("sel", sel), ("win", win)):
        out[name + "_p"] = a[:, None, :T]
    out["cmp_s"], out["sel_s"] = cmp[:, T:, None], sel[:, T:, None]
    kept = r["win_kept"]
    keys = kept[:, :, :, :1024].reshape(2, B, 2, 64, 2, 512).transpose(0, 1, 5, 4, 2, 3).reshape(2, B, 512, 4, 64)
    vals = kept[:, :, :, 1024:].reshape(2, B, P, 4, 4, 64).transpose(0, 1, 3, 2, 4, 5).reshape(2, B, 512, 4, 64)
    old = np.stack([keys, vals], axis=3)[:, :, 1:]
    out["win_s"] = np.concatenate([old, win[:, T:, None]], axis=2)
    return out


ORDER = ["y_prompt", "y_sample", "cmp_p", "cmp_s", "sel_p", "sel_s", "win_p", "win_s", "gS_p", "gS_s",
         "gc_p", "gc_s", "lh_p", "lh_s", "lc_p", "lc_s", "ffn_p", "ffn_s"]


def kernel(**inputs):
    import numpy as np
    import concourse.bacc as bacc
    from concourse.bass_utils import run_bass_kernel_spmd

    nc = bacc.Bacc("TRN2", target_bir_lowering=False, num_devices=1)
    arrays = {n: np.ascontiguousarray(a) for n, a in lay_out({n: np.asarray(a) for n, a in inputs.items()}).items()}
    d = {n: nc.dram_tensor(n, a.shape, mybir.dt.from_np(a.dtype), kind="ExternalInput").ap()
         for n, a in arrays.items()}
    o = {n: nc.dram_tensor(n, shape, F32, kind="ExternalOutput").ap() for n, shape in OUTPUTS.items()}
    trunk_program(nc, d, o)
    r = run_bass_kernel_spmd(nc, [arrays], core_ids=[0])
    results = assemble({n: np.asarray(r.results[0][n]) for n in OUTPUTS})
    return tuple(np.ascontiguousarray(results[n]) for n in ORDER)
```

```python
from contextlib import ExitStack

import concourse.bass as bass
from concourse import mybir

F32 = mybir.dt.float32
F32R = mybir.dt.float32r
BF16 = mybir.dt.bfloat16
I32 = mybir.dt.int32
ACT = mybir.ActivationFunctionType
ALU = mybir.AluOpType
AX = mybir.AxisListType.X

P = 128
D = 1024
KT = D // P
T = 512
B = 8
N = T + B
H = N // 2
EPS = 1e-6
NEG = -1e30
DFF = 2816
FT = DFF // P
CH = 128
NCH = T // CH
HEADS = 16
PAGES = 8
N_PHYS = 80
NCMP = 32
PCMP = T // 32

CONST_PARTS = [("ident", 128), ("ones", 128), ("neg_upper", 128), ("strict_t", 128), ("same16", 128),
               ("pair16", 128), ("pair32", 128), ("pair64", 128), ("causal", 128), ("rope_swap", 128),
               ("four_sum", 128), ("cmp_mask", 4 * PCMP), ("cmp_any", 4), ("new_mask", B), ("block_no", 16)]
CONST_AT, _at = {}, 0
for _name, _n in CONST_PARTS:
    CONST_AT[_name] = (_at, _at + _n)
    _at += _n
CONST_COLS = _at


class Steps:

    def __init__(self, eng, sem):
        self.eng, self.sem, self.n, self.at = eng, sem, 0, 0

    def did(self, ins):
        ins.then_inc(self.sem, 1)
        self.n += 1

    def settle(self):
        self.eng.wait_ge(self.sem, self.at + self.n)


def flat(ap):
    return ap.rearrange("p o n -> p (o n)")


class Scope:

    def __init__(self, nc, ctx, prefix):
        self.nc, self.ctx, self.prefix, self.sems = nc, ctx, prefix, []
        ctx.callback(self.clear)

    def clear(self):
        if self.sems:
            self.nc.clear_and_free_semaphores(self.sems)
            self.nc.all_engine_barrier()

    def sb(self, name, shape, dt=F32):
        return self.ctx.enter_context(self.nc.sbuf_tensor(f"{self.prefix}_{name}_sb", shape, dt))

    def below(self, *named):
        with ExitStack() as place:
            return [place.enter_context(self.nc.sbuf_tensor(f"{self.prefix}_{name}_sb", shape, dt))
                    for name, shape, dt in named]

    def ps(self, name, shape, dt=F32):
        return self.ctx.enter_context(self.nc.psum_tensor(f"{self.prefix}_{name}", shape, dt))

    def sem(self, name):
        self.sems.append(self.nc.alloc_semaphore(f"{self.prefix}_{name}"))
        return self.sems[-1]


class Norm:

    def __init__(self, sc, g, ps, split=False, parts=None):
        self.sc, self.g, self.ps, self.split = sc, g, ps, split
        if split:
            self.hi, self.lo = parts or [sc.sb(n, [P, KT, N], F32R) for n in ("x_hi", "x_lo")]
            self.hi_done = sc.sem("x_hi_done")
            self.lo_done = sc.sem("x_lo_done")
        self.sq = sc.sb("norm_sq", [P, 2, N])
        self.rstd = sc.sb("norm_rstd", [P, N])
        self.squared = sc.sem("norm_squared")
        self.summed = sc.sem("norm_summed")
        self.rooted = sc.sem("norm_rooted")
        self.inverted = sc.sem("norm_inverted")
        self.normed = sc.sem("norm_normed")

    def act(self, act, xt, eps):
        for kt in range(KT):
            if kt >= 2:
                act.wait_ge(self.summed, kt - 1)
            act.activation(self.sq[:, kt % 2, :], xt[:, kt, :], ACT.Square).then_inc(self.squared, 1)
        act.wait_ge(self.summed, KT)
        act.activation(self.rstd[:, :].rearrange("p (h n) -> p h n", h=2), self.ps[:, 0:2, 0:H], ACT.Sqrt,
                       bias=eps[:, 0:1], scale=1.0 / D).then_inc(self.rooted, 1)

    def pe(self, pe, ones):
        for kt in range(KT):
            pe.wait_ge(self.squared, kt + 1)
            for h in range(2):
                mm = pe.matmul(self.ps[:, h, 0:H], ones, self.sq[:, kt % 2, h * H:(h + 1) * H],
                               start=(kt == 0), stop=(kt == KT - 1))
            mm.then_inc(self.summed, 1)

    def dve(self, dve, xt, xn, meanwhile=lambda: None):
        dve.wait_ge(self.rooted, 1)
        dve.reciprocal(self.rstd[:, :], self.rstd[:, :]).then_inc(self.inverted, 1)
        meanwhile()
        dve.wait_ge(self.inverted, 1)
        for kt in range(KT):
            dve.scalar_tensor_tensor(xn[:, kt, :], xt[:, kt, :], self.g[:, kt:kt + 1], self.rstd[:, :],
                                     ALU.mult, ALU.mult).then_inc(self.normed, 1)
            if self.split and kt:
                self.rest(dve, xn, kt - 1)
        if self.split:
            self.rest(dve, xn, KT - 1)

    def act_split(self, act, xn):
        for kt in range(KT):
            act.wait_ge(self.normed, kt + 1)
            act.activation(self.hi[:, kt, :], xn[:, kt, :], ACT.Copy).then_inc(self.hi_done, 1)

    def rest(self, dve, xn, kt):
        dve.wait_ge(self.hi_done, kt + 1)
        dve.tensor_tensor(self.lo[:, kt, :], xn[:, kt, :], self.hi[:, kt, :], ALU.subtract).then_inc(self.lo_done, 1)


def three_products(pe, out, w_hi, w_lo, x_hi, x_lo, start, stop):
    for k, (w, x) in enumerate(((w_hi, x_hi), (w_hi, x_lo), (w_lo, x_hi))):
        for h in range(2):
            mm = pe.matmul(out(h), w, x[:, h * H:(h + 1) * H], start=start and k == 0, stop=stop and k == 2)
    return mm


class Weights:

    def __init__(self, sc, cols, raws, slots):
        self.raws, self.slots, self.cols = raws, slots, cols
        self.raw = sc.sb("w_raw", [P, raws, cols])
        self.hi = sc.sb("w_hi", [P, slots, cols], F32R)
        self.lo = sc.sb("w_lo", [P, slots, cols], F32R)
        self.raw_in = [sc.sem(f"w_raw_in{k}") for k in range(raws)]
        self.hi_done = sc.sem("w_hi_done")
        self.lo_done = sc.sem("w_lo_done")

    def load(self, sp, u, src):
        if u >= self.raws:
            sp.wait_ge(self.lo_done, u - self.raws + 1)
        sp.dma_start(self.raw[:, u % self.raws], src).then_inc(self.raw_in[u % self.raws], 16)

    def lead(self, act, u):
        act.wait_ge(self.raw_in[u % self.raws], 16 * (u // self.raws + 1))
        act.activation(self.hi[:, u % self.slots], self.raw[:, u % self.raws], ACT.Copy).then_inc(self.hi_done, 1)

    def rest(self, eng, u):
        eng.wait_ge(self.hi_done, u + 1)
        eng.tensor_tensor(self.lo[:, u % self.slots], self.raw[:, u % self.raws], self.hi[:, u % self.slots],
                          ALU.subtract).then_inc(self.lo_done, 1)

    def project(self, pe, u, out, norm):
        pe.wait_ge(self.lo_done, u + 1)
        for kt in range(KT):
            if u == 0:
                pe.wait_ge(norm.lo_done, kt + 1)
            part = slice(kt * P, (kt + 1) * P)
            mm = three_products(pe, out, self.hi[:, u % self.slots, part], self.lo[:, u % self.slots, part],
                                norm.hi[:, kt], norm.lo[:, kt], kt == 0, kt == KT - 1)
        return mm


def load_stage(nc, d, g):
    with ExitStack() as ctx:
        sc = Scope(nc, ctx, "load")
        loaded = sc.sem("loaded")
        block = ctx.enter_context(nc.Block())

        @block.sync
        def _(sp):
            sp.dma_start(g.xt[:], d["x_t"]).then_inc(loaded, 16)
            sp.dma_start(g.const[:], d["consts"]).then_inc(loaded, 16)
            sp.dma_start(g.norm_g[:], d["norm_g"]).then_inc(loaded, 16)
            sp.wait_ge(loaded, 48)

        @block.vector
        def _(dve):
            dve.memset(g.eps[:], EPS)
            dve.memset(g.bias_one[:], 1.0)


def ffn_stage(nc, d, o, g, layer):
    groups = ((0, 12), (12, 10))
    with ExitStack() as ctx:
        sc = Scope(nc, ctx, f"ffn{layer}")
        raw = sc.sb("raw", [P, 2, 2 * KT * P])
        w_hi = sc.sb("w_hi", [P, 2, 2 * KT * P], F32R)
        w_lo = sc.sb("w_lo", [P, 2, 2 * KT * P], F32R)
        inner_hi = sc.sb("inner_hi", [P, groups[0][1], N], F32R)
        inner_lo = sc.sb("inner_lo", [P, groups[0][1], N], F32R)
        product = sc.sb("product", [P, N])
        conv_w = sc.sb("conv_w", [P, FT * 2 * 3])
        state = sc.sb("state", [P, FT * 2, 2, B])
        pre = sc.sb("pre", [P, 2, 2, 2 + N])
        conv = sc.sb("conv", [P, 2, 2, N])
        gate = sc.sb("gate", [P, 2, N])
        last = sc.sb("last", [P, FT * 2, 10])
        ps = sc.ps("ps", [P, 2, 2, 2, 512])
        psf = ps[:, :, :, :, :].rearrange("p a b c n -> p (a b c) n")
        norm = Norm(sc, g.norm_g[:, 4 + layer, :], psf, split=True)
        small_in = sc.sem("small_in")
        raw_in = [sc.sem(f"raw_in{s}") for s in range(2)]
        hi_done = sc.sem("hi_done")
        lo_done = sc.sem("lo_done")
        zeroed = sc.sem("zeroed")
        projected = sc.sem("projected")
        copied = sc.sem("copied")
        convolved = sc.sem("convolved")
        gated = sc.sem("gated")
        joined = sc.sem("joined")
        dve_own = sc.sem("dve_own")
        out_done = sc.sem("out_done")
        added = sc.sem("added")
        stored = sc.sem("stored")
        block = ctx.enter_context(nc.Block())

        def at(f, a, b):
            return f[0] * (2 * a) + (a * f[1] + b)

        def starts(f):
            return isinstance(f[0], int) and 2 * f[0] + f[1] < 2

        def before(f):
            return f[0], f[1] - 1

        def pairs(eng, gi, pair):
            n = groups[gi][1]
            pair(0, True, False)
            with eng.Fori(1, n // 2 - 1) as i:
                pair(i, False, False)
            pair(n // 2 - 1, False, True)

        @block.sync
        def _(sp):
            def w_in_load(f, gi):
                s = f[1] % 2
                if not starts(f):
                    sp.wait_ge(lo_done, at(f, 1, 8 * gi - 1))
                src = d["ffn_w_in"][layer, bass.ds(at(f, 1, 0), 1)].rearrange("o p n -> p (o n)")
                sp.dma_start(raw[:, s], src).then_inc(raw_in[s], 16)

            for gi, (f0, n) in enumerate(groups):
                w_in_load((0, f0), gi), w_in_load((0, f0 + 1), gi)
                if gi == 0:
                    sp.dma_start(conv_w[:], d["ffn_conv_w"][layer]).then_inc(small_in, 16)
                    sp.dma_start(state[:], d["ffn_state"][layer]).then_inc(small_in, 16)
                with sp.Fori(1, n // 2) as i:
                    w_in_load((i, f0), gi), w_in_load((i, f0 + 1), gi)
                for m in range(KT):
                    sp.wait_ge(lo_done, f0 + n + 8 * gi + m - 1)
                    sp.dma_start(raw[:, m % 2, 0:n * P], d["ffn_w_out"][layer, m, :, f0 * P:(f0 + n) * P]).then_inc(raw_in[m % 2], 16)
            sp.wait_ge(joined, FT)
            sp.dma_start(o["ffn_last"][layer], last[:]).then_inc(stored, 16)
            sp.dma_start(o["ffn_old"][layer], state[:, :, 1, :]).then_inc(stored, 16)
            sp.wait_ge(stored, 32)

        @block.tensor
        def _(pe):
            norm.pe(pe, g.ones)

            def three(bank, w, xh, xl, start, stop):
                for k, (wp, xp) in enumerate(((w_hi, xh), (w_hi, xl), (w_lo, xh))):
                    for h in range(2):
                        mm = pe.matmul(psf[:, bank + h, 0:H], wp[:, w[0], w[1]:w[1] + P], xp[:, h * H:(h + 1) * H],
                                       start=start and k == 0, stop=stop and k == 2)
                return mm

            def tile(f, gi):
                s = f[1] % 2
                pe.wait_ge(lo_done, at(f, 1, 8 * gi + 1))
                if not starts(f):
                    pe.wait_ge(copied, at(f, 2, -2))
                for vg in range(2):
                    for kt in range(KT):
                        if starts(f) and s == 0 and vg == 0:
                            pe.wait_ge(norm.lo_done, kt + 1)
                        mm = three(4 * s + 2 * vg, (s, (vg * KT + kt) * P), norm.hi[:, kt], norm.lo[:, kt],
                                   kt == 0, kt == KT - 1)
                    mm.then_inc(projected, 1)

            for gi, (f0, n) in enumerate(groups):
                if gi:
                    pe.wait_ge(added, KT * gi)
                pairs(pe, gi, lambda i, *_: (tile((i, f0), gi), tile((i, f0 + 1), gi)))
                for m in range(KT):
                    pe.wait_ge(lo_done, f0 + n + 8 * gi + m + 1)
                    if m == 0:
                        pe.wait_ge(copied, 2 * (f0 + n) - 2)
                        pe.wait_ge(joined, f0 + n - 2)
                    if m >= 4:
                        pe.wait_ge(added, KT * gi + m - 3)
                    for k in range(n):
                        if m == 0 and k >= n - 2:
                            pe.wait_ge(joined, f0 + k + 1)
                        mm = three(2 * (m % 4), (m % 2, k * P), inner_hi[:, k], inner_lo[:, k], k == 0, k == n - 1)
                    mm.then_inc(out_done, 1)

        @block.scalar
        def _(act):
            def split(gi, s, size, f=None, c=None):
                act.wait_ge(raw_in[s], 16 * (c // 2 + 1) if f is None
                            else f[0] * 16 + 16 * ((f[1] + 8 * gi) // 2 + 2))
                act.activation(w_hi[:, s, 0:size], raw[:, s, 0:size], ACT.Copy).then_inc(hi_done, 1)

            norm.act(act, g.xt, g.eps)
            split(0, 0, 2 * KT * P, c=0)
            norm.act_split(act, g.xn)
            split(0, 1, 2 * KT * P, c=1)
            act.wait_ge(small_in, 32)

            def copy(f):
                s = f[1] % 2
                for vg in range(2):
                    if not starts(f):
                        if vg == 0:
                            act.wait_ge(joined, at(f, 1, -1))
                        act.wait_ge(convolved, at(f, 2, vg - 3))
                    act.wait_ge(projected, at(f, 2, vg + 1))
                    src = ps[:, s, vg, :, 0:H]
                    act.activation(pre[:, s, vg, 2:2 + N].rearrange("p (h n) -> p h n", h=2), src, ACT.Copy)
                    tap = conv_w[:, bass.ds(at(f, 6, 3 * vg + 2), 1)]
                    act.activation(conv[:, s, vg, :].rearrange("p (h n) -> p h n", h=2), src, ACT.Copy,
                                   scale=tap).then_inc(copied, 1)

            def silu(f):
                act.wait_ge(convolved, at(f, 2, 2))
                act.activation(gate[:, f[1] % 2, :], conv[:, f[1] % 2, 1, :], ACT.Silu).then_inc(gated, 1)

            for gi, (f0, n) in enumerate(groups):
                def pair(i, first, last_pair):
                    for f in ((i, f0), (i, f0 + 1)):
                        copy(f)
                        if not last_pair or f[1] == f0:
                            split(gi, f[1] % 2, n * P if last_pair else 2 * KT * P, f=f)
                        if not first or f[1] > f0:
                            silu(before(f))

                pairs(act, gi, pair)
                silu((n // 2 - 1, f0 + 1))
                split(gi, 1, n * P, f=(n // 2 - 1, f0 + 1))
                for m in range(KT):
                    c = f0 + n + 8 * gi + m + 2
                    if c < FT + 2 * KT:
                        act.wait_ge(out_done, KT * gi + m + 1)
                        split(gi, m % 2, n * P if m < KT - 2 else 2 * KT * P, c=c)

        @block.vector
        def _(dve):
            own = Steps(dve, dve_own)

            def split(s, size, count):
                dve.wait_ge(hi_done, count)
                dve.tensor_tensor(w_lo[:, s, 0:size], raw[:, s, 0:size], w_hi[:, s, 0:size], ALU.subtract).then_inc(lo_done, 1)

            dve.memset(pre[:, :, :, 0:2], 0.0).then_inc(zeroed, 1)
            norm.dve(dve, g.xt, g.xn, meanwhile=lambda: split(0, 2 * KT * P, 1))
            split(1, 2 * KT * P, 2)
            dve.wait_ge(small_in, 32)
            dve.wait_ge(zeroed, 1)

            def taps(f, vg):
                dve.wait_ge(copied, at(f, 2, vg + 1))
                y, x = conv[:, f[1] % 2, vg, :], pre[:, f[1] % 2, vg, :]
                row = bass.ds(at(f, 2, vg), 1)
                w = [conv_w[:, bass.ds(at(f, 6, 3 * vg + j), 1)] for j in range(2)]
                old = [state[:, row, j, :].rearrange("p o b -> p (o b)") for j in range(2)]
                own.did(dve.scalar_tensor_tensor(y[:, 0:T], x[:, 1:1 + T], w[1], y[:, 0:T], ALU.mult, ALU.add))
                own.did(dve.scalar_tensor_tensor(y[:, T:N], old[1], w[1], y[:, T:N], ALU.mult, ALU.add))
                dve.tensor_copy(last[:, row, :].rearrange("p o c -> p (o c)"), x[:, T:T + 10])
                own.settle()
                dve.scalar_tensor_tensor(y[:, 0:T], x[:, 0:T], w[0], y[:, 0:T], ALU.mult, ALU.add)
                dve.scalar_tensor_tensor(y[:, T:N], old[0], w[0], y[:, T:N], ALU.mult, ALU.add).then_inc(convolved, 1)

            def join(f, f0):
                s = f[1] % 2
                k = bass.ds(at(f, 1, -f0), 1)
                dve.wait_ge(gated, at(f, 1, 1))
                dve.wait_ge(convolved, at(f, 2, 1))
                if not starts(f):
                    dve.wait_ge(joined, at(f, 1, 0))
                own.did(dve.tensor_tensor(flat(inner_hi[:, k, :]), conv[:, s, 0, :], gate[:, s, :], ALU.mult))
                own.did(dve.tensor_tensor(product[:, :], conv[:, s, 0, :], gate[:, s, :], ALU.mult))
                own.settle()
                dve.tensor_tensor(flat(inner_lo[:, k, :]), product[:, :], flat(inner_hi[:, k, :]), ALU.subtract).then_inc(joined, 1)

            for gi, (f0, n) in enumerate(groups):
                base = 6 * f0

                def pair(i, first, last_pair):
                    own.n, own.at = 0, (base if first else i * 12 + (base - 2))
                    for f in ((i, f0), (i, f0 + 1)):
                        taps(f, 0), taps(f, 1)
                        if not last_pair or f[1] == f0:
                            split(f[1] % 2, n * P if last_pair else 2 * KT * P, at(f, 1, 8 * gi + 3))
                        if not first or f[1] > f0:
                            join(before(f), f0)

                pairs(dve, gi, pair)
                join((n // 2 - 1, f0 + 1), f0)
                split(1, n * P, at((n // 2 - 1, f0 + 1), 1, 8 * gi + 3))
                for m in range(KT):
                    dve.wait_ge(out_done, KT * gi + m + 1)
                    x = g.xt[:, m, :].rearrange("p (h n) -> p h n", h=2)
                    dve.tensor_tensor(x, x, psf[:, 2 * (m % 4):2 * (m % 4) + 2, 0:H], ALU.add).then_inc(added, 1)
                    c = f0 + n + 8 * gi + m + 2
                    if c < FT + 2 * KT:
                        split(m % 2, n * P if m < KT - 2 else 2 * KT * P, c + 1)


class OutProjection:

    def __init__(self, sc, ps, w, first, hi, lo):
        self.ps, self.w, self.first = ps, w, first
        self.hi, self.lo = hi, lo
        self.hi_done = sc.sem("y_hi_done")
        self.lo_done = sc.sem("y_lo_done")
        self.done = sc.sem("out_done")
        self.added = sc.sem("out_added")

    def load(self, sp, src):
        for m in range(KT):
            self.w.load(sp, self.first + m, src[m])

    def lead(self, act, y, kt):
        act.activation(self.hi[:, kt, :], y[:, kt, :], ACT.Copy).then_inc(self.hi_done, 1)

    def rest(self, dve, y, kt):
        dve.wait_ge(self.hi_done, kt + 1)
        dve.tensor_tensor(self.lo[:, kt, :], y[:, kt, :], self.hi[:, kt, :], ALU.subtract).then_inc(self.lo_done, 1)

    def pe(self, pe, then=lambda: None):
        def tile(m, kt):
            if kt == 0:
                pe.wait_ge(self.w.lo_done, self.first + m + 1)
                if m >= 4:
                    pe.wait_ge(self.added, m - 3)
            slot, part = (self.first + m) % self.w.slots, slice(kt * P, (kt + 1) * P)
            mm = three_products(pe, lambda h: self.ps[:, 2 * (m % 4) + h, 0:H], self.w.hi[:, slot, part],
                                self.w.lo[:, slot, part], self.hi[:, kt], self.lo[:, kt], kt == 0, kt == KT - 1)
            if kt == KT - 1:
                mm.then_inc(self.done, 1)

        for kt in range(KT):
            pe.wait_ge(self.lo_done, kt + 1)
            for m in range(2):
                tile(m, kt)
        then()
        for m in range(2, KT):
            for kt in range(KT):
                tile(m, kt)

    def act(self, act):
        for m in range(self.w.slots, KT):
            act.wait_ge(self.done, m - self.w.slots + 1)
            self.w.lead(act, self.first + m)

    def dve(self, dve, xt):
        for m in range(KT):
            dve.wait_ge(self.done, m + 1)
            x = xt[:, m, :].rearrange("p (h n) -> p h n", h=2)
            dve.tensor_tensor(x, x, self.ps[:, 2 * (m % 4):2 * (m % 4) + 2, 0:H], ALU.add).then_inc(self.added, 1)


def log1p_of(own, dve, out, x, tmp):
    s, z = tmp
    own.did(dve.tensor_scalar(z, x, 2.0, None, ALU.add))
    own.settle()
    own.did(dve.reciprocal(z, z))
    own.settle()
    own.did(dve.tensor_tensor(s, x, z, ALU.mult))
    own.settle()
    own.did(dve.tensor_tensor(z, s, s, ALU.mult))
    own.settle()
    terms = [2.0 / k for k in range(17, 0, -2)]
    own.did(dve.tensor_scalar(out, z, terms[0], terms[1], ALU.mult, ALU.add))
    for c in terms[2:]:
        own.settle()
        own.did(dve.tensor_tensor(out, out, z, ALU.mult))
        own.settle()
        own.did(dve.tensor_scalar(out, out, c, None, ALU.add))
    own.settle()
    own.did(dve.tensor_tensor(out, out, s, ALU.mult))
    own.settle()


def lru_stage(nc, d, o, g):
    with ExitStack() as ctx:
        sc = Scope(nc, ctx, "lru")
        small = sc.sb("small", [P, KT, 8])
        state = sc.sb("state", [P, KT, 3, B])
        h0 = sc.sb("h0", [P, KT, B])
        w_gates = sc.sb("w_gates", [P, 2, KT, P])
        pre = sc.sb("pre", [P, 2, 3 + N])
        xc = sc.sb("xc", [P, 3, N])
        raw = sc.sb("raw_gate", [P, 3, N])
        r = sc.sb("r", [P, 2, N])
        i_g = sc.sb("i", [P, 2, N])
        t2 = sc.sb("t", [P, 2, N])
        root = sc.sb("root", [P, 2, N])
        r1 = sc.sb("r1", [P, N])
        hs = sc.sb("hs", [P, KT, N])
        gelu = raw
        y = g.xn
        rate = sc.sb("rate", [P, KT])
        rtmp = sc.sb("rtmp", [P, 4, KT])
        last = sc.sb("last", [P, KT, 11])
        ps = sc.ps("ps", [P, 8, 512])
        norm = Norm(sc, g.norm_g[:, 2, :], ps, split=True)
        w_in = Weights(sc, KT * P, 3, 3)
        proj = OutProjection(sc, ps, w_in, 2 * KT, norm.hi, norm.lo)
        small_in = sc.sem("small_in")
        zeroed = sc.sem("zeroed")
        projected = sc.sem("projected")
        copied = sc.sem("copied")
        convolved = sc.sem("convolved")
        gates_done = sc.sem("gates_done")
        activated = sc.sem("activated")
        rooted = sc.sem("rooted")
        gelued = sc.sem("gelued")
        finished = sc.sem("finished")
        abs_done = sc.sem("abs_done")
        exp_done = sc.sem("exp_done")
        rate_done = sc.sem("rate_done")
        act_own = sc.sem("act_own")
        dve_own = sc.sem("dve_own")
        stored = sc.sem("stored")
        block = ctx.enter_context(nc.Block())

        @block.sync
        def _(sp):
            for u in range(2 * KT):
                w_in.load(sp, u, d["lru_w_in"][u // 2, :, u % 2 * KT * P:(u % 2 + 1) * KT * P])
                if u == 1:
                    sp.dma_start(small[:], d["lru_small"]).then_inc(small_in, 16)
                    sp.dma_start(state[:], d["lru_state"]).then_inc(small_in, 16)
                    sp.dma_start(h0[:], d["lru_h0"]).then_inc(small_in, 16)
                    sp.dma_start(w_gates[:], d["lru_w_gates"]).then_inc(small_in, 16)
            proj.load(sp, d["lru_w_out"])
            sp.wait_ge(finished, KT)
            sp.dma_start(o["lru_last"], last[:]).then_inc(stored, 16)
            sp.dma_start(o["lru_h"], hs[:, :, T - 1:N]).then_inc(stored, 16)
            sp.dma_start(o["lru_old"], state[:, :, 1:3, :]).then_inc(stored, 16)
            sp.wait_ge(stored, 48)

        @block.tensor
        def _(pe):
            norm.pe(pe, g.ones)
            pe.wait_ge(small_in, 64)

            def gate_products(n):
                pe.wait_ge(convolved, n + 1)
                if n >= 1:
                    pe.wait_ge(activated, n)
                for w in range(2):
                    for h in range(2):
                        mm = pe.matmul(ps[:, 4 + 2 * w + h, 0:H], w_gates[:, w, n, :],
                                       xc[:, n % 3, h * H:(h + 1) * H], start=True, stop=True)
                mm.then_inc(gates_done, 1)

            for n in range(KT):
                for w in range(2):
                    if n >= 1:
                        pe.wait_ge(copied, 2 * (n - 1) + w + 1)
                    w_in.project(pe, 2 * n + w, lambda h: ps[:, 2 * w + h, 0:H], norm).then_inc(projected, 1)
                if n >= 1:
                    gate_products(n - 1)
            gate_products(KT - 1)
            pe.wait_ge(copied, 2 * KT)
            proj.pe(pe, then=lambda: pe.wait_ge(activated, KT))

        @block.scalar
        def _(act):
            norm.act(act, g.xt, g.eps)
            w_in.lead(act, 0)
            norm.act_split(act, g.xn)
            w_in.lead(act, 1), w_in.lead(act, 2)
            act.wait_ge(small_in, 64)
            own = Steps(act, act_own)
            act.wait_ge(abs_done, 1)
            act.activation(rtmp[:, 1, :], rtmp[:, 0, :], ACT.Exp, scale=-1.0).then_inc(exp_done, 1)

            def halves(ap):
                return ap.rearrange("p (h n) -> p h n", h=2)

            def gates(n):
                s = n % 2
                act.wait_ge(gates_done, n + 1)
                if n >= 2:
                    act.wait_ge(finished, n - 1)
                own.did(act.activation(halves(r[:, s, :]), ps[:, 4:6, 0:H], ACT.Sigmoid, bias=small[:, n, 5:6]))
                act.activation(halves(i_g[:, s, :]), ps[:, 6:8, 0:H], ACT.Sigmoid, bias=small[:, n, 6:7])
                own.settle()
                act.wait_ge(rate_done, 1)
                act.activation(t2[:, s, :], r[:, s, :], ACT.Tanh, scale=rate[:, n:n + 1]).then_inc(activated, 1)
                act.wait_ge(activated, n + 1)
                act.activation(gelu[:, n % 3, :], raw[:, n % 3, :], ACT.Gelu_apprx_tanh).then_inc(gelued, 1)
                act.activation(root[:, s, :], t2[:, s, :], ACT.Sqrt).then_inc(rooted, 1)

            for n in range(KT):
                s = n % 2
                act.wait_ge(projected, 2 * n + 1)
                if n >= 2:
                    act.wait_ge(convolved, n - 1)
                if n >= 3:
                    act.wait_ge(finished, n - 2)
                act.activation(halves(pre[:, s, 3:3 + N]), ps[:, 0:2, 0:H], ACT.Copy)
                act.activation(halves(xc[:, n % 3, :]), ps[:, 0:2, 0:H], ACT.Identity, bias=small[:, n, 4:5],
                               scale=small[:, n, 3:4]).then_inc(copied, 1)
                w_in.lead(act, 2 * n + 3)
                act.wait_ge(projected, 2 * n + 2)
                act.activation(halves(raw[:, n % 3, :]), ps[:, 2:4, 0:H], ACT.Copy).then_inc(copied, 1)
                w_in.lead(act, 2 * n + 4)
                if n >= 1:
                    gates(n - 1)
            act.wait_ge(projected, 2 * KT)
            for kt in range(KT):
                if kt == KT - 2:
                    gates(KT - 1)
                act.wait_ge(finished, kt + 1)
                proj.lead(act, y, kt)
            proj.act(act)

        @block.gpsimd
        def _(pool):
            for u in range(3 * KT):
                w_in.rest(pool, u)

        @block.vector
        def _(dve):
            own = Steps(dve, dve_own)
            dve.memset(pre[:, :, 0:3], 0.0).then_inc(zeroed, 1)
            norm.dve(dve, g.xt, g.xn)
            dve.wait_ge(small_in, 64)
            dve.wait_ge(zeroed, 1)
            lam = small[:, :, 7]
            dve.scalar_tensor_tensor(rtmp[:, 0, :], lam, -1.0, lam, ALU.mult, ALU.max).then_inc(abs_done, 1)
            dve.wait_ge(exp_done, 1)
            log1p_of(own, dve, rate[:, :], rtmp[:, 1, :], (rtmp[:, 2, :], rtmp[:, 3, :]))
            own.did(dve.tensor_scalar(rtmp[:, 0, :], lam, -1.0, 0.0, ALU.mult, ALU.max))
            own.settle()
            own.did(dve.tensor_tensor(rate[:, :], rate[:, :], rtmp[:, 0, :], ALU.add))
            own.settle()
            dve.tensor_scalar(rate[:, :], rate[:, :], 4.0, None, ALU.mult).then_inc(rate_done, 1)

            def recur(n):
                s = n % 2
                a, bb = t2[:, s], root[:, s]
                dve.wait_ge(rooted, n + 1)
                own.did(dve.tensor_scalar(r1[:, :], t2[:, s, :], 1.0, None, ALU.add))
                dve.tensor_tensor(i_g[:, s, :], i_g[:, s, :], xc[:, n % 3, :], ALU.mult)
                own.settle()
                own.did(dve.reciprocal(r1[:, :], r1[:, :]))
                own.settle()
                own.did(dve.tensor_scalar(a[:, :], r1[:, :], 2.0, -1.0, ALU.mult, ALU.add))
                own.did(dve.scalar_tensor_tensor(bb[:, :], root[:, s, :], 2.0, r1[:, :], ALU.mult, ALU.mult))
                own.settle()
                own.did(dve.tensor_tensor(bb[:, :], bb[:, :], i_g[:, s, :], ALU.mult))
                own.settle()
                own.did(dve.tensor_tensor_scan(hs[:, n, 0:T], a[:, 0:T], bb[:, 0:T], 0.0, ALU.mult, ALU.add))
                own.did(dve.tensor_tensor(hs[:, n, T:N], a[:, T:N], h0[:, n, :], ALU.mult))
                own.settle()
                own.did(dve.tensor_tensor(hs[:, n, T:N], hs[:, n, T:N], bb[:, T:N], ALU.add))
                own.settle()
                dve.wait_ge(gelued, n + 1)
                dve.tensor_tensor(y[:, n, :], hs[:, n, :], gelu[:, n % 3, :], ALU.mult).then_inc(finished, 1)

            for n in range(KT):
                s = n % 2
                dve.wait_ge(copied, 2 * n + 1)
                x, u = pre[:, s, :], xc[:, n % 3, :]
                dve.tensor_copy(last[:, n, :], x[:, T:T + 11])
                for j in (2, 1, 0):
                    own.did(dve.scalar_tensor_tensor(u[:, 0:T], x[:, j:j + T], small[:, n, j:j + 1], u[:, 0:T],
                                                     ALU.mult, ALU.add))
                    ins = dve.scalar_tensor_tensor(u[:, T:N], state[:, n, j, :], small[:, n, j:j + 1], u[:, T:N],
                                                   ALU.mult, ALU.add)
                    if j:
                        own.did(ins)
                        own.settle()
                    else:
                        ins.then_inc(convolved, 1)
                if n >= 1:
                    recur(n - 1)
            for kt in range(KT):
                if kt == KT - 2:
                    recur(KT - 1)
                proj.rest(dve, y, kt)
            proj.dve(dve, g.xt)


GH = 8
GR = 40


def gdn_project(nc, d, o, g, v):
    with ExitStack() as ctx:
        sc = Scope(nc, ctx, "gdnp")
        w_ab = sc.sb("w_ab", [P, KT, GR])
        taps_w = sc.sb("taps", [P, GH, 3, 4])
        state = sc.sb("state", [P, GH, 3, 3, B])
        heads_w = sc.sb("head_w", [GH, 2])
        decay = sc.sb("decay", [GH, 1])
        pre = sc.sb("pre", [P, 3, 3 + N])
        conv = sc.sb("conv", [P, 3, N])
        sq = sc.sb("sq", [P, 2, N])
        rs = sc.sb("rs", [P, 2, N])
        last = sc.sb("last", [P, GH, 3, 11])
        soft = v.v[0:GH, 4:8, :]
        ps = sc.ps("ps", [P, 8, 512])
        norm = Norm(sc, g.norm_g[:, 1, :], ps, split=True)
        w = Weights(sc, KT * P, 3, 2)
        small_in = sc.sem("small_in")
        zeroed = sc.sem("zeroed")
        ab_done = sc.sem("ab_done")
        ab_copied = sc.sem("ab_copied")
        abs_done = sc.sem("abs_done")
        exp_done = sc.sem("exp_done")
        projected = sc.sem("projected")
        copied = sc.sem("copied")
        convolved = sc.sem("convolved")
        silued = sc.sem("silued")
        squared = sc.sem("squared")
        summed = sc.sem("summed")
        rooted = sc.sem("rooted")
        scaled = sc.sem("scaled")
        cum_done = sc.sem("cum_done")
        turned = sc.sem("turned")
        dve_own = sc.sem("dve_own")
        stored = sc.sem("stored")
        block = ctx.enter_context(nc.Block())
        qkv = [v.q, v.k, v.v]

        def w_load(sp, u):
            w.load(sp, u, d["gdn_w_in"][u // 4, :, u % 4 * KT * P:(u % 4 + 1) * KT * P])

        @block.sync
        def _(sp):
            sp.dma_start(w_ab[:], d["gdn_w_ab"]).then_inc(small_in, 16)
            sp.dma_start(heads_w[:], d["gdn_head_w"]).then_inc(small_in, 16)
            for u in range(2):
                w_load(sp, u)
            sp.dma_start(taps_w[:], d["gdn_taps"]).then_inc(small_in, 16)
            sp.dma_start(state[:], d["gdn_conv_state"]).then_inc(small_in, 16)
            sp.dma_start(v.norm_g[:], d["gdn_norm_g"]).then_inc(small_in, 16)
            for u in range(2, 4 * GH):
                w_load(sp, u)
            sp.wait_ge(convolved, 3 * GH)
            sp.dma_start(o["gdn_last"], last[:]).then_inc(stored, 16)
            sp.dma_start(o["gdn_old"], state[:, :, :, 1:3, :]).then_inc(stored, 16)
            sp.wait_ge(stored, 32)

        @block.tensor
        def _(pe):
            norm.pe(pe, g.ones)
            pe.wait_ge(norm.normed, KT)
            pe.wait_ge(small_in, 80)
            for kt in range(KT):
                for h in range(2):
                    mm = pe.matmul(ps[0:GR, 6 + h, 0:H], w_ab[:, kt, :], g.xn[:, kt, h * H:(h + 1) * H],
                                   start=(kt == 0), stop=(kt == KT - 1))
            mm.then_inc(ab_done, 1)

            def sums(h, t):
                at = 2 * h + t
                pe.wait_ge(squared, at + 1)
                if at == 0:
                    pe.wait_ge(ab_copied, 1)
                else:
                    pe.wait_ge(rooted, at)
                for u in range(2):
                    mm = pe.matmul(ps[:, 6 + u, 0:H], g.ones, sq[:, t, u * H:(u + 1) * H], start=True, stop=True)
                mm.then_inc(summed, 1)

            for h in range(GH):
                for t in range(4):
                    at = 4 * h + t
                    if at >= 3:
                        pe.wait_ge(copied, at - 2)
                    w.project(pe, at, lambda u: ps[:, 2 * (at % 3) + u, 0:H], norm).then_inc(projected, 1)
                    if h >= 1 and t in (1, 3):
                        sums(h - 1, t // 2)
            sums(GH - 1, 0), sums(GH - 1, 1)
            pe.wait_ge(cum_done, 1)
            for c in range(NCH):
                mm = pe.transpose(ps[:, 0, GH * c:GH * c + GH], v.rows[0:GH, c * CH:(c + 1) * CH],
                                  g.ident[0:GH, 0:GH])
            mm.then_inc(turned, 1)

        @block.scalar
        def _(act):
            norm.act(act, g.xt, g.eps)
            w.lead(act, 0)
            norm.act_split(act, g.xn)
            w.lead(act, 1)
            act.wait_ge(small_in, 80)
            act.wait_ge(zeroed, 1)
            act.wait_ge(ab_done, 1)
            act.activation(soft[:, 0, :].rearrange("p (h n) -> p h n", h=2), ps[0:GH, 6:8, 0:H], ACT.Identity,
                           bias=heads_w[:, 1:2])
            act.activation(v.rows[32:GR, :].rearrange("p (h n) -> p h n", h=2), ps[32:GR, 6:8, 0:H],
                           ACT.Sigmoid).then_inc(ab_copied, 1)
            act.wait_ge(abs_done, 1)
            act.activation(decay[:, :], heads_w[:, 0:1], ACT.Exp)
            act.activation(soft[:, 1, :], soft[:, 1, :], ACT.Exp, scale=-1.0).then_inc(exp_done, 1)

            def norms(h, t):
                act.wait_ge(summed, 2 * h + t + 1)
                if h >= 1:
                    act.wait_ge(scaled, 2 * (h - 1) + t + 1)
                act.activation(rs[:, t, :].rearrange("p (h n) -> p h n", h=2), ps[:, 6:8, 0:H], ACT.Sqrt,
                               bias=g.eps[:, 0:1]).then_inc(rooted, 1)

            for h in range(GH):
                for t in range(3):
                    at = 4 * h + t
                    act.wait_ge(projected, at + 1)
                    if h >= 1:
                        act.wait_ge(convolved, 3 * (h - 1) + t + 1)
                        act.wait_ge(silued, h)
                    src = ps[:, 2 * (at % 3):2 * (at % 3) + 2, 0:H]
                    act.activation(pre[:, t, 3:3 + N].rearrange("p (h n) -> p h n", h=2), src, ACT.Copy)
                    act.activation(conv[:, t, :].rearrange("p (h n) -> p h n", h=2), src, ACT.Copy,
                                   scale=taps_w[:, h, t, 3:4]).then_inc(copied, 1)
                    if at + 2 < 4 * GH:
                        w.lead(act, at + 2)
                    if h >= 1 and t == 2:
                        norms(h - 1, 0)
                at = 4 * h + 3
                act.wait_ge(projected, at + 1)
                act.activation(v.gate[:, h, :].rearrange("p (h n) -> p h n", h=2),
                               ps[:, 2 * (at % 3):2 * (at % 3) + 2, 0:H], ACT.Silu).then_inc(copied, 1)
                if at + 2 < 4 * GH:
                    w.lead(act, at + 2)
                for t in range(3):
                    act.wait_ge(convolved, 3 * h + t + 1)
                    ins = act.activation(qkv[t][:, h, :], conv[:, t, :], ACT.Silu)
                ins.then_inc(silued, 1)
                if h >= 1:
                    norms(h - 1, 1)
                act.wait_ge(silued, h + 1)
                for t in range(2):
                    if h >= 1:
                        act.wait_ge(summed, 2 * (h - 1) + t + 1)
                    act.activation(sq[:, t, :], qkv[t][:, h, :], ACT.Square).then_inc(squared, 1)
            norms(GH - 1, 0), norms(GH - 1, 1)

        @block.gpsimd
        def _(pool):
            for u in range(4 * GH):
                w.rest(pool, u)

        @block.vector
        def _(dve):
            own = Steps(dve, dve_own)
            dve.memset(pre[:, :, 0:3], 0.0)
            dve.memset(v.rows[:, :], 0.0).then_inc(zeroed, 1)
            norm.dve(dve, g.xt, g.xn)
            dve.wait_ge(small_in, 80)
            dve.wait_ge(zeroed, 1)
            dve.wait_ge(ab_copied, 1)
            dve.scalar_tensor_tensor(soft[:, 1, :], soft[:, 0, :], -1.0, soft[:, 0, :], ALU.mult,
                                     ALU.max).then_inc(abs_done, 1)
            dve.wait_ge(exp_done, 1)
            log1p_of(own, dve, v.rows[0:GH, :], soft[:, 1, :], (soft[:, 2, :], soft[:, 3, :]))
            own.did(dve.scalar_tensor_tensor(soft[:, 1, :], soft[:, 0, :], 0.0, v.rows[0:GH, :], ALU.max, ALU.add))
            own.settle()
            own.did(dve.tensor_scalar(soft[:, 0, :], soft[:, 1, :], decay[:, 0:1], -1.0, ALU.mult, ALU.mult))
            own.did(dve.memset(soft[:, 2, 0:CH], 1.0))
            own.settle()
            for c in range(NCH):
                sl = slice(c * CH, (c + 1) * CH)
                dve.tensor_tensor_scan(v.rows[0:GH, sl], soft[:, 2, 0:CH], soft[:, 0, sl], 0.0, ALU.mult, ALU.add)
            dve.tensor_copy(v.rows[0:GH, T:N], soft[:, 0, T:N]).then_inc(cum_done, 1)

            def scale(h):
                for t in range(2):
                    dve.wait_ge(rooted, 2 * h + t + 1)
                    own.did(dve.reciprocal(rs[:, t, :], rs[:, t, :]))
                    own.settle()
                    x = qkv[t][:, h, :]
                    dve.scalar_tensor_tensor(x, x, CH ** -0.5 if t == 0 else 1.0, rs[:, t, :], ALU.mult,
                                             ALU.mult).then_inc(scaled, 1)

            for h in range(GH):
                for t in range(3):
                    dve.wait_ge(copied, 4 * h + t + 1)
                    x, u = pre[:, t, :], conv[:, t, :]
                    for j in (2, 1, 0):
                        w = taps_w[:, h, t, j:j + 1]
                        own.did(dve.scalar_tensor_tensor(u[:, 0:T], x[:, j:j + T], w, u[:, 0:T], ALU.mult, ALU.add))
                        own.did(dve.scalar_tensor_tensor(u[:, T:N], state[:, h, t, j, :], w, u[:, T:N],
                                                         ALU.mult, ALU.add))
                        own.settle()
                    dve.tensor_copy(last[:, h, t, :], x[:, T:T + 11]).then_inc(convolved, 1)
                if h >= 1:
                    scale(h - 1)
            scale(GH - 1)
            dve.wait_ge(turned, 1)
            own.did(dve.tensor_copy(v.cum_tok[:, :, :], ps[:, 0, 0:NCH * GH].rearrange("p (c h) -> p c h", c=NCH)))
            for i in range(2 * GH):
                k = i if i < GH else 32 + i - GH
                dve.tensor_copy(v.spread[:, i, :], g.ident[:, k:k + 1].to_broadcast([P, P]))


def gdn_chunks(nc, d, o, g, v):
    pe_steps = ["spread_g", "spread_b", "qk", "kk", "turn_l", "square0", "square_t0", "grow0", "square1", "square_t1",
                "grow1", "square2", "grow2", "pair0", "turn0", "join0", "pair1", "turn1", "join1", "pair2",
                "turn2", "join2", "turn_v", "k_state", "solve", "turn_k", "out", "update"]
    act_steps = ["exp_g", "exp_decay", "lower", "power0", "power_t0", "power1", "power_t1", "power2", "paired0", "inv0",
                 "paired1", "inv1", "paired2", "inv2", "v_tok", "u"]
    dve_steps = ["k", "k_beta", "v_beta", "decay", "q_exp", "k_exp", "attn", "lower_t", "strict", "power_t", "inv_t",
                 "power", "grown0", "grown1", "grown2", "mask0", "joined0", "mask1", "joined1", "mask2", "joined2",
                 "rhs", "k_left", "store_o", "decay_s", "add_s"]
    with ExitStack() as ctx:
        sc = Scope(nc, ctx, "gdnc")
        names = ("k", "exp_g", "decay", "k_beta", "q_exp", "k_exp", "v_beta", "lower_t", "attn", "lower", "power",
                 "power_t", "inv_t", "inv", "mask", "u", "rhs", "k_left")
        buf = {n: sc.sb(n, [P, 2, 4, CH]) for n in names}
        state = sc.sb("state", [P, 2, 4, CH])
        ps = sc.ps("ps", [P, 2, 4, 4, CH])
        pe_did = [sc.sem(f"pe_did{x}") for x in range(2)]
        act_did = [sc.sem(f"act_did{x}") for x in range(2)]
        dve_did = [sc.sem(f"dve_did{x}") for x in range(2)]
        cleared = sc.sem("cleared")
        stored = sc.sem("stored")
        block = ctx.enter_context(nc.Block())

        def after(eng, who, x, step, c):
            sem, steps = {"pe": (pe_did, pe_steps), "act": (act_did, act_steps), "dve": (dve_did, dve_steps)}[who]
            eng.wait_ge(sem[x], c * len(steps) + (steps.index(step) + 1 if step else 0))

        def chunk(t, x, c):
            return t[:, 4 * x:4 * x + 4, bass.ds(c * CH, CH)]

        def wide(col):
            return col.to_broadcast([P, 4, CH])

        def mask(m):
            return m.rearrange("p (o c) -> p o c", o=1).to_broadcast([P, 4, CH])

        @block.tensor
        def _(pe):
            pe.wait_ge(cleared, 1)

            def products(x, bank, lhs, rhs):
                for j in range(4):
                    mm = pe.matmul(ps[:, x, bank, j, :], lhs(j), rhs(j), start=True, stop=True)
                mm.then_inc(pe_did[x], 1)

            def turns(x, bank, src):
                for j in range(4):
                    mm = pe.transpose(ps[:, x, bank, j, :], src[:, x, j, :], g.ident)
                mm.then_inc(pe_did[x], 1)

            with pe.Fori(0, NCH) as c:
                cols = bass.ds(c * CH, CH)
                for x in range(2):
                    after(pe, "dve", x, None, c)
                    after(pe, "act", x, None, c)
                    products(x, 0, lambda j: v.spread[:, 4 * x + j, :], lambda j: v.rows[:, cols])
                    products(x, 1, lambda j: v.spread[:, GH + 4 * x + j, :], lambda j: v.rows[:, cols])
                for x in range(2):
                    after(pe, "dve", x, "k", c)
                    products(x, 3, lambda j: buf["k"][:, x, j, :], lambda j: flat(v.q[:, 4 * x + j:4 * x + j + 1, cols]))
                for x in range(2):
                    after(pe, "dve", x, "k_beta", c)
                    products(x, 2, lambda j: buf["k"][:, x, j, :], lambda j: buf["k_beta"][:, x, j, :])
                for x in range(2):
                    after(pe, "dve", x, "strict", c)
                    turns(x, 0, buf["lower_t"])
                for e in range(3):
                    for x in range(2):
                        if e == 0:
                            after(pe, "dve", x, "power", c)
                        else:
                            after(pe, "act", x, f"power_t{e - 1}", c)
                        products(x, 2, lambda j: buf["power_t"][:, x, j, :], lambda j: buf["power"][:, x, j, :])
                        if e < 2:
                            products(x, 3, lambda j: buf["power"][:, x, j, :], lambda j: buf["power_t"][:, x, j, :])
                    for x in range(2):
                        after(pe, "act", x, f"power{e}", c)
                        after(pe, "dve", x, "inv_t" if e == 0 else f"grown{e - 1}", c)
                        products(x, 1, lambda j: buf["power"][:, x, j, :], lambda j: buf["inv_t"][:, x, j, :])
                for m in range(3):
                    for x in range(2):
                        after(pe, "dve", x, "grown2" if m == 0 else f"joined{m - 1}", c)
                        after(pe, "dve", x, f"mask{m}", c)
                        products(x, 2, lambda j: buf["mask"][:, x, j, :], lambda j: buf["inv_t"][:, x, j, :])
                        turns(x, 3, buf["inv_t"])
                    for x in range(2):
                        after(pe, "act", x, f"inv{m}", c)
                        products(x, 1, lambda j: buf["inv"][:, x, j, :], lambda j: buf["u"][:, x, j, :])
                for x in range(2):
                    turns(x, 0, buf["v_beta"])
                    after(pe, "dve", x, "joined2", c)
                    products(x, 1, lambda j: buf["k_exp"][:, x, j, :], lambda j: state[:, x, j, :])
                for x in range(2):
                    after(pe, "dve", x, "rhs", c)
                    products(x, 2, lambda j: buf["inv_t"][:, x, j, :], lambda j: buf["rhs"][:, x, j, :])
                    turns(x, 0, buf["k"])
                for x in range(2):
                    after(pe, "act", x, "u", c)
                    for j in range(4):
                        pe.matmul(ps[:, x, 3, j, :], state[:, x, j, :], buf["q_exp"][:, x, j, :], start=True, stop=False)
                        mm = pe.matmul(ps[:, x, 3, j, :], buf["u"][:, x, j, :], buf["attn"][:, x, j, :],
                                       start=False, stop=True)
                    mm.then_inc(pe_did[x], 1)
                    after(pe, "dve", x, "k_left", c)
                    products(x, 1, lambda j: buf["k_left"][:, x, j, :], lambda j: buf["u"][:, x, j, :])

        @block.scalar
        def _(act):
            def run(x, out, src, func=ACT.Copy):
                act.activation(out, src, func).then_inc(act_did[x], 1)

            with act.Fori(0, NCH) as c:
                for x in range(2):
                    after(act, "dve", x, None, c)
                    after(act, "pe", x, "spread_g", c)
                    run(x, buf["exp_g"][:, x], ps[:, x, 0], ACT.Exp)
                for x in range(2):
                    after(act, "dve", x, "decay", c)
                    run(x, buf["decay"][:, x], buf["decay"][:, x], ACT.Exp)
                for x in range(2):
                    after(act, "pe", x, "turn_l", c)
                    run(x, buf["lower"][:, x], ps[:, x, 0])
                for e in range(3):
                    for x in range(2):
                        after(act, "pe", x, f"square_t{e}" if e < 2 else "square2", c)
                        run(x, buf["power"][:, x], ps[:, x, 2])
                        if e < 2:
                            run(x, buf["power_t"][:, x], ps[:, x, 3])
                for m in range(3):
                    for x in range(2):
                        after(act, "pe", x, f"pair{m}", c)
                        run(x, buf["u"][:, x], ps[:, x, 2])
                        after(act, "pe", x, f"turn{m}", c)
                        run(x, buf["inv"][:, x], ps[:, x, 3])
                for x in range(2):
                    after(act, "pe", x, "turn_v", c)
                    run(x, buf["rhs"][:, x], ps[:, x, 0])
                for x in range(2):
                    after(act, "pe", x, "solve", c)
                    run(x, buf["u"][:, x], ps[:, x, 2])

        @block.vector
        def _(dve):
            def tt(x, out, a, b, op=ALU.mult):
                dve.tensor_tensor(out, a, b, op).then_inc(dve_did[x], 1)

            dve.memset(state[:], 0.0).then_inc(cleared, 1)
            dve.wait_ge(cleared, 1)
            with dve.Fori(0, NCH) as c:
                for x in range(2):
                    after(dve, "pe", x, None, c)
                    dve.tensor_copy(buf["k"][:, x], chunk(v.k, x, c)).then_inc(dve_did[x], 1)
                for x in range(2):
                    after(dve, "pe", x, "spread_b", c)
                    after(dve, "dve", x, "k", c)
                    tt(x, buf["k_beta"][:, x], buf["k"][:, x], ps[:, x, 1])
                    tt(x, buf["v_beta"][:, x], chunk(v.v, x, c), ps[:, x, 1])
                    after(dve, "act", x, "exp_g", c)
                    for j in range(4):
                        at = v.cum_tok[:, bass.ds(c, 1), 4 * x + j:4 * x + j + 1].rearrange("p a b -> p (a b)")
                        ins = dve.scalar_tensor_tensor(buf["decay"][:, x, j, :], ps[:, x, 0, j, :], at,
                                                       g.neg_upper, ALU.subtract, ALU.add)
                    ins.then_inc(dve_did[x], 1)
                for x in range(2):
                    tt(x, buf["q_exp"][:, x], chunk(v.q, x, c), buf["exp_g"][:, x])
                    after(dve, "dve", x, "k_beta", c)
                    tt(x, buf["k_exp"][:, x], buf["k_beta"][:, x], buf["exp_g"][:, x])
                for x in range(2):
                    after(dve, "act", x, "exp_decay", c)
                    after(dve, "pe", x, "qk", c)
                    tt(x, buf["attn"][:, x], ps[:, x, 3], buf["decay"][:, x])
                    after(dve, "pe", x, "kk", c)
                    tt(x, buf["lower_t"][:, x], ps[:, x, 2], buf["decay"][:, x])
                for x in range(2):
                    after(dve, "dve", x, "lower_t", c)
                    tt(x, buf["lower_t"][:, x], buf["lower_t"][:, x], mask(g.strict_t))
                for x in range(2):
                    after(dve, "dve", x, "strict", c)
                    dve.scalar_tensor_tensor(buf["power_t"][:, x], buf["lower_t"][:, x], -1.0, mask(g.same16),
                                             ALU.mult, ALU.mult).then_inc(dve_did[x], 1)
                for x in range(2):
                    after(dve, "dve", x, "power_t", c)
                    tt(x, buf["inv_t"][:, x], buf["power_t"][:, x], mask(g.ident), ALU.add)
                for x in range(2):
                    after(dve, "act", x, "lower", c)
                    dve.scalar_tensor_tensor(buf["power"][:, x], buf["lower"][:, x], -1.0, mask(g.same16),
                                             ALU.mult, ALU.mult).then_inc(dve_did[x], 1)
                for e in range(3):
                    for x in range(2):
                        after(dve, "pe", x, f"grow{e}", c)
                        tt(x, buf["inv_t"][:, x], buf["inv_t"][:, x], ps[:, x, 1], ALU.add)
                for m, pair in enumerate((g.pair16, g.pair32, g.pair64)):
                    for x in range(2):
                        if m:
                            after(dve, "pe", x, f"pair{m - 1}", c)
                        tt(x, buf["mask"][:, x], buf["lower"][:, x], mask(pair))
                    for x in range(2):
                        after(dve, "pe", x, f"join{m}", c)
                        tt(x, buf["inv_t"][:, x], buf["inv_t"][:, x], ps[:, x, 1], ALU.subtract)
                for x in range(2):
                    after(dve, "act", x, "v_tok", c)
                    after(dve, "pe", x, "k_state", c)
                    tt(x, buf["rhs"][:, x], buf["rhs"][:, x], ps[:, x, 1], ALU.subtract)
                for x in range(2):
                    after(dve, "pe", x, "turn_k", c)
                    tt(x, buf["k_left"][:, x], ps[:, x, 0], wide(buf["decay"][:, x, :, CH - 1:CH]))
                for x in range(2):
                    after(dve, "pe", x, "out", c)
                    dve.tensor_copy(chunk(v.y, x, c), ps[:, x, 3]).then_inc(dve_did[x], 1)
                    tt(x, state[:, x], state[:, x], wide(buf["exp_g"][:, x, :, CH - 1:CH]))
                for x in range(2):
                    after(dve, "pe", x, "update", c)
                    after(dve, "dve", x, "decay_s", c)
                    tt(x, state[:, x], state[:, x], ps[:, x, 1], ALU.add)

        @block.sync
        def _(sp):
            for x in range(2):
                after(sp, "dve", x, None, NCH)
            sp.dma_start(o["gdn_state_p"], state[:]).then_inc(stored, 16)
            sp.wait_ge(stored, 16)


SQ = 16


def gdn_samples(nc, d, o, g, v):
    with ExitStack() as ctx:
        sc = Scope(nc, ctx, "gdns")
        pairs = GH * B
        state = sc.sb("state", [P, pairs, P])
        kq = sc.sb("kq", [P, pairs, 2])
        qk = sc.sb("qk", [P, pairs])
        eg, beta, u, t1, t2, dot = [sc.sb(n, [P, pairs]) for n in ("exp_g", "beta", "u", "t1", "t2", "dot")]
        k_t = sc.sb("k_t", [P, P])
        u_t = sc.sb("u_t", [pairs, P])
        spread_u = sc.sb("spread_u", [P, 2, SQ, P])
        ps = sc.ps("ps", [P, 8, 512])
        zeroed = sc.sem("zeroed")
        states_in = [sc.sem(f"states_in{k}") for k in range(4)]
        packed = sc.sem("packed")
        spread = sc.sem("spread")
        read = sc.sem("read")
        applied = sc.sem("applied")
        act_done = sc.sem("act_done")
        solved = sc.sem("solved")
        turned = sc.sem("turned")
        turned_copied = sc.sem("turned_copied")
        masked = sc.sem("masked")
        outer = sc.sem("outer")
        updated = sc.sem("updated")
        dve_own = sc.sem("dve_own")
        stored = sc.sem("stored")
        block = ctx.enter_context(nc.Block())

        def cols(t):
            return t[:, :, T:N]

        def by_head(t):
            return t.rearrange("p (h b) -> p h b", b=B)

        @block.sync
        def _(sp):
            for k in range(4):
                sl = slice(k * SQ, (k + 1) * SQ)
                sp.dma_start(state[:, sl], d["gdn_state"][:, sl]).then_inc(states_in[k], 16)
            for k in range(4):
                sp.wait_ge(updated, k + 1)
                sp.dma_start(o["gdn_state_s"][:, k * SQ:(k + 1) * SQ, :], state[:, k * SQ:(k + 1) * SQ, :]).then_inc(stored, 16)
            sp.wait_ge(stored, 64)

        @block.gpsimd
        def _(pool):
            pool.memset(k_t[pairs:, :], 0.0)
            pool.memset(spread_u[pairs:].rearrange("p a b c -> p (a b c)"), 0.0).then_inc(zeroed, 1)

        @block.tensor
        def _(pe):
            for h in range(GH):
                pe.matmul(ps[:, 0, B * h:B * h + B], v.spread[:, h, :], v.rows[:, T:N], start=True, stop=True)
            for h in range(GH):
                mm = pe.matmul(ps[:, 1, B * h:B * h + B], v.spread[:, GH + h, :], v.rows[:, T:N], start=True, stop=True)
            mm.then_inc(spread, 1)
            pe.wait_ge(packed, 2)
            pe.matmul(ps[:, 2, 0:pairs], g.ones, qk[:, :], start=True, stop=True).then_inc(spread, 1)
            pe.transpose(ps[0:pairs, 3, 0:P], kq[:, :, 0], g.ident).then_inc(turned, 1)
            for i in range(pairs):
                if i % SQ == 0:
                    pe.wait_ge(states_in[i // SQ], 16)
                mm = pe.matmul(ps[:, 4, 2 * i:2 * i + 2], state[:, i, :], kq[:, i, :], start=True, stop=True)
            mm.then_inc(applied, 1)
            pe.wait_ge(solved, 1)
            pe.transpose(ps[0:pairs, 5, 0:P], u[:, :], g.ident).then_inc(turned, 1)
            pe.wait_ge(zeroed, 1)
            for k in range(4):
                pe.wait_ge(masked, k + 1)
                pe.wait_ge(turned_copied, 2)
                if k:
                    pe.wait_ge(updated, k)
                for n in range(4):
                    mm = pe.matmul(ps[:, n, :], k_t[:, :],
                                   spread_u[:, k % 2, 4 * n:4 * n + 4, :].rearrange("p a c -> p (a c)"),
                                   start=True, stop=True)
                mm.then_inc(outer, 1)

        @block.scalar
        def _(act):
            act.wait_ge(spread, 1)
            act.activation(eg[:, :], ps[:, 0, 0:pairs], ACT.Exp)
            act.activation(beta[:, :], ps[:, 1, 0:pairs], ACT.Copy).then_inc(act_done, 1)
            act.wait_ge(turned, 1)
            act.activation(k_t[0:pairs, :], ps[0:pairs, 3, 0:P], ACT.Copy).then_inc(turned_copied, 1)
            act.wait_ge(turned, 2)
            act.activation(u_t[:, :], ps[0:pairs, 5, 0:P], ACT.Copy).then_inc(turned_copied, 1)

        @block.vector
        def _(dve):
            own = Steps(dve, dve_own)
            dve.tensor_copy(kq[:, :, 0].rearrange("p (h b) -> p h b", b=B), cols(v.k))
            dve.tensor_copy(kq[:, :, 1].rearrange("p (h b) -> p h b", b=B), cols(v.q)).then_inc(packed, 1)
            dve.tensor_tensor(by_head(qk[:, :]), cols(v.k), cols(v.q), ALU.mult).then_inc(packed, 1)
            dve.wait_ge(act_done, 1)
            dve.wait_ge(spread, 2)
            dve.wait_ge(applied, 1)
            ks, qs = [ps[:, 4, 0:2 * pairs].rearrange("p (i w) -> p i w", w=2)[:, :, w] for w in range(2)]
            own.did(dve.tensor_tensor(t1[:, :], ks, eg[:, :], ALU.mult))
            own.did(dve.tensor_tensor(t2[:, :], qs, eg[:, :], ALU.mult))
            own.settle()
            own.did(dve.tensor_tensor(by_head(t1[:, :]), cols(v.v), by_head(t1[:, :]), ALU.subtract))
            own.settle()
            dve.tensor_tensor(u[:, :], t1[:, :], beta[:, :], ALU.mult).then_inc(solved, 1)
            dve.wait_ge(solved, 1)
            own.did(dve.tensor_tensor(dot[:, :], u[:, :], ps[:, 2, 0:pairs], ALU.mult))
            own.settle()
            own.did(dve.tensor_tensor(cols(v.y), by_head(dot[:, :]), by_head(t2[:, :]), ALU.add))
            dve.wait_ge(turned_copied, 2)

            def spread_rows(k):
                if k >= 2:
                    dve.wait_ge(outer, k - 1)
                at = g.ident[0:pairs, k * SQ:(k + 1) * SQ].rearrange("p (i o) -> p i o", o=1).to_broadcast([pairs, SQ, P])
                rows = u_t[:, :].rearrange("p (o c) -> p o c", o=1).to_broadcast([pairs, SQ, P])
                dve.tensor_tensor(spread_u[0:pairs, k % 2], rows, at, ALU.mult).then_inc(masked, 1)

            spread_rows(0)
            for k in range(4):
                if k < 3:
                    spread_rows(k + 1)
                part = state[:, k * SQ:(k + 1) * SQ, :]
                own.did(dve.tensor_tensor(part, part, eg[:, k * SQ:(k + 1) * SQ].rearrange("p (i o) -> p i o", o=1)
                                          .to_broadcast([P, SQ, P]), ALU.mult))
                own.settle()
                dve.wait_ge(outer, k + 1)
                dve.tensor_tensor(part, part, ps[:, 0:4, :].rearrange("p a (b c) -> p (a b) c", c=P),
                                  ALU.add).then_inc(updated, 1)


def gdn_out(nc, d, o, g, v):
    with ExitStack() as ctx:
        sc = Scope(nc, ctx, "gdno")
        ps = sc.ps("ps", [P, 8, 512])
        w = Weights(sc, KT * P, 3, 3)
        y_hi, y_lo = [sc.sb(n, [P, KT, N], F32R) for n in ("y_hi", "y_lo")]
        proj = OutProjection(sc, ps, w, 0, y_hi, y_lo)
        sq = sc.sb("sq", [P, 3, N])
        to_row = sc.sb("to_row", [P, GH, GH])
        rows = sc.sb("rows", [P, N])
        made = sc.sem("made")
        squared = sc.sem("squared")
        summed = sc.sem("summed")
        rooted = sc.sem("rooted")
        inverted = sc.sem("inverted")
        spread = sc.sem("spread")
        scaled = sc.sem("scaled")
        dve_own = sc.sem("dve_own")
        block = ctx.enter_context(nc.Block())

        @block.sync
        def _(sp):
            proj.load(sp, d["gdn_w_out"])

        @block.tensor
        def _(pe):
            pe.wait_ge(made, 2)
            for h in range(GH):
                pe.wait_ge(squared, h + 1)
                for u in range(2):
                    mm = pe.matmul(ps[0:GH, u, 0:H], to_row[:, h, :], sq[:, h % 3, u * H:(u + 1) * H],
                                   start=(h == 0), stop=(h == GH - 1))
                mm.then_inc(summed, 1)
            pe.wait_ge(inverted, 1)
            for h in range(GH):
                if h >= 3:
                    pe.wait_ge(scaled, h - 2)
                for u in range(2):
                    mm = pe.matmul(ps[:, 2 + 2 * (h % 3) + u, 0:H], v.spread[:, h, :], rows[:, u * H:(u + 1) * H],
                                   start=True, stop=True)
                mm.then_inc(spread, 1)
            pe.wait_ge(scaled, GH - 1)
            proj.pe(pe, then=lambda: pe.wait_ge(scaled, GH))

        @block.scalar
        def _(act):
            for h in range(GH):
                if h >= 3:
                    act.wait_ge(summed, h - 2)
                act.activation(sq[:, h % 3, :], v.y[:, h, :], ACT.Square).then_inc(squared, 1)
            for u in range(2):
                w.lead(act, u)
            act.wait_ge(summed, GH)
            act.wait_ge(made, 2)
            act.activation(rows[0:GH, :].rearrange("p (h n) -> p h n", h=2), ps[0:GH, 0:2, 0:H], ACT.Sqrt,
                           bias=g.eps[0:GH, 0:1], scale=1.0 / P).then_inc(rooted, 1)
            w.lead(act, 2)
            for kt in range(GH):
                act.wait_ge(scaled, kt + 1)
                proj.lead(act, v.y, kt)
            proj.act(act)

        @block.gpsimd
        def _(pool):
            for u in range(KT):
                w.rest(pool, u)

        @block.vector
        def _(dve):
            own = Steps(dve, dve_own)
            flat_rows = to_row[:].rearrange("p a b -> p (a b)")
            dve.memset(rows[:, :], 0.0).then_inc(made, 1)
            own.did(dve.memset(flat_rows, 0.0))
            own.settle()
            dve.memset(flat_rows[:, 0:GH * GH:GH + 1], 1.0).then_inc(made, 1)
            dve.wait_ge(rooted, 1)
            dve.reciprocal(rows[0:GH, :], rows[0:GH, :]).then_inc(inverted, 1)
            for h in range(GH):
                dve.wait_ge(spread, h + 1)
                y = v.y[:, h, :]
                own.did(dve.scalar_tensor_tensor(halves(y), halves(y), v.norm_g[:, 0:1],
                                                 ps[:, 2 + 2 * (h % 3):4 + 2 * (h % 3), 0:H], ALU.mult, ALU.mult))
                own.settle()
                dve.tensor_tensor(y, y, v.gate[:, h, :], ALU.mult).then_inc(scaled, 1)
                if h:
                    proj.rest(dve, v.y, h - 1)
            proj.rest(dve, v.y, GH - 1)
            proj.dve(dve, g.xt)


def gdn_stage(nc, d, o, g):
    with ExitStack() as ctx:
        sc = Scope(nc, ctx, "gdn")
        v = Shared()
        v.q, v.k, v.v, v.gate = [sc.sb(n, [P, GH, N]) for n in ("q", "k", "v", "gate")]
        v.rows = sc.sb("rows", [P, N])
        v.cum_tok = sc.sb("cum_tok", [P, NCH, GH])
        v.spread = sc.sb("spread", [P, 2 * GH, P])
        v.norm_g = sc.sb("head_norm_g", [P, 1])
        v.y = g.xn
        gdn_project(nc, d, o, g, v)
        gdn_chunks(nc, d, o, g, v)
        gdn_samples(nc, d, o, g, v)
        gdn_out(nc, d, o, g, v)


def halves(ap):
    return ap.rearrange("p (h n) -> p h n", h=2)


def column(gr):
    return 8 * (gr % 2) + 4 * (gr // 2)


def nsa_project(nc, d, o, g, v, layer, j):
    with ExitStack() as ctx:
        sc = Scope(nc, ctx, f"nsap{j}")
        w_v = sc.sb("w_v", [P, KT, 560])
        rope = sc.sb("rope", [P, 2, N])
        turned = sc.sb("rope_part", [P, N])
        ps = sc.ps("ps", [P, 8, 512])
        norm = Norm(sc, g.norm_g[:, layer, :], ps, split=True,
                    parts=v.parts)
        w = Weights(sc, KT * P, 3, 2)
        small_in = sc.sem("small_in")
        w_v_in = sc.sem("w_v_in")
        zeroed = sc.sem("zeroed")
        projected = sc.sem("projected")
        copied = sc.sem("copied")
        swapped = sc.sem("swapped")
        added = sc.sem("added")
        rotated = sc.sem("rotated")
        kn_done = sc.sem("kn_done")
        dve_own = sc.sem("dve_own")
        stored = sc.sem("stored")
        block = ctx.enter_context(nc.Block())
        rotate = list(range(8)) + list(range(12, 16))

        @block.sync
        def _(sp):
            for u in range(16):
                w.load(sp, u, d["nsa_w_in"][j, u // 2, :, u % 2 * KT * P:(u % 2 + 1) * KT * P])
                if u == 2:
                    sp.dma_start(rope[:], d["rope"]).then_inc(small_in, 16)
                if u == 8:
                    sp.dma_start(w_v[:], d["nsa_w_v"][j]).then_inc(w_v_in, 16)
            sp.wait_ge(projected, 16)
            sp.dma_start(v.w_cmp[:], d["nsa_w_cmp"][j]).then_inc(stored, 16)
            sp.wait_ge(rotated, len(rotate))
            sp.wait_ge(copied, 21)
            sp.dma_start(o["nsa_kv"][j], v.kv[:]).then_inc(stored, 16)
            sp.dma_start(o["nsa_v"][j], v.vt[:]).then_inc(stored, 16)
            sp.dma_start(o["nsa_v_new"][j], v.vn[0:B, :]).then_inc(stored, 16)
            sp.wait_ge(stored, 64)

        def raw(i):
            return v.qu[:, i, :] if i < 8 else v.kv[:, i - 8, :]

        @block.tensor
        def _(pe):
            norm.pe(pe, g.ones)
            pe.wait_ge(norm.normed, KT)

            def swap(r):
                i = rotate[r]
                pe.wait_ge(copied, i + 1)
                if r:
                    pe.wait_ge(added, r)
                for h in range(2):
                    mm = pe.matmul(ps[:, 6 + h, 0:H], g.rope_swap, raw(i)[:, h * H:(h + 1) * H], start=True, stop=True)
                mm.then_inc(swapped, 1)

            for i in range(16):
                if i >= 3:
                    pe.wait_ge(copied, i - 2)
                w.project(pe, i, lambda h: ps[:, 2 * (i % 3) + h, 0:H], norm).then_inc(projected, 1)
                if i - 1 in rotate:
                    swap(rotate.index(i - 1))
            pe.wait_ge(w_v_in, 16)
            for tt in range(5):
                i = 16 + tt
                m = min(P, N - tt * P)
                pe.wait_ge(copied, i - 2)
                for kt in range(KT):
                    x = g.xn[:, kt, tt * P:tt * P + m]
                    pe.matmul(ps[0:m, 2 * (i % 3), :], x, w_v[:, kt, 0:512], start=(kt == 0), stop=(kt == KT - 1))
                    mm = pe.matmul(ps[0:m, 2 * (i % 3) + 1, 0:48], x, w_v[:, kt, 512:560], start=(kt == 0),
                                   stop=(kt == KT - 1))
                mm.then_inc(projected, 1)
                if tt == 0:
                    swap(len(rotate) - 1)

        @block.scalar
        def _(act):
            norm.act(act, g.xt, g.eps)
            w.lead(act, 0)
            norm.act_split(act, g.xn)
            w.lead(act, 1)
            act.wait_ge(zeroed, 1)
            for i in range(16):
                act.wait_ge(projected, i + 1)
                act.activation(halves(raw(i)), ps[:, 2 * (i % 3):2 * (i % 3) + 2, 0:H], ACT.Copy,
                               scale=0.125 if i < 8 else 1.0).then_inc(copied, 1)
                if i + 2 < 16:
                    w.lead(act, i + 2)
            for tt in range(5):
                i = 16 + tt
                m = min(P, N - tt * P)
                act.wait_ge(projected, i + 1)
                act.activation(v.vt[:, tt, :] if tt < 4 else v.vn[0:B, :], ps[0:m, 2 * (i % 3), :], ACT.Copy)
                act.activation(v.gate[:, tt, :] if tt < 4 else v.gate_new[0:B, :], ps[0:m, 2 * (i % 3) + 1, 0:48],
                               ACT.Sigmoid).then_inc(copied, 1)

        @block.gpsimd
        def _(pool):
            for u in range(16):
                w.rest(pool, u)

        @block.vector
        def _(dve):
            own = Steps(dve, dve_own)
            dve.memset(v.vn[:, :], 0.0)
            dve.memset(v.kn[:, :, :], 0.0).then_inc(zeroed, 1)
            norm.dve(dve, g.xt, g.xn)
            dve.wait_ge(small_in, 16)
            dve.wait_ge(zeroed, 1)
            for r, i in enumerate(rotate):
                dve.wait_ge(swapped, r + 1)
                out = v.qr[:, i, :] if i < 8 else raw(i)
                dve.tensor_tensor(halves(turned[:, :]), ps[:, 6:8, 0:H], halves(rope[:, 1, :]), ALU.mult).then_inc(added, 1)
                own.did(dve.tensor_tensor(out, raw(i), rope[:, 0, :], ALU.mult))
                own.settle()
                dve.wait_ge(added, r + 1)
                dve.tensor_tensor(out, out, turned[:, :], ALU.add).then_inc(rotated, 1)
                dve.wait_ge(rotated, r + 1)
                if i >= 12:
                    dve.tensor_copy(v.kn[:, i - 12, 0:B], raw(i)[:, T:N])


def nsa_compress(nc, d, o, g, v, j):
    with ExitStack() as ctx:
        sc = Scope(nc, ctx, f"nsac{j}")
        w = v.w_cmp
        table = sc.sb("table", [1, B * PAGES], I32)
        pages = sc.sb("pages", [P, 69, 256])
        slots = (pages[:, 0:37], pages[:, 37:69])
        free = g.xn[:].rearrange("p t n -> p (t n)")
        cmp_s = v.drop[:].rearrange("p t n -> p (t n)").rearrange("p (k n) -> p k n", k=4)
        v_tok = free[0:NCMP, KT * N - B * 2 * P:].rearrange("p (b t n) -> p b t n", b=B, t=2)
        halves_of = free[0:16, 0:PAGES * 2 * 64].rearrange("p (t h n) -> p t h n", t=PAGES, h=2)
        drop_t, prob_t, st = [free[0:r, at * P:(at + 1) * P] for r, at in ((16, 8), (NCMP, 9), (NCMP, 10))]
        at = 11 * P
        imp, equal, drop = [free[:, at + 16 * k:at + 16 * k + 16] for k in range(3)]
        bias, prob = free[:, at + 48:at + 52], free[:, at + 64:at + 64 + NCMP]
        nmax, total, least, last_eq = [free[:, at + 52 + k:at + 53 + k] for k in range(4)]
        pe_in = free[:, at + P:at + P + 64].rearrange("p (k l) -> p k l", k=2)
        ps = sc.ps("ps", [P, 8, 512])
        w_loaded = sc.sem("w_loaded")
        table_in = sc.sem("table_in")
        pages_in = [[sc.sem(f"pages_in{s}_{w}") for w in ("sp", "pool", "act")] for s in range(2)]
        permuted = sc.sem("permuted")
        bias_done = sc.sem("bias_done")
        unit_done = sc.sem("unit_done")
        unit_copied = sc.sem("unit_copied")
        pe_step = sc.sem("pe_step")
        act_step = sc.sem("act_step")
        dve_own = sc.sem("dve_own")
        normed = sc.sem("normed")
        dropped = sc.sem("dropped")
        expanded = sc.sem("expanded")
        c_exped = sc.sem("c_exped")
        block = ctx.enter_context(nc.Block())

        def page_loads(eng, which, u):
            lo, hi = ((0, 12), (12, 20), (20, 32))[which]
            if u >= 2:
                eng.wait_ge(unit_done, u - 1)
            kv, quad = u // 2, u % 2
            slot = slots[u % 2]
            with eng.Fori(lo // 4, hi // 4) as i:
                for k in range(4):
                    page = eng.value_load(table[0:1, bass.ds(i * 4 + (quad * 32 + k), 1)], min_val=0, max_val=N_PHYS - 1)
                    eng.dma_start(flat(slot[:, bass.ds(i * 4 + k, 1), :]),
                                  flat(d["cmp_pages"][j, bass.ds(page, 1), :, kv * 256:(kv + 1) * 256]
                                       .rearrange("o p n -> p o n"))).then_inc(pages_in[u % 2][which], 16)

        @block.sync
        def _(sp):
            sp.dma_start(table[:], d["page_table"]).then_inc(table_in, 16)
            sp.dma_start(pe_in, d["nsa_pe"][j]).then_inc(w_loaded, 16)
            sp.wait_ge(table_in, 16)
            for u in range(4):
                page_loads(sp, 0, u)

        @block.gpsimd
        def _(pool):
            pool.wait_ge(table_in, 16)
            for u in range(4):
                page_loads(pool, 1, u)

        @block.tensor
        def _(pe):
            pe.wait_ge(w_loaded, 16)
            for u in range(4):
                kv = u // 2
                for which, n in enumerate((12, 8, 12)):
                    pe.wait_ge(pages_in[u % 2][which], 16 * n * (u // 2 + 1))
                if u >= 2:
                    pe.wait_ge(unit_copied, u - 1)
                if u % 2 == 0:
                    pe.wait_ge(permuted, u // 2 + 1)
                cols = slots[u % 2].shape[1] * 4
                for gp in range(2):
                    for l in range(32):
                        at = gp * 128 + l * 4
                        rhs = slots[u % 2][:, :, at:at + 4]
                        mm = pe.matmul(ps[:, 1 + u % 2, gp * 256:gp * 256 + cols], w[:, kv, l, :], rhs,
                                       start=(l == 0), stop=(l == 31))
                mm.then_inc(unit_done, 1)
            pe.wait_ge(unit_copied, 4)
            for gp in range(2):
                pe.transpose(ps[0:PCMP, 3, gp * P:(gp + 1) * P], v.cmp_p[:, 2 + gp, :], g.ident)
            for b in range(B):
                for gp in range(2):
                    mm = pe.transpose(ps[0:NCMP, 4 + b // 2, (b % 2 * 2 + gp) * P:(b % 2 * 2 + gp + 1) * P],
                                      cmp_s[:, 2 + gp, b * NCMP:(b + 1) * NCMP], g.ident)
            mm.then_inc(pe_step, 1)
            for b in range(B):
                for gr in range(4):
                    gp, lo = gr // 2, 64 * (gr % 2)
                    at = b * 8 + 4 * gp
                    mm = pe.matmul(ps[0:NCMP, 2 * (gr % 2), at:at + 4],
                                   cmp_s[lo:lo + 64, gp, b * NCMP:(b + 1) * NCMP],
                                   v.qu[lo:lo + 64, 4 * gp:4 * gp + 4, T + b], start=True, stop=True)
            mm.then_inc(pe_step, 1)
            pe.wait_ge(act_step, 2)
            pe.transpose(ps[:, 1, 0:NCMP], st[:, :], g.ident[0:NCMP, 0:NCMP]).then_inc(pe_step, 1)
            pe.wait_ge(normed, 1)
            pe.transpose(ps[0:NCMP, 2, 0:P], prob[:, :], g.ident).then_inc(pe_step, 1)
            pe.matmul(ps[:, 0, 0:NCMP], g.four_sum, prob[:, :], start=True, stop=True).then_inc(pe_step, 1)
            pe.wait_ge(act_step, 3)
            for b in range(B):
                for gr in range(4):
                    gp, lo = gr // 2, 64 * (gr % 2)
                    mm = pe.matmul(ps[lo:lo + 64, 3, b * 8 + 4 * gp:b * 8 + 4 * gp + 4],
                                   v_tok[:, b, gp, lo:lo + 64],
                                   prob_t[:, b * 16 + column(gr):b * 16 + column(gr) + 4],
                                   start=True, stop=True)
            mm.then_inc(pe_step, 1)
            pe.wait_ge(dropped, 1)
            pe.transpose(ps[0:16, 1, 0:P], drop[:, :], g.ident).then_inc(pe_step, 1)
            pe.wait_ge(act_step, 5)
            pe.wait_ge(expanded, 1)
            for t in range(PAGES):
                mm = pe.matmul(ps[:, 4 + t // 4, t % 4 * P:(t % 4 + 1) * P],
                               halves_of[:, t].rearrange("p h n -> p (h n)"), drop_t[:, :], start=True, stop=True)
            mm.then_inc(pe_step, 1)

        @block.scalar
        def _(act):
            act.wait_ge(table_in, 16)
            for u in range(2):
                page_loads(act, 2, u)
            for u in range(4):
                kv, quad = u // 2, u % 2
                act.wait_ge(unit_done, u + 1)
                if quad == 0:
                    for gp in range(2):
                        k = 2 * kv + gp
                        ins = act.activation(bias[:, k:k + 1], ps[:, 1, gp * 256 + P + PCMP:gp * 256 + P + PCMP + 1],
                                             ACT.Copy)
                    ins.then_inc(bias_done, 1)
                    act.wait_ge(bias_done, kv + 1)
                    for gp in range(2):
                        k = 2 * kv + gp
                        act.activation(v.cmp_p[:, k, :], ps[:, 1, gp * 256 + P:gp * 256 + P + PCMP], ACT.Identity,
                                       bias=bias[:, k:k + 1])
                for gp in range(2):
                    k = 2 * kv + gp
                    ins = act.activation(cmp_s[:, k, quad * P:(quad + 1) * P], ps[:, 1 + u % 2, gp * 256:gp * 256 + P],
                                         ACT.Identity, bias=bias[:, k:k + 1])
                ins.then_inc(unit_copied, 1)
                if u < 2:
                    page_loads(act, 2, u + 2)
            act.wait_ge(pe_step, 1)
            act.activation(v.cmp_v[:, :, :].rearrange("p a n -> p (a n)"), ps[0:PCMP, 3, 0:2 * P], ACT.Copy)
            act.activation(v_tok[:, :, :, :].rearrange("p (q b) g n -> p q (b g n)", q=4), ps[0:NCMP, 4:8, :],
                           ACT.Copy).then_inc(act_step, 1)
            act.wait_ge(pe_step, 2)
            act.activation(st[:, :].rearrange("p (b a h) -> p a b h", a=2, h=8),
                           ps[0:NCMP, 0:4:2, 0:64].rearrange("p a (b h) -> p a b h", h=8), ACT.Copy).then_inc(act_step, 1)
            act.wait_ge(dve_own, 1)
            act.activation(prob[:, :], ps[:, 1, 0:NCMP], ACT.Exp, bias=nmax[:, 0:1],
                           accum_out=total[:, 0:1]).then_inc(c_exped, 1)
            act.wait_ge(pe_step, 4)
            act.activation(prob_t[:, :], ps[0:NCMP, 2, 0:P], ACT.Copy).then_inc(act_step, 1)
            act.wait_ge(pe_step, 6)
            act.activation(v.out_c[:, :, :].rearrange("p b t -> p (b t)"), ps[:, 3, 0:64], ACT.Copy).then_inc(act_step, 1)
            act.wait_ge(pe_step, 7)
            act.activation(drop_t[:, :], ps[0:16, 1, 0:P], ACT.Copy).then_inc(act_step, 1)
            act.wait_ge(pe_step, 8)
            act.activation(v.drop[:, :, :].rearrange("p (a b) n -> p a (b n)", a=2), ps[:, 4:6, :], ACT.Copy)

        @block.vector
        def _(dve):
            own = Steps(dve, dve_own)
            dve.wait_ge(w_loaded, 16)
            for kv in range(2):
                if kv:
                    dve.wait_ge(unit_done, 1)
                for gp in range(2):
                    part = slice(gp * P, (gp + 1) * P)
                    dve.tensor_copy(slots[0][:, 32:36, part].rearrange("p t (l c) -> p t l c", c=4),
                                    v.kv[:, 2 * kv + gp, 0:T].rearrange("p (t c l) -> p t l c", t=4, c=4))
                    ins = dve.tensor_copy(slots[0][:, 36, part].rearrange("p (l c) -> p l c", c=4),
                                          pe_in[:, kv, :].rearrange("p (l o) -> p l o", o=1).to_broadcast([P, 32, 4]))
                ins.then_inc(permuted, 1)
            dve.tensor_copy(halves_of[:].rearrange("p t h n -> p (t h) n"),
                            g.ident[0:16, 0:16].rearrange("p (a o) -> p a o", o=1).to_broadcast([16, 16, 64])).then_inc(expanded, 1)
            dve.wait_ge(pe_step, 3)
            own.did(dve.tensor_reduce(nmax[:, 0:1], ps[:, 1, 0:NCMP], AX, ALU.max, negate=True))
            dve.wait_ge(c_exped, 1)
            own.did(dve.reciprocal(total[:, 0:1], total[:, 0:1]))
            own.settle()
            dve.tensor_scalar(prob[:, :], prob[:, :], total[:, 0:1], None, ALU.mult).then_inc(normed, 1)
            dve.wait_ge(pe_step, 5)
            own.did(dve.tensor_reduce(imp[:, :], ps[:, 0, 0:NCMP].rearrange("p (a b) -> p a b", b=2), AX, ALU.add))
            own.settle()
            own.did(dve.tensor_reduce(least[:, 0:1], imp[:, 1:16], AX, ALU.min))
            own.settle()
            own.did(dve.scalar_tensor_tensor(equal[:, 1:16], imp[:, 1:16], least[:, 0:1], g.block_no[:, 1:16],
                                             ALU.is_equal, ALU.mult))
            own.settle()
            own.did(dve.tensor_reduce(last_eq[:, 0:1], equal[:, 1:16], AX, ALU.max))
            own.settle()
            dve.tensor_scalar(drop[:, :], g.block_no, last_eq[:, 0:1], NEG, ALU.is_equal, ALU.mult).then_inc(dropped, 1)


NT = PAGES + 1 + 4 + 1


def nsa_samples(nc, d, o, g, v, j):
    with ExitStack() as ctx:
        sc = Scope(nc, ctx, f"nsas{j}")
        table = sc.sb("table", [1, B * PAGES], I32)
        pages = sc.sb("pages", [P, 3, PAGES, 512])
        win = sc.sb("win", [P, 3, 2048])
        s = sc.sb("scores", [P, 2, NT, 16])
        pmax = sc.sb("pmax", [P, 2, 2, 16])
        m32 = sc.sb("m32", [32, 2])
        diag = sc.sb("diag", [32, 2, 32])
        psum_p = sc.sb("part_sums", [P, 2, 2, 16])
        inv = sc.sb("inv", [P, B, 3, 16])
        out = sc.sb("out", [P, B, 3, 8])
        rows = sc.sb("rows", [B, B, P])
        acc = sc.sb("acc", [P, 3, B, 8])
        q_pair = sc.sb("q_pair", [P, B, 2, 2, 4])
        ps = sc.ps("ps", [P, 8, 512])
        table_in = sc.sem("table_in")
        kv_in = [sc.sem(f"kv_in{x}") for x in range(3)]
        win_stored = [sc.sem(f"win_stored{x}") for x in range(3)]
        rows_done = sc.sem("rows_done")
        paired = sc.sem("paired")
        gates_done = sc.sem("gates_done")
        gates_copied = sc.sem("gates_copied")
        scored = sc.sem("scored")
        part_max = sc.sem("part_max")
        turned = sc.sem("turned")
        diagonal = sc.sem("diagonal")
        max_spread = sc.sem("max_spread")
        shifted = sc.sem("shifted")
        exped = sc.sem("exped")
        summed = sc.sem("summed")
        sum_spread = sc.sem("sum_spread")
        inverted = sc.sem("inverted")
        valued = sc.sem("valued")
        out_copied = sc.sem("out_copied")
        dve_own = sc.sem("dve_own")
        block = ctx.enter_context(nc.Block())

        @block.sync
        def _(sp):
            sp.dma_start(table[:], d["page_table"]).then_inc(table_in, 16)
            sp.wait_ge(table_in, 16)
            for b in range(B):
                x = b % 3
                if b >= 3:
                    sp.wait_ge(valued, b - 2)
                    sp.wait_ge(win_stored[x], 16 * (b // 3))
                with sp.Fori(0, PAGES // 4) as i:
                    for k in range(4):
                        page = sp.value_load(table[0:1, bass.ds(i * 4 + (b * PAGES + k), 1)], min_val=0, max_val=N_PHYS - 1)
                        sp.dma_start(flat(pages[:, x, bass.ds(i * 4 + k, 1), :]),
                                     flat(d["sel_pages"][j, bass.ds(page, 1)].rearrange("o p n -> p o n"))).then_inc(kv_in[x], 16)
                sp.dma_start(win[:, x], d["win_state"][j, b]).then_inc(kv_in[x], 16)

        @block.gpsimd
        def _(pool):
            for b in range(B):
                pool.wait_ge(kv_in[b % 3], 144 * (b // 3 + 1))
                pool.dma_start(o["win_kept"][j, b], win[:, b % 3]).then_inc(win_stored[b % 3], 16)
            for x in range(3):
                pool.wait_ge(win_stored[x], 16 * len(range(x, B, 3)))

        @block.tensor
        def _(pe):
            pe.wait_ge(rows_done, 1)
            for b in range(B):
                mm = pe.matmul(ps[:, 7, b * 48:b * 48 + 48], rows[:, b, :], v.gate_new[0:B, :], start=True, stop=True)
            mm.then_inc(gates_done, 1)

            def scores(b):
                x, y = b % 2, b % 3
                pe.wait_ge(kv_in[y], 144 * (b // 3 + 1))
                if b >= 2:
                    pe.wait_ge(part_max, b - 1)
                for t in range(NT):
                    for gp in range(2):
                        if t < PAGES:
                            keys = pages[:, y, t, gp * P:(gp + 1) * P]
                        elif t == PAGES:
                            keys = v.kn[:, gp, :]
                        elif t < NT - 1:
                            at = gp * 512 + (t - PAGES - 1) * P
                            keys = win[:, y, at:at + P]
                        else:
                            keys = v.kn[:, 2 + gp, :]
                        out_cols = ps[:, x, 16 * t:16 * t + 16].rearrange("p (a g h) -> p a g h", a=2, g=2)[:, :, gp]
                        mm = pe.matmul(out_cols, keys, q_pair[:, b, gp], start=True, stop=True)
                mm.then_inc(scored, 1)

            def values(b):
                x, y = b % 2, b % 3
                for br, tiles in ((1, range(0, PAGES + 1)), (2, range(PAGES + 1, NT))):
                    for gr in range(4):
                        gp, lo = gr // 2, 64 * (gr % 2)
                        for t in tiles:
                            if t < PAGES:
                                val = pages[:, y, t, 256 + 64 * gr:320 + 64 * gr]
                            elif t == PAGES:
                                val = v.vn[:, 64 * gr:64 * gr + 64]
                            elif t < NT - 1:
                                at = 1024 + (t - PAGES - 1) * 256 + 64 * gr
                                val = win[:, y, at:at + 64]
                            else:
                                val = v.vn[:, 256 + 64 * gr:320 + 64 * gr]
                            at = 8 * (br - 1) + 4 * gp
                            mm = pe.matmul(ps[lo:lo + 64, 7, at:at + 4], val, s[:, x, t, column(gr):column(gr) + 4],
                                           start=(t == tiles[0]), stop=(t == tiles[-1]))
                mm.then_inc(valued, 1)

            pe.wait_ge(paired, 1)
            scores(0)
            for b in range(B):
                x = b % 2
                pe.wait_ge(part_max, b + 1)
                if b:
                    pe.wait_ge(diagonal, b)
                pe.transpose(ps[0:32, 4, 0:P], pmax[:, x].rearrange("p a h -> p (a h)"), g.ident).then_inc(turned, 1)
                if b < B - 1:
                    scores(b + 1)
                pe.wait_ge(diagonal, b + 1)
                if b:
                    pe.wait_ge(shifted, b)
                pe.matmul(ps[:, 5, 0:32], g.ones[0:32, :], diag[:, x, :], start=True, stop=True).then_inc(max_spread, 1)
                pe.wait_ge(summed, b + 1)
                if b:
                    pe.wait_ge(inverted, b)
                pe.matmul(ps[:, 6, 0:32], g.ones, psum_p[:, x].rearrange("p a h -> p (a h)"), start=True,
                          stop=True).then_inc(sum_spread, 1)
                if b:
                    pe.wait_ge(out_copied, b)
                else:
                    pe.wait_ge(gates_copied, 1)
                values(b)

        @block.scalar
        def _(act):
            act.wait_ge(gates_done, 1)
            act.activation(inv[:].rearrange("p b r h -> p (b r h)"), ps[:, 7, 0:B * 48], ACT.Copy).then_inc(gates_copied, 1)
            for b in range(B):
                x = b % 2
                act.wait_ge(shifted, b + 1)
                act.activation(s[:, x], s[:, x], ACT.Exp).then_inc(exped, 1)
                act.wait_ge(valued, b + 1)
                act.activation(out[:, b, 1:3, :], ps[:, 7, 0:16].rearrange("p (r t) -> p r t", r=2),
                               ACT.Copy).then_inc(out_copied, 1)

        @block.vector
        def _(dve):
            own = Steps(dve, dve_own)
            dve.tensor_copy(rows[:], g.ident[0:B, 0:B].rearrange("p (a o) -> p a o", o=1).to_broadcast([B, B, P])).then_inc(rows_done, 1)
            dve.tensor_copy(out[:, :, 0, :], v.out_c[:, :, :])
            own.did(dve.memset(q_pair[:].rearrange("p b g a h -> p (b g a h)"), 0.0))
            own.settle()
            for g2 in range(2):
                half = slice(64 * g2, 64 * g2 + 64)
                for gp in range(2):
                    ins = dve.tensor_copy(q_pair[half, :, gp, g2, :],
                                          v.qr[half, 4 * gp:4 * gp + 4, T:N].rearrange("p h b -> p b h"))
            ins.then_inc(paired, 1)
            parts = (slice(0, PAGES + 1), slice(PAGES + 1, NT))

            def by_key(ap):
                return ap.rearrange("p t h -> p h t")

            def first(b):
                x = b % 2
                dve.wait_ge(scored, b + 1)
                if b >= 2:
                    dve.wait_ge(valued, b - 1)
                src = ps[:, x, 0:16 * NT].rearrange("p (t h) -> p t h", h=16)
                drop = v.drop[:, :, b * 16:b * 16 + 16]
                own.did(dve.tensor_tensor(s[:, x, 0:PAGES], src[:, 0:PAGES], drop, ALU.add))
                for t in (PAGES, NT - 1):
                    own.did(dve.tensor_scalar(s[:, x, t], src[:, t], g.new_mask[:, b:b + 1], None, ALU.add))
                own.did(dve.tensor_copy(s[:, x, PAGES + 1:NT - 1], src[:, PAGES + 1:NT - 1]))
                own.settle()
                for k, part in enumerate(parts):
                    ins = dve.tensor_reduce(pmax[:, x, k, :], by_key(s[:, x, part]), AX, ALU.max)
                ins.then_inc(part_max, 1)

            first(0)
            for b in range(B):
                x = b % 2
                dve.wait_ge(turned, b + 1)
                own.did(dve.tensor_reduce(m32[:, x:x + 1], ps[0:32, 4, 0:P], AX, ALU.max))
                own.settle()
                dve.tensor_scalar(diag[:, x, :], g.ident[0:32, 0:32], m32[:, x:x + 1], None, ALU.mult).then_inc(diagonal, 1)
                if b < B - 1:
                    first(b + 1)
                dve.wait_ge(max_spread, b + 1)
                for k, part in enumerate(parts):
                    n = part.stop - part.start
                    m = ps[:, 5, 16 * k:16 * k + 16].rearrange("p (o h) -> p o h", o=1).to_broadcast([P, n, 16])
                    ins = dve.tensor_tensor(s[:, x, part], s[:, x, part], m, ALU.subtract)
                ins.then_inc(shifted, 1)
                dve.wait_ge(exped, b + 1)
                for k, part in enumerate(parts):
                    ins = dve.tensor_reduce(psum_p[:, x, k, :], by_key(s[:, x, part]), AX, ALU.add)
                ins.then_inc(summed, 1)
                dve.wait_ge(sum_spread, b + 1)
                dve.reciprocal(pmax[:, x].rearrange("p a h -> p (a h)"), ps[:, 6, 0:32]).then_inc(inverted, 1)
                dve.wait_ge(inverted, b + 1)
                dve.wait_ge(gates_copied, 1)
                own.did(dve.tensor_tensor(inv[:, b, 1:3, :], inv[:, b, 1:3, :], pmax[:, x], ALU.mult))
            dve.wait_ge(out_copied, B)
            own.settle()
            for br in range(3):
                for gr in range(4):
                    gp, lo = gr // 2, 64 * (gr % 2)
                    half = slice(lo, lo + 64)
                    own.did(dve.tensor_tensor(acc[half, br, :, 4 * gp:4 * gp + 4], out[half, :, br, 4 * gp:4 * gp + 4],
                                              inv[half, :, br, column(gr):column(gr) + 4], ALU.mult))
            own.settle()
            own.did(dve.tensor_tensor(acc[:, 0], acc[:, 0], acc[:, 1], ALU.add))
            own.settle()
            dve.tensor_tensor(v.y[:, :, T:N].rearrange("p t b -> p b t"), acc[:, 0], acc[:, 2], ALU.add)


def nsa_prompt(nc, d, o, g, v, j):
    units = [(i, hh) for i in range(NCH) for hh in range(HEADS)]
    last = len(units)
    with ExitStack() as ctx:
        sc = Scope(nc, ctx, f"nsaq{j}")
        ident16 = sc.sb("ident16", [P, P], BF16)
        causal16 = sc.sb("causal16", [P, P], BF16)
        q_pad = sc.sb("q_pad", [P, 2, HEADS, P])
        prob = sc.sb("prob", [P, 4, 512])
        prob_t = sc.sb("prob_t", [P, 4, 512])
        nmax = sc.sb("neg_max", [P, 4])
        total = sc.sb("total", [P, 4])
        factor = sc.sb("factor", [P, 2, 2])
        keys_c = sc.sb("keys_c", [P, 2, 2, PCMP])
        pc = sc.sb("prob_c", [P, NCH, HEADS, PCMP])
        pct = sc.sb("prob_c_t", [P, NCH, 2, P])
        stat = sc.sb("stat", [P, 2, NCH, HEADS])
        repeat = sc.sb("repeat", [PCMP, KT, PCMP])
        values_c = sc.sb("values_c", [P, 2, KT, 64])
        ps = sc.ps("ps", [P, 8, 512])
        w = Weights(sc, KT * P, 3, 2)
        y_lo = sc.sb("y_lo", [P, KT, N], F32R)
        proj = OutProjection(sc, ps, w, 0, v.y_hi, y_lo)
        masks = sc.sem("masks")
        zeroed = sc.sem("zeroed")
        padded = sc.sem("padded")
        c_made = sc.sem("c_made")
        c_repeated = sc.sem("c_repeated")
        c_scored = sc.sem("c_scored")
        c_shifted = sc.sem("c_shifted")
        c_exped = sc.sem("c_exped")
        c_scaled = sc.sem("c_scaled")
        c_turned = sc.sem("c_turned")
        c_copied = sc.sem("c_copied")
        scored = sc.sem("scored")
        maxed = sc.sem("maxed")
        exped = sc.sem("exped")
        scaled = sc.sem("scaled")
        turned = sc.sem("turned")
        copied_t = sc.sem("copied_t")
        copied_w = sc.sem("copied_w")
        valued = sc.sem("valued")
        out_copied = sc.sem("out_copied")
        dve_own = sc.sem("dve_own")
        block = ctx.enter_context(nc.Block())

        @block.sync
        def _(sp):
            proj.load(sp, d["nsa_w_out"][j])

        @block.gpsimd
        def _(pool):
            for i in range(NCH):
                if i:
                    pool.wait_ge(padded, i)
                if i < 2:
                    pool.memset(q_pad[:, i], 0.0).then_inc(zeroed, 1)
                    pool.wait_ge(zeroed, i + 1)
                if i >= 2:
                    pool.wait_ge(scored, 2 * HEADS * (i - 1))
                for g2 in range(2):
                    half = slice(64 * g2, 64 * g2 + 64)
                    ins = pool.tensor_copy(q_pad[half, i % 2, g2::2, :], v.qr[half, :, i * P:(i + 1) * P])
                ins.then_inc(padded, 1)
            pool.wait_ge(padded, NCH)
            for u in range(KT):
                w.rest(pool, u)

        @block.tensor
        def _(pe):
            pe.wait_ge(c_made, 1)
            pe.matmul(ps[:, 6, 0:2 * P], repeat[:].rearrange("p a c -> p (a c)"),
                      v.cmp_v[:, :, :].rearrange("p a n -> p (a n)"), start=True, stop=True).then_inc(c_repeated, 1)
            for i in range(NCH):
                for t in range(KT):
                    mm = pe.matmul(ps[:, i, t * 32:(t + 1) * 32], v.qu[:, t, i * P:(i + 1) * P],
                                   keys_c[:, t // 4].rearrange("p a c -> p (a c)"), start=True, stop=True)
            mm.then_inc(c_scored, 1)
            pe.wait_ge(c_scaled, 1)
            for i in range(NCH):
                for k in range(2):
                    mm = pe.transpose(ps[:, 4 + i // 2, (i % 2 * 2 + k) * P:(i % 2 * 2 + k + 1) * P],
                                      pc[:, i, 8 * k:8 * k + 8, :].rearrange("p h c -> p (h c)"), g.ident)
            mm.then_inc(c_turned, 1)

            def scores(n):
                i, hh = units[n]
                pe.wait_ge(padded, i + 1)
                for br in range(2):
                    k = 2 * n + br
                    if k >= 4:
                        pe.wait_ge(exped, k - 3)
                    pe.matmul(ps[:, k % 4, 0:(i + 1) * P], q_pad[:, i % 2, hh, :],
                              v.kv[:, 4 + 2 * br + hh // 8, 0:(i + 1) * P], start=True, stop=False)
                    pe.matmul(ps[:, k % 4, i * P:(i + 1) * P], ident16[:, :], causal16[:, :], start=False,
                              stop=True).then_inc(scored, 1)

            def turn(n):
                i, hh = units[n]
                for br in range(2):
                    k = 2 * n + br
                    pe.wait_ge(scaled, k + 1)
                    if n >= 1:
                        pe.wait_ge(copied_w if br else copied_t, n)
                    for kt in range(i + 1):
                        mm = pe.transpose(ps[:, 4 + br, kt * P:(kt + 1) * P], prob[:, k % 4, kt * P:(kt + 1) * P], g.ident)
                    mm.then_inc(turned, 1)

            def values(n):
                i, hh = units[n]
                t, g2 = hh // 2, hh % 2
                out = ps[64 * g2:64 * g2 + 64, 6 + t % 2, 0:P]
                if g2 == 0 and n >= 4:
                    pe.wait_ge(out_copied, n // 2 - 1)
                pe.matmul(out, values_c[:, hh // 8, hh % 8, :], pct[:, i, hh // 8, :], start=True, stop=False)
                for br in range(2):
                    pe.wait_ge(copied_w if br else copied_t, n + 1)
                    at = 256 * br + 128 * (hh // 8) + 64 * g2
                    for kt in range(i + 1):
                        mm = pe.matmul(out, v.vt[:, kt, at:at + 64], prob_t[:, (2 * n + br) % 4, kt * P:(kt + 1) * P],
                                       start=False, stop=(br == 1 and kt == i))
                mm.then_inc(valued, 1)

            pe.wait_ge(masks, 2)
            for n in range(last + 3):
                if n < last:
                    scores(n)
                if n == 2:
                    pe.wait_ge(c_copied, 1)
                if 0 <= n - 2 < last:
                    turn(n - 2)
                if n == 3:
                    pe.wait_ge(c_made, 2)
                if 0 <= n - 3 < last:
                    values(n - 3)
            pe.wait_ge(out_copied, last // 2)
            proj.pe(pe)

        @block.scalar
        def _(act):
            w.lead(act, 0), w.lead(act, 1)
            act.activation(ident16[:, :], g.ident, ACT.Copy).then_inc(masks, 1)
            act.activation(causal16[:, :], g.causal, ACT.Copy).then_inc(masks, 1)
            act.wait_ge(c_shifted, 1)
            act.activation(pc[:], pc[:], ACT.Exp).then_inc(c_exped, 1)
            act.wait_ge(c_turned, 1)
            act.activation(pct[:].rearrange("p (b i) k n -> p b (i k n)", b=2), ps[:, 4:6, :], ACT.Copy).then_inc(c_copied, 1)
            for n in range(last + 4):
                if n < last:
                    i = units[n][0]
                    for br in range(2):
                        k = 2 * n + br
                        act.wait_ge(maxed, k + 1)
                        if k >= 4:
                            act.wait_ge(turned, k - 3)
                        act.activation(prob[:, k % 4, 0:(i + 1) * P], ps[:, k % 4, 0:(i + 1) * P], ACT.Exp,
                                       bias=nmax[:, k % 4:k % 4 + 1],
                                       accum_out=total[:, k % 4:k % 4 + 1]).then_inc(exped, 1)
                if 0 <= n - 2 < last:
                    m = n - 2
                    i = units[m][0]
                    act.wait_ge(turned, 2 * m + 1)
                    if m >= 2:
                        act.wait_ge(valued, m - 1)
                    act.activation(prob_t[:, (2 * m) % 4, 0:(i + 1) * P], ps[:, 4, 0:(i + 1) * P],
                                   ACT.Copy).then_inc(copied_t, 1)
                m = n - 4
                if m >= 0 and m % 2:
                    i, hh = units[m]
                    act.wait_ge(valued, m + 1)
                    act.activation(v.y[:, hh // 2, i * P:(i + 1) * P], ps[:, 6 + hh // 2 % 2, 0:P],
                                   ACT.Copy).then_inc(out_copied, 1)
            for kt in range(KT):
                act.wait_ge(out_copied, last // 2 - KT + kt + 1)
                proj.lead(act, v.y, kt)
            proj.act(act)

        @block.vector
        def _(dve):
            own = Steps(dve, dve_own)
            own.did(dve.memset(keys_c[:], 0.0))
            dve.tensor_copy(repeat[:], g.ident[0:PCMP, 0:PCMP].rearrange("p (o c) -> p o c", o=1)
                            .to_broadcast([PCMP, KT, PCMP]))
            own.settle()
            for g2 in range(2):
                half = slice(64 * g2, 64 * g2 + 64)
                ins = dve.tensor_copy(keys_c[half, :, g2, :], v.cmp_p[half, 0:2, :])
            ins.then_inc(c_made, 1)
            dve.wait_ge(c_repeated, 1)
            for k in range(KT):
                at = 64 * (k % 2)
                vals = ps[:, 6, 0:2 * P].rearrange("p (a n) -> p a n", a=2)[:, :, at:at + 64]
                ins = dve.tensor_scalar(values_c[:, :, k, :], vals, g.same16[:, 16 * k:16 * k + 1], None, ALU.mult)
            ins.then_inc(c_made, 1)

            def spread16(ap):
                return ap.rearrange("p i (h o) -> p i h o", o=1).to_broadcast([P, NCH, HEADS, PCMP])

            dve.wait_ge(c_scored, 1)
            mask = g.cmp_mask.rearrange("p (i o c) -> p i o c", o=1, c=PCMP).to_broadcast([P, NCH, HEADS, PCMP])
            own.did(dve.tensor_tensor(pc[:], ps[:, 0:4, 0:HEADS * PCMP].rearrange("p i (h c) -> p i h c", c=PCMP), mask, ALU.add))
            own.settle()
            own.did(dve.tensor_reduce(stat[:, 0], pc[:], AX, ALU.max))
            own.settle()
            dve.tensor_tensor(pc[:], pc[:], spread16(stat[:, 0]), ALU.subtract).then_inc(c_shifted, 1)
            dve.wait_ge(c_exped, 1)
            own.did(dve.tensor_reduce(stat[:, 1], pc[:], AX, ALU.add))
            own.settle()
            own.did(dve.reciprocal(stat[:, 1], stat[:, 1]))
            own.settle()
            for i in range(NCH):
                s = stat[:, 1, i].rearrange("p (t a) -> p t a", a=2)
                own.did(dve.scalar_tensor_tensor(s, s, g.cmp_any[:, i:i + 1],
                                                 v.gate[:, i, 0:16].rearrange("p (a t) -> p t a", a=2), ALU.mult, ALU.mult))
            own.settle()
            dve.tensor_tensor(pc[:], pc[:], spread16(stat[:, 1]), ALU.mult).then_inc(c_scaled, 1)

            for n in range(last + 2):
                if n < last:
                    i = units[n][0]
                    for br in range(2):
                        k = 2 * n + br
                        dve.wait_ge(scored, k + 1)
                        if k >= 4:
                            dve.wait_ge(exped, k - 3)
                        dve.tensor_reduce(nmax[:, k % 4:k % 4 + 1], ps[:, k % 4, 0:(i + 1) * P], AX, ALU.max,
                                          negate=True).then_inc(maxed, 1)
                if 0 <= n - 1 < last:
                    m = n - 1
                    i, hh = units[m]
                    dve.wait_ge(exped, 2 * m + 2)
                    if m >= 2:
                        dve.wait_ge(scaled, 2 * m - 2)
                    f = factor[:, m % 2, :]
                    at = 16 + 8 * (hh % 2) + hh // 2
                    own.did(dve.reciprocal(f, total[:, (2 * m) % 4:(2 * m) % 4 + 2]))
                    own.settle()
                    own.did(dve.tensor_tensor(f, f, v.gate[:, i, at:at + 17:16], ALU.mult))
                    own.settle()
                    for br in range(2):
                        p = prob[:, (2 * m + br) % 4, 0:(i + 1) * P]
                        dve.tensor_scalar(p, p, f[:, br:br + 1], None, ALU.mult).then_inc(scaled, 1)
                if 0 <= n - 2 < last:
                    m = n - 2
                    i = units[m][0]
                    dve.wait_ge(turned, 2 * m + 2)
                    if m >= 2:
                        dve.wait_ge(valued, m - 1)
                    dve.tensor_copy(prob_t[:, (2 * m + 1) % 4, 0:(i + 1) * P], ps[:, 5, 0:(i + 1) * P]).then_inc(copied_w, 1)
            for kt in range(KT):
                proj.rest(dve, v.y, kt)
            proj.dve(dve, g.xt)


def nsa_stage(nc, d, o, g, layer):
    j = layer // 3
    with ExitStack() as ctx:
        sc = Scope(nc, ctx, f"nsa{j}")
        v = Shared()
        [v.y_hi] = sc.below(("y_hi", [P, KT, N], F32R))
        v.qu = sc.sb("q_plain", [P, KT, N])
        v.qr = sc.sb("q_rotated", [P, KT, N])
        v.kv = sc.sb("kv", [P, 8, N])
        v.vt = sc.sb("v_tokens", [P, NCH, 512])
        v.vn = sc.sb("v_new", [P, 512])
        v.kn = sc.sb("k_new", [P, 4, P])
        v.gate = sc.sb("gate", [P, NCH, 48])
        v.gate_new = sc.sb("gate_new", [B, 48])
        v.cmp_p = sc.sb("cmp_prompt", [P, 4, PCMP])
        v.cmp_v = sc.sb("cmp_values", [PCMP, 2, P])
        v.out_c = sc.sb("out_c", [P, B, 8])
        v.drop = sc.sb("drop_keys", [P, PAGES, P])
        v.y = g.xn
        with ExitStack() as early:
            esc = Scope(nc, early, f"nsae{j}")
            v.parts = esc.below(("x_hi", [P, KT, N], F32R), ("x_lo", [P, KT, N], F32R))
            v.w_cmp = esc.sb("w_cmp", [P, 2, 32, P])
            v.spare = esc.sb("spare", [P, 2 * KT * N - 2 * 32 * P])
            nsa_project(nc, d, o, g, v, layer, j)
            nsa_compress(nc, d, o, g, v, j)
        nsa_samples(nc, d, o, g, v, j)
        nsa_prompt(nc, d, o, g, v, j)


def final_stage(nc, d, o, g):
    with ExitStack() as ctx:
        sc = Scope(nc, ctx, "final")
        ps = sc.ps("ps", [P, 2, 512])
        norm = Norm(sc, g.norm_g[:, 8, :], ps)
        stored = sc.sem("stored")
        block = ctx.enter_context(nc.Block())

        @block.tensor
        def _(pe):
            norm.pe(pe, g.ones)

        @block.scalar
        def _(act):
            norm.act(act, g.xt, g.eps)

        @block.vector
        def _(dve):
            norm.dve(dve, g.xt, g.xn)

        @block.sync
        def _(sp):
            sp.wait_ge(norm.normed, KT)
            sp.dma_start(o["y_t"], g.xn[:]).then_inc(stored, 16)
            sp.wait_ge(stored, 16)


class Shared:
    pass


def const(g, name):
    a, b = CONST_AT[name]
    return g.const[:, a:b]


OUTPUTS = {
    "y_t": (P, KT, N), "ffn_last": (4, P, FT * 2, 10), "ffn_old": (4, P, FT * 2, B),
    "nsa_kv": (2, P, 8, N), "nsa_v": (2, P, NCH, 512), "nsa_v_new": (2, B, 512), "win_kept": (2, B, P, 2048),
    "gdn_last": (P, 8, 3, 11), "gdn_old": (P, 8, 3, 2, B), "gdn_state_p": (P, 8, P), "gdn_state_s": (P, 8 * B, P),
    "lru_last": (P, KT, 11), "lru_h": (P, KT, 9), "lru_old": (P, KT, 2, B),
}


def trunk_program(nc, d, o):
    with ExitStack() as ctx:
        sc = Scope(nc, ctx, "all")
        g = Shared()
        g.xt = sc.sb("x_t", [P, KT, N])
        g.xn = sc.sb("xn_t", [P, KT, N])
        g.const = sc.sb("consts", [P, CONST_COLS])
        g.norm_g = sc.sb("norm_g", [P, 9, KT])
        g.eps = sc.sb("eps", [P, 1])
        g.bias_one = sc.sb("bias_one", [P, 1])
        g.ident, g.ones, g.neg_upper, g.strict_t, g.same16, g.pair16, g.pair32, g.pair64 = [
            const(g, n) for n in ("ident", "ones", "neg_upper", "strict_t", "same16", "pair16", "pair32", "pair64")]
        g.causal, g.rope_swap, g.four_sum, g.cmp_mask, g.cmp_any, g.new_mask, g.block_no = [
            const(g, n) for n in ("causal", "rope_swap", "four_sum", "cmp_mask", "cmp_any", "new_mask", "block_no")]
        load_stage(nc, d, g)
        for layer in range(4):
            if layer % 3 == 0:
                nsa_stage(nc, d, o, g, layer)
            elif layer % 3 == 1:
                gdn_stage(nc, d, o, g)
            else:
                lru_stage(nc, d, o, g)
            ffn_stage(nc, d, o, g, layer)
        final_stage(nc, d, o, g)


def constants():
    import numpy as np

    i = np.arange(P)
    r, c = i[:, None], i[None, :]

    def blocks(n):
        return (r // n) == (c // n)

    swap = np.zeros((P, P))
    for base in (0, 64):
        for k in range(8):
            swap[base + k + 8, base + k] = 1.0
            swap[base + k, base + k + 8] = 1.0
    q = np.arange(T).reshape(4, P)
    c_end = (np.arange(PCMP) + 1) * 32 - 1
    valid = c_end[None, None, :] <= q.T[:, :, None]
    parts = {
        "ident": np.eye(P), "ones": np.ones((P, P)),
        "neg_upper": np.where(c >= r, 0.0, NEG),
        "strict_t": (c > r) * 1.0,
        "same16": blocks(16) * 1.0, "pair16": (blocks(32) & ~blocks(16)) * 1.0,
        "pair32": (blocks(64) & ~blocks(32)) * 1.0, "pair64": (~blocks(64)) * 1.0,
        "causal": np.where(c <= r, 0.0, NEG),
        "rope_swap": swap,
        "four_sum": blocks(4) * 1.0,
        "cmp_mask": np.where(valid, 0.0, NEG).reshape(P, -1),
        "cmp_any": valid.any(-1) * 1.0,
        "new_mask": np.where(r == np.arange(B)[None], 0.0, NEG),
        "block_no": np.broadcast_to(np.arange(16.0)[None], (P, 16)),
    }
    return np.concatenate([parts[n] for n, _ in CONST_PARTS], axis=1).astype(np.float32)


def rope_tables():
    import numpy as np

    half = 8
    inv = np.float32(500000.0) ** (-np.arange(half, dtype=np.float32) / np.float32(half))
    pos = np.concatenate([np.arange(T), np.full(B, 1024)]).astype(np.float32)
    ang = pos[None, :] * inv[:, None].astype(np.float32)
    cos, sin = np.ones((P, N), np.float32), np.zeros((P, N), np.float32)
    for base in (0, 64):
        cos[base:base + 8] = cos[base + 8:base + 16] = np.cos(ang)
        sin[base:base + 8], sin[base + 8:base + 16] = -np.sin(ang), np.sin(ang)
    return np.stack([cos, sin], axis=1)


def feature_major(a, lead=()):
    import numpy as np

    t = a.reshape(a.shape[:-1] + (a.shape[-1] // P, P))
    return np.ascontiguousarray(np.moveaxis(np.moveaxis(t, -1, 0), -1, 1))


def weight_tiles(w, cols):
    import numpy as np

    k, m = w.shape
    return np.ascontiguousarray(w.reshape(k // P, P, m // cols, cols).transpose(2, 1, 0, 3))


def lay_out(i):
    import numpy as np

    d = {}
    x = np.concatenate([i["x_prompt"][0], i["x_sample"][:, 0]], axis=0)
    d["x_t"] = feature_major(x)
    d["consts"] = constants()
    g = np.concatenate([i["norm_mix_g"], i["norm_ffn_g"], i["norm_final_g"][None]])
    d["norm_g"] = np.ascontiguousarray(g.reshape(9, KT, P).transpose(2, 0, 1))
    w = i["ffn_w_in"].reshape(4, KT, P, 2, FT, P)
    d["ffn_w_in"] = np.ascontiguousarray(w.transpose(0, 4, 2, 3, 1, 5)).reshape(4, FT, P, 2 * KT * P)
    w = i["ffn_w_out"].reshape(4, FT, P, KT, P)
    d["ffn_w_out"] = np.ascontiguousarray(w.transpose(0, 3, 2, 1, 4)).reshape(4, KT, P, FT * P)
    w = i["ffn_conv_w"].reshape(4, 3, 2, FT, P)
    d["ffn_conv_w"] = np.ascontiguousarray(w.transpose(0, 4, 3, 2, 1)).reshape(4, P, FT * 6)
    w = i["state_ffn_conv"].reshape(4, B, 2, 2, FT, P)
    d["ffn_state"] = np.ascontiguousarray(w.transpose(0, 5, 4, 3, 2, 1)).reshape(4, P, FT * 2, 2, B)
    w = i["lru_w_in"][0].reshape(KT, P, 2, KT, P)
    d["lru_w_in"] = np.ascontiguousarray(w.transpose(3, 1, 2, 0, 4)[:, :, ::-1]).reshape(KT, P, 2 * KT * P)
    d["lru_w_out"] = weight_tiles(i["lru_w_out"][0], P).reshape(KT, P, KT * P)
    small = np.concatenate([i["lru_conv_w"][0], i["lru_conv_b"], i["lru_b_ga"], i["lru_b_gx"], i["lru_lambda"]])
    d["lru_small"] = np.ascontiguousarray(small.reshape(8, KT, P).transpose(2, 1, 0))
    d["lru_state"] = np.ascontiguousarray(i["state_lru_conv"][0].reshape(B, 3, KT, P).transpose(3, 2, 1, 0))
    d["lru_h0"] = np.ascontiguousarray(i["state_lru_h"][0].reshape(B, KT, P).transpose(2, 1, 0))
    w = np.concatenate([i["lru_w_ga"], i["lru_w_gx"]])
    d["lru_w_gates"] = np.ascontiguousarray(w.transpose(2, 0, 1, 3))
    w = i["gdn_w_in"][0]
    heads = w[:, :4096].reshape(KT, P, 4, 8, P)
    d["gdn_w_in"] = np.ascontiguousarray(heads.transpose(3, 1, 2, 0, 4)).reshape(8, P, 4 * KT * P)
    ab = np.zeros((P, KT, 40), np.float32)
    gates = w[:, 4096:].reshape(KT, P, 2, 8).transpose(1, 0, 2, 3)
    ab[:, :, 0:8], ab[:, :, 32:40] = gates[:, :, 0], gates[:, :, 1]
    d["gdn_w_ab"] = ab
    d["gdn_head_w"] = np.ascontiguousarray(np.stack([i["gdn_A_log"][0], i["gdn_dt_bias"][0]], axis=1))
    d["gdn_taps"] = np.ascontiguousarray(i["gdn_conv_w"][0].reshape(4, 3, 8, P).transpose(3, 2, 1, 0))
    d["gdn_conv_state"] = np.ascontiguousarray(i["state_gdn_conv"][0].reshape(B, 3, 3, 8, P).transpose(4, 3, 2, 1, 0))
    d["gdn_norm_g"] = np.ascontiguousarray(i["gdn_norm_g"].reshape(P, 1))
    d["gdn_state"] = np.ascontiguousarray(i["state_gdn_S"][0].transpose(2, 1, 0, 3)).reshape(P, 8 * B, P)
    d["gdn_w_out"] = weight_tiles(i["gdn_w_out"][0], P).reshape(KT, P, KT * P)
    head = np.array([(2 * gp + g2) * 4 + jj for gp in range(2) for jj in range(4) for g2 in range(2)])
    order = (head[:, None] * 64 + np.arange(64)).reshape(-1)
    w = i["nsa_w_in"]
    kv0 = 1024
    cols = np.concatenate([order] + [kv0 + 256 * k + np.arange(256) for k in (0, 1, 2, 4)])
    wf = w[:, :, cols].reshape(2, KT, P, 8, 2, P)
    d["nsa_w_in"] = np.ascontiguousarray(wf.transpose(0, 3, 2, 4, 1, 5)).reshape(2, 8, P, 2 * KT * P)
    gates = w[:, :, 2560:].reshape(2, D, 3, 2, 2, 4).transpose(0, 1, 2, 4, 3, 5).reshape(2, D, 48)
    wv = np.concatenate([w[:, :, kv0 + 768:kv0 + 1024], w[:, :, kv0 + 1280:kv0 + 1536], gates], axis=2)
    d["nsa_w_v"] = np.ascontiguousarray(wv.reshape(2, KT, P, 560).transpose(0, 2, 1, 3))
    wo = i["nsa_w_out"][:, order].reshape(2, KT, P, KT, P)
    d["nsa_w_out"] = np.ascontiguousarray(wo.transpose(0, 3, 2, 1, 4)).reshape(2, KT, P, KT * P)
    d["rope"] = rope_tables()
    pe = i["nsa_cmp_pe"].transpose(0, 3, 1, 2)
    d["nsa_pe"] = np.ascontiguousarray(np.concatenate([pe, pe], axis=1))
    wc = np.zeros((2, P, 2, 32, P), np.float32)
    wt = i["nsa_cmp_w"].transpose(0, 3, 1, 2, 4)
    wc[:, 0:64, :, :, 0:64], wc[:, 64:, :, :, 64:] = wt, wt
    d["nsa_w_cmp"] = wc
    d["page_table"] = i["page_table"].reshape(1, -1)
    c = i["cache_nsa_cmp"].reshape(2, 80, 4, 32, 2, 2, 2, 64)
    d["cmp_pages"] = np.ascontiguousarray(c.transpose(0, 1, 6, 7, 4, 5, 3, 2)).reshape(2, 80, P, 512)
    c = i["cache_nsa_sel"].reshape(2, 80, P, 2, 2, 2, 64)
    keys = c[:, :, :, 0].transpose(0, 1, 4, 5, 3, 2).reshape(2, 80, P, 256)
    d["sel_pages"] = np.concatenate([keys, c[:, :, :, 1].reshape(2, 80, P, 256)], axis=3)
    c = i["state_nsa_win"].reshape(2, B, 512, 2, 2, 2, 64)
    keys = c[:, :, :, 0].transpose(0, 1, 4, 5, 3, 2).reshape(2, B, P, 1024)
    vals = c[:, :, :, 1].reshape(2, B, 4, P, 256).transpose(0, 1, 3, 2, 4).reshape(2, B, P, 1024)
    d["win_state"] = np.concatenate([keys, vals], axis=3)
    return d


def assemble(r):
    import numpy as np

    out = {}
    y = r["y_t"].transpose(2, 1, 0).reshape(N, D)
    out["y_prompt"], out["y_sample"] = y[None, :T], y[T:, None]
    last = r["ffn_last"].reshape(4, P, FT, 2, 10).transpose(0, 4, 3, 2, 1).reshape(4, 10, 2 * DFF)
    old = r["ffn_old"].reshape(4, P, FT, 2, B).transpose(0, 4, 3, 2, 1).reshape(4, B, 2 * DFF)
    out["ffn_p"] = last[:, None, 0:2]
    out["ffn_s"] = np.stack([old, last[:, 2:]], axis=2)
    last = r["lru_last"].transpose(2, 1, 0).reshape(11, D)
    old = r["lru_old"].transpose(3, 2, 1, 0).reshape(B, 2, D)
    out["lc_p"] = last[None, None, 0:3]
    out["lc_s"] = np.concatenate([old, last[3:, None]], axis=1)[None]
    h = r["lru_h"].transpose(2, 1, 0).reshape(9, D)
    out["lh_p"], out["lh_s"] = h[None, 0:1], h[None, 1:]
    last = r["gdn_last"].transpose(3, 2, 1, 0).reshape(11, 3072)
    old = r["gdn_old"].transpose(4, 3, 2, 1, 0).reshape(B, 2, 3072)
    out["gc_p"] = last[None, None, 0:3]
    out["gc_s"] = np.concatenate([old, last[3:, None]], axis=1)[None]
    out["gS_p"] = r["gdn_state_p"].transpose(1, 0, 2)[None, None]
    out["gS_s"] = r["gdn_state_s"].reshape(P, 8, B, P).transpose(2, 1, 0, 3)[None]
    kv = r["nsa_kv"].reshape(2, 2, 64, 4, 2, N)
    kv = kv.transpose(3, 0, 5, 4, 1, 2).reshape(4, 2, N, 4, 64)
    vp = r["nsa_v"].transpose(0, 2, 1, 3).reshape(2, T, 2, 4, 64)
    v = np.concatenate([vp, r["nsa_v_new"].reshape(2, B, 2, 4, 64)], axis=1)
    cmp = np.stack([kv[0], kv[1]], axis=2)
    sel = np.stack([kv[2], v[:, :, 0]], axis=2)
    win = np.stack([kv[3], v[:, :, 1]], axis=2)
    for name, a in (("cmp", cmp), ("sel", sel), ("win", win)):
        out[name + "_p"] = a[:, None, :T]
    out["cmp_s"], out["sel_s"] = cmp[:, T:, None], sel[:, T:, None]
    kept = r["win_kept"]
    keys = kept[:, :, :, :1024].reshape(2, B, 2, 64, 2, 512).transpose(0, 1, 5, 4, 2, 3).reshape(2, B, 512, 4, 64)
    vals = kept[:, :, :, 1024:].reshape(2, B, P, 4, 4, 64).transpose(0, 1, 3, 2, 4, 5).reshape(2, B, 512, 4, 64)
    old = np.stack([keys, vals], axis=3)[:, :, 1:]
    out["win_s"] = np.concatenate([old, win[:, T:, None]], axis=2)
    return out


ORDER = ["y_prompt", "y_sample", "cmp_p", "cmp_s", "sel_p", "sel_s", "win_p", "win_s", "gS_p", "gS_s",
         "gc_p", "gc_s", "lh_p", "lh_s", "lc_p", "lc_s", "ffn_p", "ffn_s"]


def kernel(**inputs):
    import numpy as np
    import concourse.bacc as bacc
    from concourse.bass_utils import run_bass_kernel_spmd

    nc = bacc.Bacc("TRN2", target_bir_lowering=False, num_devices=1)
    arrays = {n: np.ascontiguousarray(a) for n, a in lay_out({n: np.asarray(a) for n, a in inputs.items()}).items()}
    d = {n: nc.dram_tensor(n, a.shape, mybir.dt.from_np(a.dtype), kind="ExternalInput").ap()
         for n, a in arrays.items()}
    o = {n: nc.dram_tensor(n, shape, F32, kind="ExternalOutput").ap() for n, shape in OUTPUTS.items()}
    trunk_program(nc, d, o)
    r = run_bass_kernel_spmd(nc, [arrays], core_ids=[0])
    results = assemble({n: np.asarray(r.results[0][n]) for n in OUTPUTS})
    return tuple(np.ascontiguousarray(results[n]) for n in ORDER)
```
